# Optimizing a Trainium2 kernel written in Bass

```python
import jax, jax.numpy as jnp
from jax import lax
import numpy as np
import math

D_MODEL = 1024
BATCH = 1
SEQ = 1024
DEPTH = 1

CHUNK = 64
Q_BLOCK = 128
HEAD_DIM = 64
N_HEADS_FOX = 8
N_HEADS_DSA = 8
IDX_HEADS = 8
IDX_DIM = 64
TOPK_MAX = 256
ROPE_THETA = 10000.0
N_GROUPS = 4
EXPERTS_PER_GROUP = 8
N_EXPERTS = N_GROUPS * EXPERTS_PER_GROUP
TOP_K_INNER = 2
D_EXPERT = 512
EPS = 1e-6

W_FOX = N_HEADS_FOX * HEAD_DIM
W_DSA = N_HEADS_DSA * HEAD_DIM
IN_SPLITS = (W_FOX, W_FOX, W_FOX, N_HEADS_FOX,
             W_DSA, HEAD_DIM, HEAD_DIM,
             IDX_HEADS * IDX_DIM, IDX_DIM, IDX_HEADS,
             D_MODEL, D_MODEL)
IN_COLS = 3 * W_FOX + N_HEADS_FOX + W_DSA + 2 * HEAD_DIM + IDX_HEADS * IDX_DIM + IDX_DIM + IDX_HEADS + 2 * D_MODEL


def rmsnorm(x, g):
    xf = x.astype(jnp.float32)
    y = xf * lax.rsqrt(jnp.mean(xf * xf, axis=-1, keepdims=True) + EPS)
    return (y * g.astype(jnp.float32)).astype(x.dtype)

def rope(x, pos):
    half = x.shape[-1] // 2
    inv = ROPE_THETA ** (-jnp.arange(half, dtype=jnp.float32) / half)
    ang = pos.astype(jnp.float32)[..., None] * inv
    cos = jnp.cos(ang)[:, :, None, :]
    sin = jnp.sin(ang)[:, :, None, :]
    x1 = x[..., :half].astype(jnp.float32)
    x2 = x[..., half:].astype(jnp.float32)
    out = jnp.concatenate([x1 * cos - x2 * sin, x2 * cos + x1 * sin], axis=-1)
    return out.astype(x.dtype)

def forgetting_attention(q, k, v, log_f):
    B, S, H, D = q.shape
    Ft = jnp.cumsum(log_f, axis=1).transpose(0, 2, 1)
    scale = D ** -0.5
    outs = []
    for start in range(0, S, Q_BLOCK):
        end = start + Q_BLOCK
        s = jnp.einsum('bqhd,bkhd->bhqk', q[:, start:end], k[:, :end],
                       preferred_element_type=jnp.float32) * scale
        s = s + Ft[:, :, start:end, None] - Ft[:, :, None, :end]
        tq = jnp.arange(start, end)[:, None]
        tk = jnp.arange(end)[None, :]
        s = jnp.where(tk <= tq, s, -jnp.inf)
        p = jax.nn.softmax(s, axis=-1)
        outs.append(jnp.einsum('bhqk,bkhd->bqhd', p.astype(v.dtype), v[:, :end]))
    return jnp.concatenate(outs, axis=1)

def dsa_attention(q, k, v, qi, ki, wi):
    B, S, H, D = q.shape
    topk = min(TOPK_MAX, S // 4)
    chunk_id = jnp.arange(S) // CHUNK
    scale = D ** -0.5
    gather = jax.vmap(lambda arr, ids: arr[ids])
    outs = []
    for start in range(0, S, Q_BLOCK):
        end = start + Q_BLOCK
        kk = min(topk, end)
        dots = jnp.einsum('bqhd,bkd->bqhk', qi[:, start:end], ki[:, :end],
                          preferred_element_type=jnp.float32)
        score = jnp.einsum('bqh,bqhk->bqk', wi[:, start:end].astype(jnp.float32), jax.nn.relu(dots))
        cq = chunk_id[start:end]
        allowed = chunk_id[:end][None, :] <= cq[:, None]
        score = jnp.where(allowed[None], score, -jnp.inf)
        _, idx = lax.top_k(score, kk)
        valid = chunk_id[idx] <= cq[None, :, None]
        kg = gather(k[:, :end], idx)
        vg = gather(v[:, :end], idx)
        s = jnp.einsum('bqhd,bqkd->bhqk', q[:, start:end], kg,
                       preferred_element_type=jnp.float32) * scale
        s = jnp.where(valid[:, None], s, -jnp.inf)
        p = jax.nn.softmax(s, axis=-1)
        outs.append(jnp.einsum('bhqk,bqkd->bqhd', p.astype(vg.dtype), vg))
    return jnp.concatenate(outs, axis=1)

def hierarchical_moe(h, w_grp, b_grp, w_exp, b_exp, w1, w3, w2):
    N, D = h.shape
    g_logits = jnp.matmul(h, w_grp).astype(jnp.float32) + b_grp.astype(jnp.float32)
    g_prob = jax.nn.softmax(g_logits, axis=-1)
    g_idx = jnp.argmax(g_logits, axis=-1)
    g_w = jnp.take_along_axis(g_prob, g_idx[:, None], axis=1)[:, 0]
    e_logits = (jnp.matmul(h, w_exp).astype(jnp.float32) + b_exp.astype(jnp.float32))
    e_logits = e_logits.reshape(N, N_GROUPS, EXPERTS_PER_GROUP)
    e_logits = jnp.take_along_axis(e_logits, g_idx[:, None, None], axis=1)[:, 0]
    e_prob = jax.nn.softmax(e_logits, axis=-1)
    top_p, top_local = lax.top_k(e_prob, TOP_K_INNER)
    top_p = top_p / jnp.sum(top_p, axis=-1, keepdims=True)
    weights = (g_w[:, None] * top_p).reshape(-1)
    expert = (g_idx[:, None] * EXPERTS_PER_GROUP + top_local).reshape(-1)
    order = jnp.argsort(expert)
    tok = order // TOP_K_INNER
    xs = h[tok]
    sizes = jnp.bincount(expert, length=N_EXPERTS).astype(jnp.int32)
    a = lax.ragged_dot(xs, w1, sizes)
    b = lax.ragged_dot(xs, w3, sizes)
    y = lax.ragged_dot(jax.nn.silu(a) * b, w2, sizes)
    y = (y * weights[order][:, None]).astype(h.dtype)
    return jax.ops.segment_sum(y, tok, num_segments=N)

def first_inputs(seed: int = 0) -> dict:
    key = jax.random.key(seed)
    ks = jax.random.split(key, 24)
    f32 = jnp.float32
    nrm = lambda k, shape, fan: jax.random.normal(k, shape, f32) * fan ** -0.5
    L = DEPTH
    x = jax.random.normal(ks[0], (BATCH, SEQ, D_MODEL), f32)
    c = jax.random.normal(ks[1], (BATCH, D_MODEL), f32)
    offsets = jax.random.randint(ks[2], (BATCH,), 0, 64) * CHUNK
    positions = (offsets[:, None] + jnp.arange(SEQ)[None, :]).astype(jnp.int32)
    return {
        'x': x,
        'c': c,
        'positions': positions,
        'ada_w': nrm(ks[3], (L, D_MODEL, 6 * D_MODEL), D_MODEL) * 0.5,
        'ada_b': jax.random.normal(ks[4], (L, 6 * D_MODEL), f32) * 0.02,
        'norm1_g': 1.0 + 0.05 * jax.random.normal(ks[5], (L, D_MODEL), f32),
        'norm2_g': 1.0 + 0.05 * jax.random.normal(ks[6], (L, D_MODEL), f32),
        'w_in': nrm(ks[7], (L, D_MODEL, IN_COLS), D_MODEL),
        'b_fgt': jax.random.uniform(ks[8], (L, N_HEADS_FOX), f32, 1.0, 4.0),
        'b_gate': jax.random.normal(ks[9], (L, 2 * D_MODEL), f32) * 0.02,
        'qn_fox': 1.0 + 0.05 * jax.random.normal(ks[10], (L, HEAD_DIM), f32),
        'kn_fox': 1.0 + 0.05 * jax.random.normal(ks[11], (L, HEAD_DIM), f32),
        'qn_dsa': 1.0 + 0.05 * jax.random.normal(ks[12], (L, HEAD_DIM), f32),
        'kn_dsa': 1.0 + 0.05 * jax.random.normal(ks[13], (L, HEAD_DIM), f32),
        'w_proj_fox': nrm(ks[14], (L, W_FOX, D_MODEL), W_FOX),
        'w_proj_dsa': nrm(ks[15], (L, W_DSA, D_MODEL), W_DSA),
        'w_out': nrm(ks[16], (L, D_MODEL, D_MODEL), D_MODEL),
        'router_w_grp': nrm(ks[17], (L, D_MODEL, N_GROUPS), D_MODEL),
        'router_b_grp': jax.random.normal(ks[18], (L, N_GROUPS), f32) * 0.01,
        'router_w_exp': nrm(ks[19], (L, D_MODEL, N_EXPERTS), D_MODEL),
        'router_b_exp': jax.random.normal(ks[20], (L, N_EXPERTS), f32) * 0.01,
        'exp_w1': nrm(ks[21], (L, N_EXPERTS, D_MODEL, D_EXPERT), D_MODEL),
        'exp_w3': nrm(ks[22], (L, N_EXPERTS, D_MODEL, D_EXPERT), D_MODEL),
        'exp_w2': nrm(ks[23], (L, N_EXPERTS, D_EXPERT, D_MODEL), D_EXPERT),
    }

def first_block(x, c, positions, ada_w, ada_b, norm1_g, norm2_g, w_in, b_fgt, b_gate,
              qn_fox, kn_fox, qn_dsa, kn_dsa, w_proj_fox, w_proj_dsa, w_out,
              router_w_grp, router_b_grp, router_w_exp, router_b_exp,
              exp_w1, exp_w3, exp_w2):
    B, S, D = x.shape
    split_at = np.cumsum(IN_SPLITS)[:-1].tolist()
    c_act = jax.nn.silu(c)
    for l in range(DEPTH):
        mod = jnp.matmul(c_act, ada_w[l]) + ada_b[l]
        sh1, sc1, gt1, sh2, sc2, gt2 = [m[:, None, :] for m in jnp.split(mod, 6, axis=-1)]

        h = rmsnorm(x, norm1_g[l]) * (1.0 + sc1) + sh1
        proj = jnp.matmul(h, w_in[l])
        (fq, fk, fv, flog, dq, dk, dv, iq, ik, iw, g_fox, g_dsa) = jnp.split(proj, split_at, axis=-1)

        fq = rmsnorm(fq.reshape(B, S, N_HEADS_FOX, HEAD_DIM), qn_fox[l])
        fk = rmsnorm(fk.reshape(B, S, N_HEADS_FOX, HEAD_DIM), kn_fox[l])
        fv = fv.reshape(B, S, N_HEADS_FOX, HEAD_DIM)
        log_f = jax.nn.log_sigmoid((flog + b_fgt[l]).astype(jnp.float32))
        out_fox = forgetting_attention(fq, fk, fv, log_f).reshape(B, S, W_FOX)

        dq = rope(rmsnorm(dq.reshape(B, S, N_HEADS_DSA, HEAD_DIM), qn_dsa[l]), positions)
        dk = rope(rmsnorm(dk.reshape(B, S, 1, HEAD_DIM), kn_dsa[l]), positions)[:, :, 0]
        iq = rope(iq.reshape(B, S, IDX_HEADS, IDX_DIM), positions)
        ik = rope(ik.reshape(B, S, 1, IDX_DIM), positions)[:, :, 0]
        out_dsa = dsa_attention(dq, dk, dv, iq, ik, iw).reshape(B, S, W_DSA)

        merged = (jax.nn.sigmoid(g_fox + b_gate[l, :D]) * jnp.matmul(out_fox, w_proj_fox[l])
                  + jax.nn.sigmoid(g_dsa + b_gate[l, D:]) * jnp.matmul(out_dsa, w_proj_dsa[l]))
        x = x + gt1 * jnp.matmul(merged, w_out[l])

        h2 = rmsnorm(x, norm2_g[l]) * (1.0 + sc2) + sh2
        y = hierarchical_moe(h2.reshape(B * S, D), router_w_grp[l], router_b_grp[l],
                             router_w_exp[l], router_b_exp[l],
                             exp_w1[l], exp_w3[l], exp_w2[l]).reshape(B, S, D)
        x = x + gt2 * y
    return x


POOL_WINDOWS = (2, 4, 8, 16)
POOL_GROUPS = len(POOL_WINDOWS)
POOL_WIDTH = D_MODEL // 2
POOL_GROUP_DIM = POOL_WIDTH // POOL_GROUPS
RNN_WIDTH = D_MODEL
RNN_HEADS = 16
RNN_HEAD_DIM = RNN_WIDTH // RNN_HEADS
RNN_CONV = 4
LRU_C = 8.0
D_FF = 3 * D_MODEL
FFN_CONV = 3
PLE_DIM = 256
N_BRANCH = 2
RMS_EPS = 1e-6
IN_POOL = POOL_WIDTH
IN_RNN_X = RNN_WIDTH
IN_RNN_G = RNN_WIDTH
IN_GATES = N_BRANCH * D_MODEL
IN_TOTAL = IN_POOL + IN_RNN_X + IN_RNN_G + IN_GATES


def rms_norm(x, g):
    xf = x.astype(jnp.float32)
    y = xf * lax.rsqrt(jnp.mean(xf * xf, axis=-1, keepdims=True) + RMS_EPS) * g.astype(jnp.float32)
    return y.astype(x.dtype)

def causal_dwconv(u, w, b):
    k_w = w.shape[0]
    s = u.shape[1]
    up = jnp.pad(u, ((0, 0), (k_w - 1, 0), (0, 0)))
    out = b + up[:, 0:s] * w[0]
    for k in range(1, k_w):
        out = out + up[:, k:k + s] * w[k]
    return out

def pool_mixer(u, pool_w, pool_scale):
    b, s, _ = u.shape
    uf = u.astype(jnp.float32)
    cs = jnp.pad(jnp.cumsum(uf, axis=1), ((0, 0), (1, 0), (0, 0)))
    t = jnp.arange(s, dtype=jnp.int32)
    outs = []
    for g, w in enumerate(POOL_WINDOWS):
        sl = cs[..., g * POOL_GROUP_DIM:(g + 1) * POOL_GROUP_DIM]
        prev = jnp.pad(sl, ((0, 0), (w - 1, 0), (0, 0)))[:, :s]
        count = jnp.minimum(t + 1, w).astype(jnp.float32)[None, :, None]
        outs.append((sl[:, 1:] - prev) / count)
    mean = jnp.concatenate(outs, axis=-1)
    d = (mean - uf).astype(u.dtype).reshape(b, s, POOL_GROUPS, POOL_GROUP_DIM)
    y = jnp.einsum('bsgc,gcd->bsgd', d, pool_w).reshape(b, s, POOL_WIDTH)
    return y * pool_scale

def rg_lru_branch(xb, gb, conv_w, conv_b, w_gates, b_gates, lru_lambda):
    b, s, _ = xb.shape
    xc = causal_dwconv(xb, conv_w, conv_b)
    xh = xc.reshape(b, s, RNN_HEADS, RNN_HEAD_DIM)
    gates = jnp.einsum('bshi,ghij->gbshj', xh, w_gates).reshape(2, b, s, RNN_WIDTH)
    gates = gates.astype(jnp.float32) + b_gates.astype(jnp.float32)[:, None, None, :]
    r = jax.nn.sigmoid(gates[0])
    i = jax.nn.sigmoid(gates[1])
    log_a = -LRU_C * r * jax.nn.softplus(-lru_lambda.astype(jnp.float32))
    a = jnp.exp(log_a)
    mult = jnp.sqrt(-jnp.expm1(2.0 * log_a))
    t0 = (jnp.arange(s) == 0)[None, :, None]
    mult = jnp.where(t0, 1.0, mult)
    u = mult * i * xc.astype(jnp.float32)

    def combine(left, right):
        a_l, h_l = left
        a_r, h_r = right
        return a_l * a_r, a_r * h_l + h_r

    _, h = lax.associative_scan(combine, (a, u), axis=1)
    return h.astype(xb.dtype) * jax.nn.gelu(gb)

def second_inputs(seed: int = 0) -> dict:
    key = jax.random.key(seed)
    ks = jax.random.split(key, 32)
    f32 = jnp.float32
    L = DEPTH

    def nrm(k, shape, fan_in):
        return jax.random.normal(k, shape, f32) * (fan_in ** -0.5)

    def gain(k, shape):
        return 1.0 + 0.05 * jax.random.normal(k, shape, f32)

    a_c = jax.random.uniform(ks[10], (L, RNN_WIDTH), f32, 0.9, 0.999)
    s_l = a_c ** (1.0 / LRU_C)
    lru_lambda = jnp.log(s_l) - jnp.log1p(-s_l)

    return {
        "x": jax.random.normal(ks[0], (BATCH, SEQ, D_MODEL), f32),
        "p": jax.random.normal(ks[1], (DEPTH, BATCH, SEQ, PLE_DIM), f32),
        "g_mix_pre": gain(ks[2], (L, D_MODEL)),
        "g_mix_post": gain(ks[3], (L, D_MODEL)),
        "w_in": nrm(ks[4], (L, D_MODEL, IN_TOTAL), D_MODEL),
        "pool_w": nrm(ks[5], (L, POOL_GROUPS, POOL_GROUP_DIM, POOL_GROUP_DIM), POOL_GROUP_DIM),
        "pool_scale": gain(ks[6], (L, POOL_WIDTH)),
        "w_pool_out": nrm(ks[7], (L, POOL_WIDTH, D_MODEL), POOL_WIDTH),
        "conv_w": nrm(ks[8], (L, RNN_CONV, RNN_WIDTH), RNN_CONV),
        "conv_b": 0.02 * jax.random.normal(ks[9], (L, RNN_WIDTH), f32),
        "w_rg_gates": nrm(ks[11], (L, 2, RNN_HEADS, RNN_HEAD_DIM, RNN_HEAD_DIM), RNN_HEAD_DIM),
        "b_rg_gates": 0.02 * jax.random.normal(ks[12], (L, 2, RNN_WIDTH), f32),
        "lru_lambda": lru_lambda,
        "w_rg_out": nrm(ks[13], (L, RNN_WIDTH, D_MODEL), RNN_WIDTH),
        "w_o": nrm(ks[14], (L, D_MODEL, D_MODEL), D_MODEL),
        "g_ffn_pre": gain(ks[15], (L, D_MODEL)),
        "g_ffn_post": gain(ks[16], (L, D_MODEL)),
        "w_up": nrm(ks[17], (L, D_MODEL, 2 * D_FF), D_MODEL),
        "ffn_conv_w": nrm(ks[18], (L, FFN_CONV, D_FF), FFN_CONV),
        "ffn_conv_b": 0.02 * jax.random.normal(ks[19], (L, D_FF), f32),
        "w_down": nrm(ks[20], (L, D_FF, D_MODEL), D_FF),
        "g_ple_gate": gain(ks[21], (L, D_MODEL)),
        "w_ple_gate": nrm(ks[22], (L, D_MODEL, D_MODEL), D_MODEL),
        "w_ple_proj": nrm(ks[23], (L, PLE_DIM, D_MODEL), PLE_DIM),
        "g_ple_post": gain(ks[24], (L, D_MODEL)),
    }

def second_block(x, p, g_mix_pre, g_mix_post, w_in, pool_w, pool_scale, w_pool_out,
              conv_w, conv_b, w_rg_gates, b_rg_gates, lru_lambda, w_rg_out, w_o,
              g_ffn_pre, g_ffn_post, w_up, ffn_conv_w, ffn_conv_b, w_down,
              g_ple_gate, w_ple_gate, w_ple_proj, g_ple_post):
    for l in range(DEPTH):
        h = rms_norm(x, g_mix_pre[l])
        z = h @ w_in[l]
        c0 = IN_POOL
        c1 = c0 + IN_RNN_X
        c2 = c1 + IN_RNN_G
        u_pool = z[..., :c0]
        u_rx = z[..., c0:c1]
        u_rg = z[..., c1:c2]
        gate_pool = jax.nn.sigmoid(z[..., c2:c2 + D_MODEL])
        gate_rnn = jax.nn.sigmoid(z[..., c2 + D_MODEL:])

        y_pool = pool_mixer(u_pool, pool_w[l], pool_scale[l]) @ w_pool_out[l]
        y_rnn = rg_lru_branch(u_rx, u_rg, conv_w[l], conv_b[l], w_rg_gates[l],
                              b_rg_gates[l], lru_lambda[l]) @ w_rg_out[l]
        merged = gate_pool * y_pool + gate_rnn * y_rnn
        x = x + rms_norm(merged @ w_o[l], g_mix_post[l])

        h = rms_norm(x, g_ffn_pre[l])
        up = h @ w_up[l]
        gate_h = causal_dwconv(up[..., :D_FF], ffn_conv_w[l], ffn_conv_b[l])
        hid = jax.nn.gelu(gate_h) * up[..., D_FF:]
        x = x + rms_norm(hid @ w_down[l], g_ffn_post[l])

        ple_gate = jax.nn.sigmoid(rms_norm(x, g_ple_gate[l]) @ w_ple_gate[l])
        ple = rms_norm(p[l].astype(x.dtype) @ w_ple_proj[l], g_ple_post[l])
        x = x + ple_gate * ple
    return x


def setup_inputs(seed=0):
    out = dict(first_inputs(seed))
    for name, value in second_inputs(seed + 1).items():
        if name != "x":
            out[name + "_2"] = value
    return out


def reference(
    x, c, positions, ada_w, ada_b, norm1_g, norm2_g, w_in, b_fgt, b_gate, qn_fox, kn_fox,
    qn_dsa, kn_dsa, w_proj_fox, w_proj_dsa, w_out, router_w_grp, router_b_grp, router_w_exp,
    router_b_exp, exp_w1, exp_w3, exp_w2, p_2, g_mix_pre_2, g_mix_post_2, w_in_2, pool_w_2,
    pool_scale_2, w_pool_out_2, conv_w_2, conv_b_2, w_rg_gates_2, b_rg_gates_2, lru_lambda_2,
    w_rg_out_2, w_o_2, g_ffn_pre_2, g_ffn_post_2, w_up_2, ffn_conv_w_2, ffn_conv_b_2, w_down_2,
    g_ple_gate_2, w_ple_gate_2, w_ple_proj_2, g_ple_post_2,
):
    x = first_block(
        x, c, positions, ada_w, ada_b, norm1_g, norm2_g, w_in, b_fgt, b_gate, qn_fox, kn_fox,
        qn_dsa, kn_dsa, w_proj_fox, w_proj_dsa, w_out, router_w_grp, router_b_grp, router_w_exp,
        router_b_exp, exp_w1, exp_w3, exp_w2,
    )
    return second_block(
        x, p_2, g_mix_pre_2, g_mix_post_2, w_in_2, pool_w_2, pool_scale_2, w_pool_out_2,
        conv_w_2, conv_b_2, w_rg_gates_2, b_rg_gates_2, lru_lambda_2, w_rg_out_2, w_o_2,
        g_ffn_pre_2, g_ffn_post_2, w_up_2, ffn_conv_w_2, ffn_conv_b_2, w_down_2, g_ple_gate_2,
        w_ple_gate_2, w_ple_proj_2, g_ple_post_2,
    )


_drawn_inputs = setup_inputs


def setup_inputs(seed=0):
    import zlib

    import numpy as np

    out = dict(_drawn_inputs(seed))
    spreads = {}
    factors = {'norm1_g': 4.293,
     'b_gate': 8.0,
     'qn_fox': 8.0,
     'kn_fox': 8.0,
     'qn_dsa': 8.0,
     'kn_dsa': 8.0,
     'router_b_grp': 33.189,
     'router_b_exp': 30.842,
     'b_rg_gates_2': 21.748,
     'ffn_conv_b_2': 5.176,
     'g_ple_gate_2': 8.0,
     'g_ple_post_2': 3.818,
     'norm2_g': 3.838,
     'g_mix_pre_2': 2.877,
     'g_mix_post_2': 3.319,
     'pool_scale_2': 3.786,
     'g_ffn_post_2': 3.512}
    for name, (base, spread) in spreads.items():
        noise = np.random.default_rng([zlib.crc32(name.encode()), seed]).standard_normal(out[name].shape)
        drawn = base * np.exp(spread * noise) if base else spread * noise
        out[name] = __import__('jax').numpy.asarray(drawn.astype(out[name].dtype))
    for name, factor in factors.items():
        out[name] = (out[name] * factor).astype(out[name].dtype)
    return out
```

```python
from contextlib import ExitStack

import numpy as np

import concourse.bass as bass
from concourse import mybir

F32 = mybir.dt.float32
F32R = mybir.dt.float32r
BF16 = mybir.dt.bfloat16
I32 = mybir.dt.int32
U32 = mybir.dt.uint32
ACT = mybir.ActivationFunctionType
ALU = mybir.AluOpType
AX = mybir.AxisListType
ds = bass.ds

P = 128
D = 1024
T = 1024
KD = D // P
NB = T // P
HALF = 512
HD = 64
NH = 8
TOPK = 256
EPS = 1e-6
SCALE = HD ** -0.5
NEG = -1e30
N_GRP, N_EXP, PER_GRP = 4, 32, 8
FE = 512
D_FF = 3072
POOL_WINDOWS = (2, 4, 8, 16)
LRU_C = 8.0
SLOTS = (2 * T + N_EXP * (P - 1)) // P
FAR = 3e38
ROUND = 1.5 * 2.0 ** 23
PI_IN = 3.1415925
TWO_PI = 2 * np.pi


def split_two_pi():
    a = 6.28125
    rest = TWO_PI - a
    b = float(np.round(rest * 2.0 ** 21) / 2.0 ** 21)
    return a, b, float(np.float32(rest - b))


class Chain:

    def __init__(self, engine, semaphore):
        self.e, self.s, self.n, self.off = engine, semaphore, 0, 0

    def __call__(self, ins):
        ins.then_inc(self.s, 1)
        self.n += 1
        self.e.wait_ge(self.s, self.off + self.n)

    def enter(self, i, per):
        self.off, self.start, self.per = i * per, self.n, per

    def leave(self, count):
        assert self.n - self.start == self.per, (self.n - self.start, self.per)
        self.n, self.off = self.start + self.per * count, 0


VECTORS = [
    [("ada_b", 48), ("norm1_g", 8), ("norm2_g", 8), ("b_gate", 16), ("c", 8), ("g_mix_pre_2", 8),
     ("g_mix_post_2", 8), ("g_ffn_pre_2", 8), ("g_ffn_post_2", 8), ("qn_fox", 1), ("kn_fox", 1),
     ("qn_dsa", 1), ("kn_dsa", 1), ("freq", 2)],
    [("g_ple_gate_2", 8), ("g_ple_post_2", 8), ("conv_w_2", 32), ("conv_b_2", 8), ("b_rg_gates_2", 16),
     ("lru_lambda_2", 8), ("ffn_conv_b_2", 24), ("pool_scale_2", 4)],
    [("ffn_conv_w_2", 72)],
]
VROWS = [sum(n for _, n in t) for t in VECTORS]
VCOL = {}
for _t, _tile in enumerate(VECTORS):
    _at = _t * P
    for _name, _n in _tile:
        VCOL[_name] = _at
        _at += _n

C_FQ, C_FK, C_FV, C_FL, C_DQ, C_DK, C_DV, C_IQ, C_IK, C_IW, C_G = (
    0, 512, 1024, 1536, 1544, 2056, 2120, 2184, 2696, 2760, 2768)

ITEMS = [("iq", 4), ("ik", 1), ("dviw", 1), ("fv", 4), ("flog", 1), ("dk", 1), ("gates", 16),
         ("qkd", 12), ("proj", 16), ("wout", 8),
         ("rx", 8), ("rg", 8), ("g2", 16), ("pool", 4), ("poolw", 4), ("mix", 16), ("wo", 8),
         ("ffn0", 24), ("ffn1", 24), ("ffn2", 24), ("plep", 8), ("pleg", 8)]
N0 = {}
_at = 0
for _name, _n in ITEMS:
    N0[_name] = _at
    _at += _n

N_VEC = sum(2 if n == 1 else 1 for t in VECTORS for _, n in t) + 1


def flat(ap):
    names = [f"a{i}" for i in range(len(ap.shape))]
    return ap.rearrange(f"{' '.join(names)} -> ({' '.join(names)})")


def program(nc, A, out):
    alloc = nc.alloc_sbuf_tensor_at
    sems, suffix = {}, ""

    def S(name):
        if name not in sems:
            sems[name] = nc.alloc_semaphore(name=name + suffix)
        return sems[name]

    base = 16512
    at = base

    def place(nbytes):
        nonlocal at
        o = at
        at += nbytes
        return o

    o_raw, o_whi, o_wlo = place(8192), place(8192), place(8192)
    o_ah, o_al = place(32768), place(32768)
    o_b = place(98304)
    o_bh, o_bl, o_c = o_b, o_b + 32768, o_b + 65536
    o_t = place(16384)

    wraw = alloc("wraw", [P, 2, KD, P], F32, offset=o_raw)
    whi = alloc("whi", [P, 2, KD, P], F32R, offset=o_whi)
    wlo = alloc("wlo", [P, 2, KD, P], F32R, offset=o_wlo)
    Ah = alloc("Ah", [P, KD, T], F32R, offset=o_ah)
    Al = alloc("Al", [P, KD, T], F32R, offset=o_al)
    Bh = alloc("Bh", [P, KD, T], F32R, offset=o_bh)
    Bl = alloc("Bl", [P, KD, T], F32R, offset=o_bl)
    C = alloc("C", [P, KD, T], F32, offset=o_c)
    TT = alloc("TT", [P, 4, T], F32, offset=o_t)

    def small(name, shape, dt=F32):
        n = int(np.prod(shape[1:])) * (2 if dt == BF16 else 4)
        return alloc(name, shape, dt, offset=place((n + 31) // 32 * 32))

    ident = small("ident", [P, P])
    identb = small("identb", [P, P], BF16)
    causb = small("causb", [P, P], BF16)
    meanD = small("meanD", [P, P])
    meanH = small("meanH", [P, P])
    strict = small("strict", [P, P], BF16)
    onesb = small("onesb", [P, P], BF16)
    VEC = small("VEC", [P, 3 * P])
    MOD = small("MOD", [P, 48])
    cact = small("cact", [P, 2, 8])
    gm = small("gm", [P, 2, 8])
    fb = small("fb", [NH, 1])
    bs = small("bs", [P, 10, 8])
    att = small("att", [P, 4, 2])
    gq = small("gq", [P, 13])
    one = small("one", [P, 1])
    small_end = at

    def vec(name, j=0, n=1):
        return VEC[:, VCOL[name] + j:VCOL[name] + j + n]

    def vecd(name, j):
        return VEC[:, ds(j + VCOL[name], 1)]

    xrows = alloc("xrows", [P, NB, D], F32, offset=o_bh)
    adaraw = alloc("adaraw", [P, KD, D], F32, offset=o_bl)
    vrows = alloc("vrows", [P, 3, P], F32, offset=o_ah)
    posi = alloc("posi", [P, T], I32, offset=o_t)
    trig = alloc("trig", [P, 4, T], F32, offset=o_b + 71936)
    QKD = alloc("QKD", [P, 12, T], F32, offset=o_b)
    IQ = alloc("IQ", [P, 4, T], F32, offset=o_b + 32768)
    KX = alloc("KX", [P, T], F32, offset=o_b + 49152)
    V = alloc("V", [P, NB, 512], F32, offset=o_b + 53248)
    DV = alloc("DV", [P, NB, 72], F32, offset=o_b + 69632)
    SCW = [(b + 1) * P for b in range(NB)]
    SCO = [sum(SCW[:b]) for b in range(NB)]
    SC = alloc("SC", [P, sum(SCW)], F32, offset=o_b + 71936)
    FS = alloc("FS", [NH, 4, T], F32, offset=o_b + 71936)
    nF = alloc("nF", [NH, T], F32, offset=o_b + 90368)
    E = alloc("E", [P, 8, T], F32, offset=o_b)
    junk = alloc("junk", [P, T], BF16, offset=o_b + 28672)
    IK = alloc("IK", [P, T], F32, offset=o_b + 24576)
    nFb = [alloc(f"nFb{h}", [P, T], F32, offset=(o_ah if h < 4 else o_al) + 4096 * (h % 4)) for h in range(NH)]
    Pb = [alloc(f"Pb{i}", [P, T], F32, offset=o_ah + 16384 + 4096 * i) for i in range(2)]
    PT = [alloc(f"PT{i}", [P, NB, P], F32, offset=o_ah + 24576 + 4096 * i) for i in range(2)]
    OF = alloc("OF", [P, 4, T], F32, offset=o_al + 16384)
    OD = alloc("OD", [P, 4, T], F32, offset=o_t)
    rw = alloc("rw", [P, KD, 36], F32, offset=o_bh)
    rwh = alloc("rwh", [P, KD, 36], F32R, offset=o_bh + 1152)
    rwl = alloc("rwl", [P, KD, 36], F32R, offset=o_bh + 2304)
    rbias = alloc("rbias", [P, 36], F32, offset=o_bh + 3456)
    R = lambda name, shape, off, dt=F32: alloc(name, shape, dt, offset=o_bh + 4096 + off)
    rL = R("rL", [P, NB, 36], 0)
    rG = R("rG", [P, NB, N_EXP], 1536)
    rT = R("rT", [P, NB, N_EXP], 2560)
    rO1 = R("rO1", [P, NB, N_EXP], 3584)
    rO2 = R("rO2", [P, NB, N_EXP], 4608)
    rOb = R("rOb", [P, NB, N_EXP], 5632, BF16)
    rK = R("rK", [P, NB, N_EXP], 6656)
    rS = R("rS", [P, 12, NB], 7680)
    rI = R("rI", [P, N_EXP], 8192)
    rGg = R("rGg", [P, NB, N_GRP], 8448)
    rN = R("rN", [P, N_EXP], 8704)
    rNt = R("rNt", [P, 4, N_EXP], 9344)
    rSi = R("rSi", [P, SLOTS + 1], 9856)
    rTk = R("rTk", [P, 2, NB], 10048, I32)
    rZ = R("rZ", [SLOTS + 1, P], 11808, I32)
    rLi = R("rLi", [SLOTS + 1, P], 10784, I32)
    rLf = R("rLf", [SLOTS + 1, P], 11296)
    hrow = alloc("hrow", [P, NB, D], F32, offset=o_bl)
    SLOTE = small("SLOTE", [P, SLOTS + 1], I32)
    NSL = small("NSL", [P, 1], I32)
    POS = small("POS", [P, 2, NB], I32)
    WTOK = small("WTOK", [P, 2, NB])
    IDX = small("IDX", [P, SLOTS + 1], I32)
    DST = small("DST", [P, SLOTS + 1], I32)
    IDC = small("IDC", [P, 1], I32)
    sp8 = small("sp8", [P, 3, KD])
    pfix = small("pfix", [P, 4, 16])
    IDD = small("IDD", [P, 1], I32)
    assert at <= 229344, at
    NRAW, NSP = 12, 4
    mraw = alloc("mraw", [P, NRAW, 1024], F32, offset=o_b)
    mhi = alloc("mhi", [P, NSP, 1024], F32R, offset=o_b + 49152)
    mlo = alloc("mlo", [P, NSP, 1024], F32R, offset=o_b + 65536)
    Xs = alloc("Xs", [P, D], F32, offset=o_b + 81920)
    YO = alloc("YO", [P, D], F32, offset=o_b + 86016)
    XTh = alloc("XTh", [P, KD, P], F32R, offset=o_ah)
    XTl = alloc("XTl", [P, KD, P], F32R, offset=o_ah + 4096)
    SG = alloc("SG", [P, FE], F32, offset=o_ah + 8192)
    Hm = alloc("Hm", [P, FE], F32, offset=o_ah + 10240)
    HTh = alloc("HTh", [P, 4, P], F32R, offset=o_ah + 12288)
    HTl = alloc("HTl", [P, 4, P], F32R, offset=o_ah + 14336)
    G12 = alloc("G12", [P, NB, 2, D], F32, offset=o_bh)
    RG = alloc("RG", [P, KD, T], F32, offset=o_bh)
    UP = alloc("UP", [P, 4, T], F32, offset=o_bl)
    bdr = alloc("bdr", [P, 16, P], F32, offset=o_bl + 16384)
    bdh = alloc("bdh", [P, 16, P], F32R, offset=o_t)
    bdl = alloc("bdl", [P, 16, P], F32R, offset=o_bl + 24576)
    Bl2 = alloc("Bl2", [P, 4, T], F32R, offset=o_bl + 16384)
    Cl = alloc("Cl", [P, KD, T], F32R, offset=o_c)
    AF = alloc("AF", [P, KD, T], F32, offset=o_ah)
    AG = alloc("AG", [P, KD, T], F32, offset=o_al)
    BG = alloc("BG", [P, KD, T], F32, offset=o_bl)
    PR = alloc("PR", [P, NB, 256], F32, offset=o_bl + 16384)
    pTh = alloc("pTh", [P, 2, T], F32R, offset=o_bl)
    pTl = alloc("pTl", [P, 2, T], F32R, offset=o_bl + 8192)

    assert at <= 229344, at

    acc = [nc.alloc_psum_tensor(f"acc{i}", [P, T], F32) for i in range(2)]
    X = [nc.alloc_psum_tensor(f"X{i}", [P, HALF], F32) for i in range(2)]
    Y = nc.alloc_psum_tensor("Y", [P, T], F32)

    dram = lambda name, shape, dt=F32: nc.dram_tensor(name, shape, dt).ap()
    x0T = dram("x0T", [D, T])
    gates1 = dram("gates1", [2 * D, T])
    nFd = dram("nFd", [NH, T])
    x1T = dram("x1T", [D, T])
    h2rows = dram("h2rows", [T, D])
    slotlist = dram("slotlist", [(SLOTS + 1) * P, 1], I32)
    ys = dram("ys", [2 * T + P, D])
    x2T = dram("x2T", [D, T])
    gates2 = dram("gates2", [2 * D, T])
    x3T = dram("x3T", [D, T])
    x4T = dram("x4T", [D, T])
    tiles = lambda t: t.rearrange("(m p) n -> p m n", p=P)

    w_land = [S("w_land0"), S("w_land1")]
    w_lo, w_used = S("w_lo"), S("w_used")
    acc_free = [S("acc_free0"), S("acc_free1")]

    W1 = A["w_in"][0].rearrange("(k p) n -> p k n", p=P)
    ADA = A["ada_w"][0].rearrange("(k p) n -> p k n", p=P)
    WPF = A["w_proj_fox"][0].rearrange("(k p) n -> p k n", p=P)
    WPD = A["w_proj_dsa"][0].rearrange("(k p) n -> p k n", p=P)
    WOUT = A["w_out"][0].rearrange("(k p) n -> p k n", p=P)
    W2 = A["w_in_2"][0].rearrange("(k p) n -> p k n", p=P)
    WPO = A["w_pool_out_2"][0].rearrange("(k p) n -> p k n", p=P)
    WRO = A["w_rg_out_2"][0].rearrange("(k p) n -> p k n", p=P)
    WO = A["w_o_2"][0].rearrange("(k p) n -> p k n", p=P)
    WUP = A["w_up_2"][0].rearrange("(k p) n -> p k n", p=P)
    WDN = A["w_down_2"][0].rearrange("(k p) n -> p k n", p=P)
    WPG = A["w_ple_gate_2"][0].rearrange("(k p) n -> p k n", p=P)
    WPP = A["w_ple_proj_2"][0].rearrange("(k p) n -> p k n", p=P)

    landed = {}
    count = [0, 0]
    for name, n in ITEMS:
        for j in range(n):
            i = N0[name] + j
            count[i % 2] += 16 * (2 if name in ("ik", "dk", "dviw") else 1)
            landed[i] = count[i % 2]

    stage = ExitStack()
    block = stage.enter_context(nc.Block())
    chains = {}

    def chain(e, name):
        if name not in chains:
            chains[name] = Chain(e, S(f"{name}_step"))
        chains[name].e = e
        return chains[name]

    taken = [0, 0]

    def take(r):
        taken[r] += 1
        return taken[r] - 1 or None

    def product_run(pe, n0, n, ih, il, k=KD, k0=0, rows=False):
        with pe.Fori(0, n // 2) as i:
            for r in range(2):
                if rows:
                    product_rows(pe, n0 + 2 * i + r, r, ih, il, i + taken[r])
                else:
                    product(pe, n0 + 2 * i + r, r, ih, il, k, k0, free=i + taken[r])
        taken[0] += n // 2
        taken[1] += n // 2

    def load(sp, n, r, src, k=KD, m=P, first=False, part=0):
        if not first:
            sp.wait_ge(w_lo, n - 1)
        sp.dma_start(wraw[:, r, 0:k, part:part + m], src).then_inc(w_land[r], 16)

    def load_run(sp, n0, n, src_of, k=KD):
        with sp.Fori(0, n // 2) as i:
            for r in range(2):
                load(sp, n0 + 2 * i + r, r, src_of(2 * i + r), k)

    def split(pool, n, r, land, k=KD, m=P, first=False):
        ch = chain(pool, "pool")
        pool.wait_ge(w_land[r], land)
        if not first:
            pool.wait_ge(w_used, n - 1)
        ch(pool.tensor_tensor(whi[:, r, 0:k, 0:m], wraw[:, r, 0:k, 0:m], one[:, 0:1].unsqueeze(2).broadcast_to([P, k, m]),
                              ALU.mult))
        pool.tensor_tensor(wlo[:, r, 0:k, 0:m], wraw[:, r, 0:k, 0:m], whi[:, r, 0:k, 0:m].bitcast(F32),
                           ALU.subtract).then_inc(w_lo, 1)

    def split_run(pool, n0, n, k=KD):
        ch = chain(pool, "pool")
        with pool.Fori(0, n // 2) as i:
            ch.enter(i, 2)
            for r in range(2):
                split(pool, n0 + 2 * i + r, r, i * 16 + landed[n0 + r], k)
            ch.leave(n // 2)

    def product(pe, n, r, ih, il, k=KD, k0=0, m=P, free=None, ready=None):
        pe.wait_ge(w_lo, n + 1)
        if free is not None:
            pe.wait_ge(acc_free[r], free)
        for j in range(k):
            if ready is not None:
                pe.wait_ge(ready[0], ready[1] + j + 1)
            for h in range(2):
                o = acc[r][0:m, h * HALF:(h + 1) * HALF]
                cols = slice(h * HALF, (h + 1) * HALF)
                pe.matmul(o, whi[:, r, j, 0:m], ih[:, k0 + j, cols], start=(j == 0), stop=False)
                pe.matmul(o, whi[:, r, j, 0:m], il[:, k0 + j, cols], start=False, stop=False)
                last = pe.matmul(o, wlo[:, r, j, 0:m], ih[:, k0 + j, cols], start=False, stop=(j == k - 1))
        last.then_inc(w_used, 1)

    def product_rows(pe, n, r, ih, il, free, m=P):
        pe.wait_ge(w_lo, n + 1)
        pe.wait_ge(acc_free[r], free)
        for b in range(NB):
            o = acc[r][:, b * P:b * P + m]
            rows = slice(b * P, (b + 1) * P)
            for j in range(KD):
                pe.matmul(o, ih[:, j, rows], whi[:, r, j, 0:m], start=(j == 0), stop=False)
                pe.matmul(o, ih[:, j, rows], wlo[:, r, j, 0:m], start=False, stop=False)
                last = pe.matmul(o, il[:, j, rows], whi[:, r, j, 0:m], start=False, stop=(j == KD - 1))
        last.then_inc(w_used, 1)


    def ada_load(sp, dst, q, k, landed_sem):
        sp.dma_start(dst, A["ada_w"][0, k * P:(k + 1) * P, q * D:(q + 1) * D]).then_inc(landed_sem, 16)

    def ada_rows(dve, ch, total, rows, k):
        if k == 0:
            ch(dve.tensor_scalar(total, rows, cact[:, 1, k:k + 1], None, ALU.mult))
        else:
            ch(dve.scalar_tensor_tensor(total, rows, cact[:, 1, k:k + 1], total, ALU.mult, ALU.add))
        dve.sem_inc(S("ada_used"), 1)

    def ada_columns(pe, total, cols, n):
        pe.wait_ge(S("ada_sum"), n)
        for m in range(KD):
            last = pe.matmul(cols[:, m:m + 1], total[:, m * P:(m + 1) * P], one[:], start=True, stop=True)
        last.then_inc(S("ada_cols"), 1)

    @block.gpsimd
    def _(pool):
        ch = chain(pool, "pool")
        for t, v in ((one, 1.0), (ident, 0.0), (identb, 0.0), (causb, 0.0), (strict, 1.0), (onesb, 1.0),
                     (meanD, 1.0 / D), (meanH, 0.0)):
            ch(pool.memset(t[:], v))
        ch(pool.memset(meanH[0:HD, 0:HD], 1.0 / HD))
        ch(pool.memset(meanH[HD:P, HD:P], 1.0 / HD))
        for t in (ident, identb):
            ch(pool.affine_select(out=t[:], in_=t[:], compare_op=ALU.not_equal, fill=1.0, base=0,
                                  pattern=[[-1, P]], channel_multiplier=1))
        ch(pool.affine_select(out=causb[:], in_=causb[:], compare_op=ALU.is_ge, fill=NEG, base=0,
                              pattern=[[-1, P]], channel_multiplier=1))
        ch(pool.affine_select(out=strict[:], in_=strict[:], compare_op=ALU.is_gt, fill=0.0, base=0,
                              pattern=[[1, P]], channel_multiplier=-1))
        pool.sem_inc(S("consts"), 1)

    @block.sync
    def _(sp):
        for t, tile in enumerate(VECTORS):
            for name, n in tile:
                r0 = VCOL[name] - t * P
                if n == 1:
                    for h in range(2):
                        sp.dma_start(vrows[r0:r0 + 1, t, h * HD:(h + 1) * HD], A[name]).then_inc(S("vec_in"), 16)
                else:
                    src = flat(A[name])
                    sp.dma_start(vrows[r0:r0 + n, t, :], src.rearrange("(j p) -> j p", p=P)).then_inc(S("vec_in"), 16)
        sp.dma_start(fb[:], flat(A["b_fgt"]).rearrange("(h a) -> h a", a=1)).then_inc(S("vec_in"), 16)
        sp.dma_start(posi[:], A["positions"].broadcast_to([P, T])).then_inc(S("pos_in"), 16)
        for q in range(2):
            for k in range(KD):
                if q:
                    sp.wait_ge(S("ada_used"), k + 1)
                ada_load(sp, adaraw[:, k, :], 1 - q, k, S(f"m_land{k}"))
        for b in range(NB):
            sp.dma_start(xrows[:, b, :], A["x"][0, b * P:(b + 1) * P, :]).then_inc(S("x_in"), 16)
        for n in range(2):
            load(sp, n, n, W1[:, :, C_IQ + n * P:C_IQ + (n + 1) * P], first=True)
        sp.wait_ge(S("xT_done"), 8)
        sp.dma_start(tiles(x0T), C[:]).then_inc(S("x0T_st"), 16)

    @block.tensor
    def _(pe):
        pe.wait_ge(S("consts"), 1)
        pe.wait_ge(S("vec_in"), 16 * N_VEC)
        for t, n in enumerate(VROWS):
            last = pe.transpose(X[0][:, t * P:t * P + n], vrows[0:n, t, :], ident[0:n, 0:n])
        last.then_inc(S("vecT"), 1)
        pe.wait_ge(S("x_in"), 16 * NB)
        for m in range(KD):
            free = take(m % 2)
            if free is not None:
                pe.wait_ge(acc_free[m % 2], free)
            for b in range(NB):
                last = pe.transpose(acc[m % 2][:, b * P:(b + 1) * P], xrows[:, b, m * P:(m + 1) * P], ident[:])
            last.then_inc(S("xT_ps"), 1)
        for q in range(2):
            ada_columns(pe, TT[:, 2 + q, :], X[1][:, (1 - q) * 8:(1 - q) * 8 + 8], q + 1)

    @block.scalar
    def _(act):
        ch = chain(act, "act")
        act.wait_ge(S("vecs"), 1)
        ch(act.activation(cact[:, 0, :], vec("c", 0, 8), ACT.Sigmoid))
        act.sem_inc(S("csig"), 1)
        for m in range(KD):
            act.wait_ge(S("xT_ps"), m + 1)
            ch(act.activation(C[:, m, :], acc[m % 2][:], ACT.Copy))
            act.sem_inc(acc_free[m % 2], 1)
            act.sem_inc(S("xT_done"), 1)

    @block.vector
    def _(dve):
        ch = chain(dve, "dve")
        dve.wait_ge(S("vecT"), 1)
        for t, n in enumerate(VROWS):
            ch(dve.tensor_copy(VEC[:, t * P:t * P + n], X[0][:, t * P:t * P + n]))
        dve.sem_inc(S("vecs"), 1)
        dve.wait_ge(S("csig"), 1)
        ch(dve.tensor_tensor(cact[:, 1, :], cact[:, 0, :], vec("c", 0, 8), ALU.mult))
        for q in range(2):
            for k in range(KD):
                dve.wait_ge(S(f"m_land{k}"), 16 * (q + 1))
                ada_rows(dve, ch, TT[:, 2 + q, :], adaraw[:, k, :], k)
            dve.sem_inc(S("ada_sum"), 1)
        dve.wait_ge(S("ada_cols"), 2)
        ch(dve.tensor_tensor(MOD[:, 0:16], X[1][:, 0:16], vec("ada_b", 0, 16), ALU.add))
        ch(dve.scalar_tensor_tensor(gm[:, 0, :], MOD[:, 8:16], 1.0, vec("norm1_g", 0, 8), ALU.add, ALU.mult))
        dve.sem_inc(S("gm1"), 1)

    def mean_square(tag, src, tmp, wait, summed=0):

        @block.scalar
        def _(act):
            ch = chain(act, "act")
            for m in range(KD):
                wait(act, m)
                if m >= 2:
                    act.wait_ge(S(tag + "_sum"), m - 1)
                ch(act.activation(tmp[:, m % 2, :], src[:, m, :], ACT.Square))
                act.sem_inc(S(tag + "_sq"), 1)
            act.wait_ge(S(tag + "_v"), 1)
            ch(act.activation(tmp[:, 2, :], tmp[:, 3, :], ACT.Ln))
            ch(act.activation(tmp[:, 2, :], tmp[:, 2, :], ACT.Exp, scale=-0.5))
            act.sem_inc(S(tag + "_root"), 1)

        @block.tensor
        def _(pe):
            pe.wait_ge(S(tag + "_sum"), KD)
            for h in range(2):
                last = pe.matmul(Y[:, h * HALF:(h + 1) * HALF], meanD[:], tmp[:, 2, h * HALF:(h + 1) * HALF],
                                 start=True, stop=True)
            last.then_inc(S(tag + "_mean"), 1)

        @block.vector
        def _(dve):
            ch = chain(dve, "dve")
            for m in range(summed, KD):
                dve.wait_ge(S(tag + "_sq"), m + 1)
                if m == 0:
                    ch(dve.tensor_copy(tmp[:, 2, :], tmp[:, 0, :]))
                else:
                    ch(dve.tensor_tensor(tmp[:, 2, :], tmp[:, 2, :], tmp[:, m % 2, :], ALU.add))
                dve.sem_inc(S(tag + "_sum"), 1)
            dve.wait_ge(S(tag + "_mean"), 1)
            ch(dve.tensor_scalar(tmp[:, 3, :], Y[:], EPS, None, ALU.add))
            dve.sem_inc(S(tag + "_v"), 1)
            dve.wait_ge(S(tag + "_root"), 1)
            newton_step(dve, ch, tmp[:, 2, :], tmp[:, 3, :])

    def newton_step(dve, ch, r, v):
        ch(dve.tensor_tensor(Y[:], r, r, ALU.mult))
        ch(dve.tensor_tensor(Y[:], Y[:], v, ALU.mult))
        ch(dve.tensor_scalar(Y[:], Y[:], -0.5, 1.5, ALU.mult, ALU.add))
        ch(dve.tensor_tensor(r, Y[:], r, ALU.mult))

    def normed(tag, src, rstd, gain, shift, dh, dl, wait, keep=False):

        @block.vector
        def _(dve):
            ch = chain(dve, "dve")

            def scale(m):
                ch(dve.scalar_tensor_tensor(src[:, m, :], src[:, m, :], gain(m), rstd, ALU.mult, ALU.mult))
                if shift is not None:
                    ch(dve.tensor_scalar(src[:, m, :], src[:, m, :], shift(m), None, ALU.add))
                dve.sem_inc(S(tag + "_scaled"), 1)

            def low(m):
                dve.wait_ge(S(tag + "_hi"), m + 1)
                dve.tensor_tensor(dl[:, m, :], src[:, m, :], dh[:, m, :].bitcast(F32), ALU.subtract)\
                   .then_inc(S(tag + "_lo"), 1)

            wait(dve)
            scale(0)
            for m in range(KD):
                if m + 1 < KD:
                    scale(m + 1)
                low(m)

        @block.scalar
        def _(act):
            for m in range(KD):
                act.wait_ge(S(tag + "_scaled"), m + 1)
                act.activation(dh[:, m, :], src[:, m, :], ACT.Copy).then_inc(S(tag + "_hi"), 1)

    N1T = alloc("N1T", [P, 4, T], F32, offset=o_bh)
    mean_square("n1", C, N1T, lambda act, m: act.wait_ge(S("xT_done"), m + 1) if m else act.wait_ge(S("xT_ps"), 8))

    def n1_wait(dve):
        dve.wait_ge(S("x0T_st"), 16)
    normed("n1", C, N1T[:, 2, :], lambda m: gm[:, 0, m:m + 1], lambda m: MOD[:, m:m + 1], Ah, Al, n1_wait)

    def rotate(dve, ch, x, swapped, tmp):
        ch(dve.tensor_tensor(tmp, x, TT[:, 0, :], ALU.mult))
        ch(dve.tensor_tensor(swapped, swapped, TT[:, 1, :], ALU.mult))
        ch(dve.tensor_tensor(x, tmp, swapped, ALU.add))

    def swap_halves(act, dst, src, done):
        for q in range(4):
            act.dma_start(dst[32 * q:32 * q + 32, :], src[32 * (q ^ 1):32 * (q ^ 1) + 32, :]).then_inc(done, 16)

    BY_ACT = (2, 5, 7)
    SEARCH = 30
    roped = [IQ[:, j, :] for j in range(4)] + [IK[:], KX[:]]
    SCb = [SC[:, SCO[b]:SCO[b] + SCW[b]] for b in range(NB)]
    index_units = [(b, h) for b in range(2, NB) for h in range(NH)]

    @block.sync
    def _(sp):
        for n in (2, 3):
            load(sp, n, n % 2, W1[:, :, C_IQ + n * P:C_IQ + (n + 1) * P])
        load(sp, 4, 0, W1[:, :, C_IK:C_IK + HD], m=HD)
        load(sp, 4, 0, W1[:, :, C_IK:C_IK + HD], m=HD, part=HD, first=True)
        load(sp, 5, 1, W1[:, :, C_DV:C_DV + HD], m=HD)
        load(sp, 5, 1, W1[:, :, C_IW:C_IW + 8], m=8, part=HD, first=True)
        for j in range(4):
            load(sp, 6 + j, j % 2, W1[:, :, C_FV + j * P:C_FV + (j + 1) * P])
        load(sp, 10, 0, W1[:, :, C_FL:C_FL + 8], m=8)
        load(sp, 11, 1, W1[:, :, C_DK:C_DK + HD], m=HD)
        load(sp, 11, 1, W1[:, :, C_DK:C_DK + HD], m=HD, part=HD, first=True)
        for q in range(4):
            for k in range(KD):
                n = KD * q + k
                if n == 0:
                    sp.wait_ge(S("n1_scaled"), KD)
                if n >= 2:
                    sp.wait_ge(S("ada_used"), 16 + n - 1)
                ada_load(sp, E[:, (3, 7)[k % 2], :], 2 + q, k, S(f"ada2_land{k % 2}"))
        load_run(sp, N0["gates"], 16, lambda j: W1[:, :, ds(j * P + C_G, P)])
        load_run(sp, N0["qkd"], 8, lambda j: W1[:, :, ds(j * P + C_FQ, P)])
        load_run(sp, N0["qkd"] + 8, 4, lambda j: W1[:, :, ds(j * P + C_DQ, P)])

    @block.gpsimd
    def _(pool):
        for n in range(12):
            split(pool, n, n % 2, landed[n], m={5: 72, 10: NH}.get(n, P), first=n < 2)
        split_run(pool, N0["gates"], 16)
        split_run(pool, N0["qkd"], 12)

    @block.tensor
    def _(pe):
        def to_rows(n, m):
            pe.wait_ge(S("v_cols"), n - 4)
            if n > 5:
                pe.wait_ge(S("v_rows"), n - 5)
            for b in range(NB):
                last = pe.transpose(Y[:, b * P:b * P + m], E[0:m, 4 + n % 2, b * P:(b + 1) * P], ident[0:m, 0:m])
            last.then_inc(S("v_turned"), 1)

        for n in range(12):
            product(pe, n, n % 2, Ah, Al, free=take(n % 2), ready=(S("n1_lo"), 0) if n == 0 else None,
                    m={5: 72, 10: NH}.get(n, P))
            if 6 <= n <= 10:
                to_rows(n - 1, 72 if n == 6 else P)
        pe.wait_ge(S("v_rows"), 5)
        for q in range(4):
            ada_columns(pe, TT[:, 2 + q % 2, :], Y[:, q * 8:q * 8 + 8], q + 3)

        pe.wait_ge(S("roped"), 5)
        for u, (b, h) in enumerate(index_units):
            pe.wait_ge(acc_free[u % 2], take(u % 2))
            rows = slice(HD * (h % 2), HD * (h % 2) + HD)
            for c in range(0, SCW[b], HALF):
                w = min(HALF, SCW[b] - c)
                last = pe.matmul(acc[u % 2][:, c:c + w], IQ[rows, h // 2, b * P:(b + 1) * P],
                                 IK[rows, c:c + w], start=True, stop=True)
            last.then_inc(S("dots"), 1)
            if u == 0:
                pe.wait_ge(S("mod2"), 1)
                pe.wait_ge(S("k_sq"), 1)
                for h2 in range(2):
                    last = pe.matmul(Y[:, h2 * HALF:(h2 + 1) * HALF], meanH[:], E[:, 4, h2 * HALF:(h2 + 1) * HALF],
                                     start=True, stop=True)
                last.then_inc(S("k_mean"), 1)
        product_run(pe, N0["gates"], 16, Ah, Al)

        def q_mean(j):
            pe.wait_ge(S("q_sq"), j + 1)
            for h in range(2):
                last = pe.matmul(Y[:, h * HALF:(h + 1) * HALF], meanH[:], TT[:, 2, h * HALF:(h + 1) * HALF],
                                 start=True, stop=True)
            last.then_inc(S("q_mean"), 1)

        n0 = N0["qkd"]
        product(pe, n0, 0, Ah, Al, free=take(0))
        with pe.Fori(0, 5) as i:
            product(pe, n0 + 1 + 2 * i, 1, Ah, Al, free=i + taken[1])
            q_mean(2 * i)
            product(pe, n0 + 2 + 2 * i, 0, Ah, Al, free=i + taken[0])
            q_mean(2 * i + 1)
        taken[0] += 5
        taken[1] += 5
        product(pe, n0 + 11, 1, Ah, Al, free=take(1))
        q_mean(10)
        q_mean(11)

    @block.scalar
    def _(act):
        ch = chain(act, "act")

        def out_of(n, dst, src, func=ACT.Copy, **kw):
            act.wait_ge(w_used, n + 1)
            ch(act.activation(dst, src, func, **kw))
            act.sem_inc(acc_free[n % 2], 1)

        act.wait_ge(S("angles"), 1)
        ch(act.activation(trig[:, 3, :], trig[:, 1, :], ACT.Sin))
        ch(act.activation(TT[:, 0, :], trig[:, 2, :], ACT.Sin))
        act.sem_inc(S("sines"), 1)
        for j in range(4):
            out_of(j, IQ[:, j, :], acc[j % 2][:])
            if j >= 2:
                act.wait_ge(S("roped"), j - 1)
            swap_halves(act, E[:, 2 * (j % 2), :], IQ[:, j, :], S(f"swapped{j % 2}"))
        out_of(4, IK[:], acc[0][:])
        act.wait_ge(S("roped"), 3)
        swap_halves(act, E[:, 0, :], IK[:], S("swapped0"))
        def from_rows(n):
            act.wait_ge(S("v_turned"), n - 4)
            rows = Y[:].rearrange("p (b n) -> p b n", b=NB)
            if n == 5:
                ch(act.activation(DV[:], rows[:, :, 0:72], ACT.Copy))
            else:
                ch(act.activation(V[:, :, (n - 6) * P:(n - 5) * P], rows, ACT.Copy))
            act.sem_inc(S("v_rows"), 1)

        for n in range(5, 10):
            m = 72 if n == 5 else P
            out_of(n, E[0:m, 4 + n % 2, :], acc[n % 2][0:m, :])
            act.sem_inc(S("v_cols"), 1)
            if n >= 6:
                from_rows(n - 1)
        from_rows(9)
        out_of(10, FS[:, 0, :], acc[0][0:NH, :], ACT.Identity, bias=fb[:])
        act.sem_inc(S("forget"), 1)
        act.wait_ge(S("roped"), 5)
        out_of(11, KX[:], acc[1][:])
        ch(act.activation(E[:, 4, :], KX[:], ACT.Square))
        act.sem_inc(S("k_sq"), 1)
        act.wait_ge(S("forget_abs"), 1)
        ch(act.activation(FS[:, 1, :], FS[:, 1, :], ACT.Exp, scale=-1.0))
        ch(act.activation(FS[:, 2, :], FS[:, 1, :], ACT.Ln, bias=1.0))
        act.sem_inc(S("forget_ln"), 1)
        act.wait_ge(S("k_v"), 1)
        ch(act.activation(E[:, 4, :], E[:, 5, :], ACT.Ln))
        ch(act.activation(E[:, 4, :], E[:, 4, :], ACT.Exp, scale=-0.5))
        act.sem_inc(S("k_root"), 1)
        act.wait_ge(S("k_normed"), 1)
        swap_halves(act, E[:, 2, :], KX[:], S("swapped1"))
        for u, (b, h) in enumerate(index_units):
            act.wait_ge(S("dots"), u + 1)
            if u >= 2:
                act.wait_ge(S("index_sum"), u - 1)
            ch(act.activation(E[:, 4 + u % 2, 0:SCW[b]], acc[u % 2][:, 0:SCW[b]], ACT.Relu))
            act.sem_inc(acc_free[u % 2], 1)
            act.sem_inc(S("relu"), 1)
        for r in range(2):
            act.sem_inc(S(f"gates1_st{r}"), 16)
        def gate_tiles(i0, n, searches):
            with act.Fori(0, n) as i:
                ch.enter(i, 2 + 2 * searches * len(BY_ACT))
                for r in range(2):
                    j = 2 * i + 2 * i0 + r
                    act.wait_ge(w_used, N0["gates"] + j + 1)
                    act.wait_ge(S(f"gates1_st{r}"), i * 16 + 16 * (i0 + 1))
                    ch(act.activation(TT[:, 2 + r, :], acc[r][:], ACT.Sigmoid, bias=vecd("b_gate", j)))
                    act.sem_inc(acc_free[r], 1)
                    act.dma_start(gates1[ds(j * P, P), :], TT[:, 2 + r, :]).then_inc(S(f"gates1_st{r}"), 16)
                    for q in range(searches):
                        act.wait_ge(S("mid"), i * (2 * searches) + r * searches + q + 1)
                        for b in BY_ACT:
                            ch(act.activation(E[:, 5, 0:SCW[b]], SCb[b], ACT.Sign, bias=bs[:, 5, b - 2:b - 1],
                                              accum_out=bs[:, 3, b - 2:b - 1]))
                        act.sem_inc(S("signs"), 1)
                ch.leave(n)

        gate_tiles(0, 5, SEARCH // 10)
        gate_tiles(5, 3, 0)
        for r in range(2):
            act.wait_ge(S(f"gates1_st{r}"), 16 * 9)
        act.wait_ge(S("masks"), 1)
        with act.Fori(0, 6) as i:
            ch.enter(i, 8)
            for r in range(2):
                j = 2 * i + r
                act.wait_ge(w_used, N0["qkd"] + j + 1)
                act.wait_ge(S("q_normed"), j + 1)
                ch(act.activation(QKD[:, ds(j, 1), :].rearrange("p a n -> p (a n)"), acc[r][:], ACT.Copy))
                ch(act.activation(TT[:, 2, :], acc[r][:], ACT.Square))
                act.sem_inc(acc_free[r], 1)
                act.sem_inc(S("q_sq"), 1)
                act.wait_ge(S("q_v"), j + 1)
                ch(act.activation(TT[:, 2, :], TT[:, 3, :], ACT.Ln))
                ch(act.activation(TT[:, 2, :], TT[:, 2, :], ACT.Exp, scale=-0.5))
                act.sem_inc(S("q_root"), 1)
            ch.leave(6)
        act.wait_ge(S("q_normed"), 13)
        for j in range(4):
            if j:
                act.wait_ge(S("q_roped"), j)
            swap_halves(act, TT[:, 3, :], QKD[:, 8 + j, :], S("swapped_q"))

    @block.vector
    def _(dve):
        ch = chain(dve, "dve")
        dve.wait_ge(S("pos_in"), 16)
        a, n, u = trig[:, 0, :], trig[:, 1, :], trig[:, 2, :]
        ch(dve.tensor_copy(u, posi[:]))
        ch(dve.tensor_scalar(a, u, vec("freq"), None, ALU.mult))
        ch(dve.tensor_scalar(n, a, 1.0 / TWO_PI, ROUND, ALU.mult, ALU.add))
        ch(dve.tensor_scalar(n, n, ROUND, None, ALU.subtract))
        for part in split_two_pi():
            ch(dve.scalar_tensor_tensor(a, n, -part, a, ALU.mult, ALU.add))
        ch(dve.tensor_scalar(u, a, float(np.float32(np.pi / 2)), -TWO_PI, ALU.is_gt, ALU.mult))
        ch(dve.scalar_tensor_tensor(u, a, float(np.pi / 2), u, ALU.add, ALU.add))
        ch(dve.tensor_scalar(n, a, PI_IN, -PI_IN, ALU.min, ALU.max))
        ch(dve.tensor_scalar(u, u, PI_IN, -PI_IN, ALU.min, ALU.max))
        dve.sem_inc(S("angles"), 1)
        dve.wait_ge(S("sines"), 1)
        ch(dve.tensor_scalar(TT[:, 1, :], trig[:, 3, :], vec("freq", 1), None, ALU.mult))
        for j in range(13):
            src = "qn_fox" if j < 4 else "kn_fox" if j < 8 else "qn_dsa" if j < 12 else "kn_dsa"
            ch(dve.tensor_copy(gq[:, j:j + 1], vec(src)))

        def rope(j, swaps):
            dve.wait_ge(S(f"swapped{j % 2}"), 64 * swaps)
            rotate(dve, ch, roped[j], E[:, 2 * (j % 2), :], E[:, 1, :])
            dve.sem_inc(S("roped"), 1)
        for j in range(5):
            rope(j, j // 2 + 1)

        dve.wait_ge(S("forget"), 1)
        z, e, l, t = (FS[:, k, :] for k in range(4))
        ch(dve.scalar_tensor_tensor(e, z, -1.0, z, ALU.mult, ALU.max))
        dve.sem_inc(S("forget_abs"), 1)
        dve.wait_ge(S("forget_ln"), 1)
        ch(dve.tensor_scalar(t, e, 1.0, 1.0, ALU.add, ALU.subtract))
        ch(dve.tensor_scalar(t, t, 1e-30, None, ALU.max))
        ch(dve.reciprocal(t, t))
        ch(dve.tensor_tensor(t, t, e, ALU.mult))
        ch(dve.tensor_scalar(t, t, 2.0, None, ALU.min))
        ch(dve.tensor_tensor(l, l, t, ALU.mult))
        ch(dve.tensor_scalar(z, z, 0.0, None, ALU.min))
        ch(dve.tensor_tensor_scan(nF[:], z, l, 0.0, ALU.add, ALU.subtract))
        ch(dve.tensor_scalar(nF[:], nF[:], -1.0 / SCALE, None, ALU.mult))
        dve.sem_inc(S("nF_done"), 1)

        for q in range(4):
            if q >= 2:
                dve.wait_ge(S("ada_cols"), q + 1)
            for k in range(KD):
                dve.wait_ge(S("ada2_land%d" % (k % 2)), 16 * (4 * q + k // 2 + 1))
                ada_rows(dve, ch, TT[:, 2 + q % 2, :], E[:, (3, 7)[k % 2], :], k)
            dve.sem_inc(S("ada_sum"), 1)
        dve.wait_ge(S("ada_cols"), 6)
        ch(dve.tensor_tensor(MOD[:, 16:48], Y[:, 0:32], vec("ada_b", 16, 32), ALU.add))
        ch(dve.scalar_tensor_tensor(gm[:, 1, :], MOD[:, 32:40], 1.0, vec("norm2_g", 0, 8), ALU.add, ALU.mult))
        dve.sem_inc(S("mod2"), 1)

        dve.wait_ge(S("k_mean"), 1)
        ch(dve.tensor_scalar(E[:, 5, :], Y[:], EPS, None, ALU.add))
        dve.sem_inc(S("k_v"), 1)
        dve.wait_ge(S("k_root"), 1)
        newton_step(dve, ch, E[:, 4, :], E[:, 5, :])
        ch(dve.scalar_tensor_tensor(KX[:], KX[:], gq[:, 12:13], E[:, 4, :], ALU.mult, ALU.mult))
        dve.sem_inc(S("k_normed"), 1)
        rope(5, 3)

        dve.wait_ge(S("v_rows"), 1)
        for u, (b, h) in enumerate(index_units):
            dve.wait_ge(S("relu"), u + 1)
            e, w = E[:, 4 + u % 2, 0:SCW[b]], DV[:, b, HD + h:HD + h + 1]
            if h == 0:
                ch(dve.tensor_scalar(SCb[b], e, w, None, ALU.mult))
            else:
                ch(dve.scalar_tensor_tensor(SCb[b], e, w, SCb[b], ALU.mult, ALU.add))
            dve.sem_inc(S("index_sum"), 1)

        lo, hi, mid, cnt, goal, nmid, t1, t2, need = (bs[:, k, 0:6] for k in range(9))
        for b in range(2, NB):
            c = slice(b - 2, b - 1)
            ch(dve.tensor_reduce(lo[:, c], SCb[b], AX.X, ALU.min))
            ch(dve.tensor_reduce(mid[:, c], SCb[b], AX.X, ALU.max))
            ch(dve.memset(goal[:, c], float(2 * TOPK - SCW[b] if b in BY_ACT else TOPK)))
        ch(dve.scalar_tensor_tensor(cnt, mid, -1.0, mid, ALU.mult, ALU.max))
        ch(dve.scalar_tensor_tensor(hi, cnt, 2.0 ** -20, mid, ALU.mult, ALU.add))
        ch(dve.tensor_scalar(hi, hi, 1e-30, None, ALU.add))
        for b in range(2, NB):
            ch(dve.memset(SC[0:HD, SCO[b] + b * P + HD:SCO[b] + (b + 1) * P], NEG))
        with dve.Fori(0, SEARCH) as i:
            ch.enter(i, 9 + NB - 2 - len(BY_ACT))
            ch(dve.tensor_tensor(t1, lo, hi, ALU.add))
            ch(dve.tensor_scalar(mid, t1, 0.5, None, ALU.mult))
            ch(dve.tensor_scalar(nmid, t1, -0.5, None, ALU.mult))
            dve.sem_inc(S("mid"), 1)
            for b in range(2, NB):
                if b not in BY_ACT:
                    ch(dve.tensor_scalar(junk[:, 0:SCW[b]], SCb[b], mid[:, b - 2:b - 1], None, ALU.is_ge, ALU.add,
                                         accum_out=cnt[:, b - 2:b - 1]))
            dve.wait_ge(S("signs"), i + 1)
            ch(dve.tensor_tensor(t1, cnt, goal, ALU.is_ge))
            ch(dve.scalar_tensor_tensor(t2, t1, FAR, mid, ALU.mult, ALU.add))
            ch(dve.tensor_tensor(hi, hi, t2, ALU.min))
            ch(dve.tensor_scalar(t1, t1, 1.0, FAR, ALU.subtract, ALU.mult))
            ch(dve.tensor_tensor(t2, t1, mid, ALU.add))
            ch(dve.tensor_tensor(lo, lo, t2, ALU.max))
            ch.leave(SEARCH)
        for b in range(2, NB):
            w, c = SCW[b], slice(b - 2, b - 1)
            above, tied, rank = E[:, 0, 0:w], E[:, 1, 0:w], E[:, 3, 0:w]
            ch(dve.tensor_scalar(above, SCb[b], hi[:, c], None, ALU.is_gt, ALU.add, accum_out=cnt[:, c]))
            ch(dve.tensor_scalar(need[:, c], cnt[:, c], -1.0, float(TOPK), ALU.mult, ALU.add))
            ch(dve.scalar_tensor_tensor(tied, SCb[b], lo[:, c], above, ALU.is_ge, ALU.subtract))
            ch(dve.tensor_tensor_scan(rank, tied, above, 0.0, ALU.add, ALU.bypass))
            ch(dve.scalar_tensor_tensor(tied, rank, need[:, c], tied, ALU.is_le, ALU.mult))
            ch(dve.tensor_tensor(above, above, tied, ALU.add))
            ch(dve.tensor_scalar(SCb[b], above, 1.0, -NEG, ALU.subtract, ALU.mult))
        for b in range(2):
            ch(dve.memset(SCb[b], 0.0))
            ch(dve.memset(SC[0:HD, SCO[b] + b * P + HD:SCO[b] + (b + 1) * P], NEG))
        dve.sem_inc(S("masks"), 1)

        dve.sem_inc(S("q_normed"), 1)
        with dve.Fori(0, 12) as j:
            ch.enter(j, 6)
            dve.wait_ge(S("q_mean"), j + 1)
            ch(dve.tensor_scalar(TT[:, 3, :], Y[:], EPS, None, ALU.add))
            dve.sem_inc(S("q_v"), 1)
            dve.wait_ge(S("q_root"), j + 1)
            newton_step(dve, ch, TT[:, 2, :], TT[:, 3, :])
            q = QKD[:, ds(j, 1), :].rearrange("p a n -> p (a n)")
            ch(dve.scalar_tensor_tensor(q, q, gq[:, ds(j, 1)], TT[:, 2, :], ALU.mult, ALU.mult))
            dve.sem_inc(S("q_normed"), 1)
            ch.leave(12)
        for j in range(4):
            dve.wait_ge(S("swapped_q"), 64 * (j + 1))
            rotate(dve, ch, QKD[:, 8 + j, :], TT[:, 3, :], TT[:, 2, :])
            dve.sem_inc(S("q_roped"), 1)

    units = [(kind, h, b) for kind in ("fox", "dsa") for h in range(NH) for b in range(NB)]
    groups = [[(c, min(4, b + 1 - c)) for c in range(0, b + 1, 4)] for _, _, b in units]
    g0 = [sum(len(g) for g in groups[:u]) for u in range(len(units) + 1)]
    nmax, psum = (lambda u: att[:, 0, u % 2:u % 2 + 1]), (lambda u: att[:, 1, u % 2:u % 2 + 1])
    rinv = lambda u: att[:, 2, u % 2:u % 2 + 1]
    pmax = lambda u: att[:, 3, u % 2:u % 2 + 1]

    @block.sync
    def _(sp):
        sp.wait_ge(S("nF_done"), 1)
        sp.dma_start(nFd, nF[:]).then_inc(S("nF_st"), 16)
        sp.wait_ge(S("nF_st"), 16)
        sp.wait_ge(w_used, N0["qkd"] + 12)
        for h in range(NH):
            sp.dma_start(nFb[h][:], nFd[h:h + 1, :].broadcast_to([P, T])).then_inc(S("nF_in"), 16)

    @block.tensor
    def _(pe):
        def scores(u):
            kind, h, b = units[u]
            rows = slice(HD * (h % 2), HD * (h % 2) + HD)
            pe.wait_ge(acc_free[u % 2], take(u % 2))
            q, k = (QKD[rows, h // 2, :], QKD[rows, 4 + h // 2, :]) if kind == "fox" else \
                   (QKD[rows, 8 + h // 2, :], KX[rows, :])
            for c in range(0, SCW[b], HALF):
                w = min(HALF, SCW[b] - c)
                diagonal = kind == "fox" and c + w == SCW[b]
                last = pe.matmul(acc[u % 2][:, c:c + w], q[:, b * P:(b + 1) * P], k[:, c:c + w],
                                 start=True, stop=not diagonal)
            if kind == "fox":
                last = pe.matmul(acc[u % 2][:, b * P:(b + 1) * P], identb[:], causb[:], start=False, stop=True)
            last.then_inc(S("s_ps"), 1)

        def turn(u):
            pe.wait_ge(S("p_ready"), u + 1)
            for i, (c, n) in enumerate(groups[u]):
                g = g0[u] + i
                if g >= 2:
                    pe.wait_ge(S("pt_ready"), g - 1)
                for j in range(n):
                    last = pe.transpose(X[g % 2][:, j * P:(j + 1) * P], Pb[u % 2][:, (c + j) * P:(c + j + 1) * P],
                                        ident[:])
                last.then_inc(S("p_turned"), 1)

        def values(u):
            kind, h, b = units[u]
            if u >= NB and b % 4 == 0:
                pe.wait_ge(S("o_out"), 2 * (u // NB - 1) + b // 4 + 1)
            pe.wait_ge(S("pt_ready"), g0[u + 1])
            out_ = Y[HD * (h % 2):HD * (h % 2) + HD, b * P:(b + 1) * P]
            for k in range(b + 1):
                v = V[:, k, h * HD:(h + 1) * HD] if kind == "fox" else DV[:, k, 0:HD]
                last = pe.matmul(out_, v, PT[u % 2][:, k, :], start=(k == 0), stop=(k == b))
            last.then_inc(S("pv"), 1)

        pe.wait_ge(S("q_normed"), 13)
        scores(0)
        scores(1)
        for u in range(len(units)):
            turn(u)
            if u:
                values(u - 1)
            if u + 2 < len(units):
                if u + 2 == NB * NH:
                    pe.wait_ge(S("q_roped"), 4)
                scores(u + 2)
        values(len(units) - 1)

    @block.vector
    def _(dve):
        ch = chain(dve, "dve")

        def biased(u):
            kind, h, b = units[u]
            w = SCW[b]
            dve.wait_ge(S("s_ps"), u + 1)
            if kind == "fox" and b == 0:
                dve.wait_ge(S("nF_in"), 16 * NH)
            if u >= 2:
                dve.wait_ge(S("p_turned"), g0[u - 1])
            bias = nFb[h][:, 0:w] if kind == "fox" else SCb[b]
            ch(dve.tensor_tensor_reduce(Pb[u % 2][:, 0:w], acc[u % 2][:, 0:w], bias, 1.0, -3e38, ALU.add, ALU.max,
                                        pmax(u)))
            dve.sem_inc(acc_free[u % 2], 1)
            ch(dve.tensor_scalar(nmax(u), pmax(u), -SCALE, None, ALU.mult))
            dve.sem_inc(S("s_max"), 1)

        def scaled(u):
            dve.wait_ge(S("exps"), u + 1)
            ch(dve.reciprocal(rinv(u), psum(u)))
            w = SCW[units[u][2]]
            dve.tensor_scalar(Pb[u % 2][:, 0:w], Pb[u % 2][:, 0:w], rinv(u), None, ALU.mult).then_inc(S("p_ready"), 1)

        biased(0)
        for u in range(len(units)):
            if u + 1 < len(units):
                biased(u + 1)
            scaled(u)

    @block.scalar
    def _(act):
        ch = chain(act, "act")

        def exps(u):
            w = SCW[units[u][2]]
            act.wait_ge(S("s_max"), u + 1)
            act.activation(Pb[u % 2][:, 0:w], Pb[u % 2][:, 0:w], ACT.Exp, bias=nmax(u), scale=SCALE,
                           accum_out=psum(u)).then_inc(S("exps"), 1)

        def turned(u):
            if u >= 2:
                act.wait_ge(S("pv"), u - 1)
            for i, (c, n) in enumerate(groups[u]):
                g = g0[u] + i
                act.wait_ge(S("p_turned"), g + 1)
                act.activation(PT[u % 2][:, c:c + n, :], X[g % 2][:, 0:n * P].rearrange("p (a b) -> p a b", b=P),
                               ACT.Copy).then_inc(S("pt_ready"), 1)

        def out_of_bank(u):
            kind, h, b = units[u]
            act.wait_ge(S("pv"), u + 1)
            rows = slice(HD * (h % 2), HD * (h % 2) + HD)
            cols = slice((b - 3) * P, (b + 1) * P)
            dst = OF if kind == "fox" else OD
            act.activation(dst[rows, h // 2, cols], Y[rows, cols], ACT.Copy).then_inc(S("o_out"), 1)

        act.wait_ge(S("q_roped"), 4)
        exps(0)
        exps(1)
        for u in range(len(units)):
            turned(u)
            if u and units[u - 1][2] % 4 == 3:
                out_of_bank(u - 1)
            if u + 2 < len(units):
                exps(u + 2)
        out_of_bank(len(units) - 1)
        act.wait_ge(S("pv"), len(units))
        act.wait_ge(S("o_out"), 32)
        for j in range(8):
            src = OF if j < 4 else OD
            act.activation(Ah[:, j, :], src[:, j % 4, :], ACT.Copy).then_inc(S("o_hi"), 1)

    @block.vector
    def _(dve):
        ch = chain(dve, "dve")
        for j in range(8):
            dve.wait_ge(S("o_hi"), 8 if j == 4 else j + 1)
            src = OF if j < 4 else OD
            ch(dve.tensor_tensor(Al[:, j, :], src[:, j % 4, :], Ah[:, j, :].bitcast(F32), ALU.subtract))
            dve.sem_inc(S("o_lo"), 1)

    @block.sync
    def _(sp):
        def weights(m):
            n = 2 * m + N0["proj"]
            load(sp, n, 0, WPF[:, :, ds(m * P, P)], k=4)
            load(sp, n + 1, 1, WPD[:, :, ds(m * P, P)], k=4)

        def gate_pair(m, r):
            for g in range(2):
                sp.dma_start(TT[:, 2 * r + g, :], gates1[ds(m * P + g * D, P), :]).then_inc(S(f"gate_in{r}"), 16)
        for m in range(2):
            weights(m)
        sp.wait_ge(S("o_lo"), 8)
        for m in range(2):
            gate_pair(m, m)
        with sp.Fori(1, 4) as i:
            for r in range(2):
                weights(2 * i + r)
                sp.wait_ge(S("merged"), 2 * i + r - 1)
                gate_pair(2 * i + r, r)
        sp.dma_start(C[:], tiles(x0T)).then_inc(S("x0T_in"), 16)
        load_run(sp, N0["wout"], 8, lambda m: WOUT[:, :, ds(m * P, P)])

    @block.gpsimd
    def _(pool):
        split_run(pool, N0["proj"], 16, k=4)
        split_run(pool, N0["wout"], 8)

    @block.tensor
    def _(pe):
        pe.wait_ge(S("o_lo"), 8)
        with pe.Fori(0, 8) as m:
            for r in range(2):
                product(pe, 2 * m + N0["proj"] + r, r, Ah, Al, 4, 4 * r, free=m + taken[r])
        taken[0] += 8
        taken[1] += 8
        pe.wait_ge(S("merged"), 8)
        product_run(pe, N0["wout"], 8, Bh, Bl)

    row = lambda t, j: t[:, ds(j, 1), :].rearrange("p a n -> p (a n)")

    @block.vector
    def _(dve):
        ch = chain(dve, "dve")
        with dve.Fori(0, 4) as i:
            ch.enter(i, 8)
            for r in range(2):
                m = 2 * i + r
                dve.wait_ge(S(f"gate_in{r}"), i * 32 + 32)
                for g in range(2):
                    dve.wait_ge(w_used, 2 * m + N0["proj"] + g + 1)
                    ch(dve.tensor_tensor(TT[:, 2 * r + g, :], TT[:, 2 * r + g, :], acc[g][:], ALU.mult))
                    dve.sem_inc(acc_free[g], 1)
                ch(dve.tensor_tensor(TT[:, 2 * r, :], TT[:, 2 * r, :], TT[:, 2 * r + 1, :], ALU.add))
                dve.sem_inc(S("merge_sum"), 1)
                dve.wait_ge(S("merge_hi"), m + 1)
                ch(dve.tensor_tensor(row(Bl, m), TT[:, 2 * r, :], row(Bh, m).bitcast(F32), ALU.subtract))
                dve.sem_inc(S("merged"), 1)
            ch.leave(4)
        dve.wait_ge(S("x0T_in"), 16)
        for m in range(KD):
            dve.wait_ge(w_used, N0["wout"] + m + 1)
            ch(dve.scalar_tensor_tensor(C[:, m, :], acc[m % 2][:], MOD[:, 16 + m:17 + m], C[:, m, :],
                                        ALU.mult, ALU.add))
            dve.sem_inc(acc_free[m % 2], 1)
            dve.sem_inc(S("x1_done"), 1)

    @block.scalar
    def _(act):
        ch = chain(act, "act")
        with act.Fori(0, 4) as i:
            for r in range(2):
                m = 2 * i + r
                act.wait_ge(S("merge_sum"), m + 1)
                act.activation(row(Bh, m), TT[:, 2 * r, :], ACT.Copy).then_inc(S("merge_hi"), 1)

    @block.sync
    def _(sp):
        for m in range(KD):
            sp.wait_ge(S("x1_done"), m + 1)
            sp.dma_start(x1T[m * P:(m + 1) * P, :], C[:, m, :]).then_inc(S("x1T_st"), 16)

    def squares_after_merge(act, m):
        if m == 0:
            act.wait_ge(S("merged"), 8)
        act.wait_ge(S("x1_done"), m + 1)
    mean_square("n2", C, TT, squares_after_merge)
    normed("n2", C, TT[:, 2, :], lambda m: gm[:, 1, m:m + 1], lambda m: MOD[:, 24 + m:25 + m], Ah, Al,
           lambda dve: dve.wait_ge(S("x1T_st"), 16 * KD))

    LOGITS = N_GRP + N_EXP

    @block.sync
    def _(sp):
        sp.wait_ge(S("x1T_st"), 16 * KD)
        sp.wait_ge(w_used, N0["wout"] + 8)
        sp.dma_start(rw[:, :, 0:N_GRP], A["router_w_grp"][0].rearrange("(k p) n -> p k n", p=P)).then_inc(S("rt_in"), 16)
        sp.dma_start(rw[:, :, N_GRP:], A["router_w_exp"][0].rearrange("(k p) n -> p k n", p=P)).then_inc(S("rt_in"), 16)
        sp.dma_start(rbias[:, 0:N_GRP], A["router_b_grp"].broadcast_to([P, N_GRP])).then_inc(S("rt_in"), 16)
        sp.dma_start(rbias[:, N_GRP:], A["router_b_exp"].broadcast_to([P, N_EXP])).then_inc(S("rt_in"), 16)
        sp.dma_start(rI[:], A["from_end"].broadcast_to([P, N_EXP])).then_inc(S("rt_in"), 16)
        sp.dma_start(rTk[:], A["result_row"]).then_inc(S("rt_in"), 16)
        sp.dma_start(rZ[:], A["no_row"].broadcast_to([SLOTS + 1, P])).then_inc(S("none_in"), 16)
        sp.wait_ge(S("none_in"), 16)
        sp.dma_start(slotlist.rearrange("(s p) a -> s (p a)", p=P), rZ[:]).then_inc(S("none_st"), 16)
        for b in range(NB):
            sp.wait_ge(S("h2_row"), b + 1)
            sp.dma_start(h2rows[b * P:(b + 1) * P, :], hrow[:, b, :]).then_inc(S("h2_st"), 16)
        sp.wait_ge(S("scattered"), 16 * 2 * NB)
        sp.dma_start(rLi[:], slotlist.rearrange("(s p) a -> s (p a)", p=P)).then_inc(S("list_in"), 16)

    @block.gpsimd
    def _(pool):
        pool.wait_ge(S("none_st"), 16)
        pool.wait_ge(S("rt_in"), 16 * 6)
        pool.wait_ge(S("placed"), 1)
        for k in range(2):
            for b in range(NB):
                pool.indirect_dma_start(slotlist, bass.IndirectOffsetOnAxis(ap=POS[:, k, b:b + 1], axis=0),
                                        rTk[:, k, b:b + 1], None).then_inc(S("scattered"), 16)

    @block.tensor
    def _(pe):
        pe.wait_ge(S("rt_split"), 1)
        pe.wait_ge(S("n2_lo"), KD)
        for b in range(NB):
            o, rows = Y[:, b * LOGITS:(b + 1) * LOGITS], slice(b * P, (b + 1) * P)
            for j in range(KD):
                pe.matmul(o, Ah[:, j, rows], rwh[:, j, :], start=(j == 0), stop=False)
                pe.matmul(o, Ah[:, j, rows], rwl[:, j, :], start=False, stop=False)
                last = pe.matmul(o, Al[:, j, rows], rwh[:, j, :], start=False, stop=(j == KD - 1))
        last.then_inc(S("logits"), 1)
        for b in range(NB):
            pe.wait_ge(acc_free[b % 2], take(b % 2))
            for m in range(KD):
                last = pe.transpose(acc[b % 2][:, m * P:(m + 1) * P], C[:, m, b * P:(b + 1) * P], ident[:])
            last.then_inc(S("h2_turned"), 1)
        pe.wait_ge(S("chosen"), 1)
        for b in range(NB + 1):
            o = Y[:, HALF + b * N_EXP:HALF + (b + 1) * N_EXP]
            if b < NB:
                last = pe.matmul(o, strict[:], rOb[:, b, :], start=True, stop=(b == 0))
            for c in range(b):
                last = pe.matmul(o, onesb[:], rOb[:, c, :], start=(b == NB and c == 0), stop=(c == b - 1))
        last.then_inc(S("ranks"), 1)
        pe.wait_ge(S("list_f"), 1)
        pe.transpose(X[0][:, 0:SLOTS + 1], rLf[:], ident[0:SLOTS + 1, 0:SLOTS + 1]).then_inc(S("list_turned"), 1)

    @block.scalar
    def _(act):
        ch = chain(act, "act")
        for b in range(NB):
            act.wait_ge(S("h2_turned"), b + 1)
            ch(act.activation(hrow[:, b, :], acc[b % 2][:], ACT.Copy))
            act.sem_inc(acc_free[b % 2], 1)
            act.sem_inc(S("h2_row"), 1)
        act.wait_ge(S("gaps"), 1)
        ch(act.activation(rGg[:], rGg[:], ACT.Exp))
        ch(act.activation(rS[:, 3, :], rS[:, 2, :], ACT.Exp))
        act.sem_inc(S("gap_exp"), 1)

    @block.vector
    def _(dve):
        ch = chain(dve, "dve")
        dve.wait_ge(S("rt_in"), 16 * 6)
        ch(dve.tensor_copy(rwh[:], rw[:]))
        ch(dve.tensor_tensor(rwl[:], rw[:], rwh[:].bitcast(F32), ALU.subtract))
        dve.sem_inc(S("rt_split"), 1)
        dve.wait_ge(S("logits"), 1)
        along = lambda t, n: t.unsqueeze(2).broadcast_to([P, NB, n])
        every = lambda t, n: t.unsqueeze(1).broadcast_to([P, NB, n])
        ch(dve.tensor_tensor(rL[:], Y[:, 0:NB * LOGITS].rearrange("p (b n) -> p b n", b=NB), every(rbias[:], LOGITS),
                             ALU.add))
        g, e = rL[:, :, 0:N_GRP], rL[:, :, N_GRP:]
        top, first, gap, p2, norm, gw = (rS[:, k, :] for k in range(6))

        def first_largest(x, n, onehot, largest):
            ch(dve.tensor_reduce(largest, x, AX.X, ALU.max))
            ch(dve.tensor_tensor(onehot, x, along(largest, n), ALU.is_equal))
            ch(dve.tensor_tensor(onehot, onehot, every(rI[:, N_EXP - n:], n), ALU.mult))
            ch(dve.tensor_reduce(first, onehot, AX.X, ALU.max))
            ch(dve.tensor_tensor(onehot, every(rI[:, N_EXP - n:], n), along(first, n), ALU.is_equal))

        grp = rGg[:]
        first_largest(g, N_GRP, grp, top)
        e4 = lambda t: t.rearrange("p b (g n) -> p b g n", g=N_GRP)
        wide = grp.unsqueeze(3).broadcast_to([P, NB, N_GRP, PER_GRP])
        ch(dve.tensor_tensor(e4(rG[:]), e4(e), wide, ALU.mult))
        ch(dve.tensor_scalar(e4(rT[:]), wide, 1.0, -NEG, ALU.subtract, ALU.mult))
        ch(dve.tensor_tensor(rG[:], rG[:], rT[:], ALU.add))
        ch(dve.tensor_tensor(grp, g, along(top, N_GRP), ALU.subtract))
        first_largest(rG[:], N_EXP, rO1[:], gap)
        ch(dve.scalar_tensor_tensor(rG[:], rO1[:], 2 * NEG, rG[:], ALU.mult, ALU.add))
        first_largest(rG[:], N_EXP, rO2[:], top)
        ch(dve.tensor_tensor(gap, top, gap, ALU.subtract))
        dve.sem_inc(S("gaps"), 1)
        ch(dve.tensor_tensor(rOb[:], rO1[:], rO2[:], ALU.add))
        dve.sem_inc(S("chosen"), 1)
        dve.wait_ge(S("gap_exp"), 1)
        ch(dve.tensor_reduce(gw, grp, AX.X, ALU.add))
        ch(dve.tensor_scalar(norm, p2, 1.0, None, ALU.add))
        ch(dve.tensor_tensor(norm, norm, gw, ALU.mult))
        ch(dve.reciprocal(WTOK[:, 0, :], norm))
        ch(dve.tensor_tensor(WTOK[:, 1, :], WTOK[:, 0, :], p2, ALU.mult))
        dve.wait_ge(S("ranks"), 1)
        number, taken_by, after, before = (rNt[:, k, :] for k in range(4))
        ch(dve.tensor_copy(number, Y[:, HALF + NB * N_EXP:HALF + (NB + 1) * N_EXP]))
        ch(dve.memset(taken_by, 0.0))
        for j in range(T // P):
            ch(dve.scalar_tensor_tensor(taken_by, number, float(j * P), taken_by, ALU.is_gt, ALU.add))
        ch(dve.tensor_tensor_scan(after, taken_by, taken_by, 0.0, ALU.add, ALU.bypass))
        ch(dve.tensor_tensor(before, after, taken_by, ALU.subtract))
        ch(dve.tensor_copy(NSL[:], after[:, N_EXP - 1:N_EXP]))
        ch(dve.tensor_scalar(before, before, float(P), None, ALU.mult))
        ch(dve.tensor_tensor(rK[:], Y[:, HALF:HALF + NB * N_EXP].rearrange("p (b n) -> p b n", b=NB),
                             every(before, N_EXP), ALU.add))
        for k, o in enumerate((rO1, rO2)):
            ch(dve.tensor_tensor(rT[:], o[:], rK[:], ALU.mult))
            ch(dve.tensor_reduce(top, rT[:], AX.X, ALU.add))
            ch(dve.tensor_copy(POS[:, k, :], top))
        dve.sem_inc(S("placed"), 1)
        for s in range(SLOTS + 1):
            ch(dve.tensor_scalar(number, after, float(s), None, ALU.is_le, ALU.add, accum_out=rSi[:, s:s + 1]))
        ch(dve.tensor_scalar(rSi[:], rSi[:], float(N_EXP - 1), None, ALU.min))
        ch(dve.tensor_copy(SLOTE[:], rSi[:]))
        dve.sem_inc(S("slots"), 1)
        dve.wait_ge(S("list_in"), 16)
        ch(dve.tensor_copy(rLf[:], rLi[:]))
        dve.sem_inc(S("list_f"), 1)
        dve.wait_ge(S("list_turned"), 1)
        ch(dve.tensor_copy(DST[:], X[0][:, 0:SLOTS + 1]))
        ch(dve.tensor_scalar(rSi[:], X[0][:, 0:SLOTS + 1], 0.5, -0.25, ALU.mult, ALU.add))
        ch(dve.tensor_scalar(rSi[:], rSi[:], ROUND, None, ALU.add))
        ch(dve.tensor_scalar(rSi[:], rSi[:], ROUND, None, ALU.subtract))
        ch(dve.tensor_scalar(rSi[:], rSi[:], float(T - 1), None, ALU.min))
        ch(dve.tensor_copy(IDX[:], rSi[:]))
        dve.sem_inc(S("idx_in"), 1)

    EW1 = A["exp_w1"].rearrange("l e (k p) n -> (l e k) p n", p=P)
    EW3 = A["exp_w3"].rearrange("l e (k p) n -> (l e k) p n", p=P)
    EW2 = A["exp_w2"].rearrange("l e (k p) n -> (l e k) p n", p=P)
    PIECES, UPS = 12, 8
    piece = lambda t, i: t[ds(i, 1)].rearrange("a p n -> p (a n)")

    def slot_count(e):
        e.wait_ge(S("slots"), 1)
        return e.value_load(NSL[0:1, 0:1], min_val=1, max_val=SLOTS)

    @block.sync
    def _(sp):
        def pieces(s, first):
            e = sp.value_load(SLOTE[0:1, ds(s, 1)], min_val=0, max_val=N_EXP - 1)
            for q in range(PIECES):
                if not first:
                    sp.wait_ge(S("m_lo"), s * PIECES - PIECES + q + 1)
                if q < UPS:
                    sp.dma_start(mraw[:, q, 0:FE], piece(EW1, e * UPS + q)).then_inc(S(f"m_land{q}"), 16)
                    sp.dma_start(mraw[:, q, FE:], piece(EW3, e * UPS + q)).then_inc(S(f"m_land{q}"), 16)
                else:
                    sp.dma_start(mraw[:, q, :], piece(EW2, e * 4 + q - UPS)).then_inc(S(f"m_land{q}"), 16)
        n = slot_count(sp)
        sp.wait_ge(S("h2_st"), 16 * NB)
        sp.wait_ge(S("idx_in"), 1)
        pieces(0, True)
        with sp.Fori(1, n) as s:
            pieces(s, False)

    @block.gpsimd
    def _(pool):
        n = slot_count(pool)
        def gather():
            pool.indirect_dma_start(Xs[:], None, h2rows, bass.IndirectOffsetOnAxis(ap=IDC[:], axis=0))\
                .then_inc(S("xs_in"), 16)
        pool.wait_ge(S("h2_st"), 16 * NB)
        pool.wait_ge(S("slot_rows"), 1)
        gather()
        with pool.Fori(0, n) as s:
            pool.wait_ge(S("x_turned"), s + 1)
            pool.wait_ge(S("slot_rows"), s + 2)
            pool.sem_inc(S("gathers"), 1)
            gather()
            pool.wait_ge(S("y_out"), s + 2)
            pool.wait_ge(S("slot_dst"), s + 1)
            pool.sem_inc(S("scatters"), 1)
            pool.indirect_dma_start(ys, bass.IndirectOffsetOnAxis(ap=IDD[:], axis=0), YO[:], None)\
                .then_inc(S("ys_st"), 16)
            pool.wait_ge(S("ys_st"), s * 16 + 16)
            pool.sem_inc(S("ys_free"), 1)

    @block.tensor
    def _(pe):
        n = slot_count(pe)
        def turn_rows():
            for m in range(KD):
                last = pe.transpose(X[m // 4][:, m % 4 * P:(m % 4 + 1) * P], Xs[:, m * P:(m + 1) * P], ident[:])
            last.then_inc(S("x_turned"), 1)
        pe.wait_ge(S("xs_in"), 16)
        turn_rows()
        with pe.Fori(0, n) as s:
            pe.wait_ge(S("x_lo"), s + 1)
            for k in range(UPS):
                pe.wait_ge(S("m_lo"), s * PIECES + k + 1)
                for h in range(2):
                    o, cols = acc[0][:, h * FE:(h + 1) * FE], slice(h * FE, (h + 1) * FE)
                    pe.matmul(o, XTh[:, k, :], mhi[:, k % NSP, cols], start=(k == 0), stop=False)
                    pe.matmul(o, XTh[:, k, :], mlo[:, k % NSP, cols], start=False, stop=False)
                    last = pe.matmul(o, XTl[:, k, :], mhi[:, k % NSP, cols], start=False, stop=(k == UPS - 1))
                last.then_inc(S("m_used"), 1)
            pe.wait_ge(S("xs_in"), s * 16 + 32)
            turn_rows()
            pe.wait_ge(S("hidden"), s + 1)
            for j in range(4):
                last = pe.transpose(Y[:, j * P:(j + 1) * P], Hm[:, j * P:(j + 1) * P], ident[:])
            last.then_inc(S("h_turned"), 1)
            pe.wait_ge(S("h_lo"), s + 1)
            pe.wait_ge(S("y_out"), s + 1)
            for j in range(4):
                q = UPS + j
                pe.wait_ge(S("m_lo"), s * PIECES + q + 1)
                for h in range(2):
                    o, cols = acc[1][:, h * HALF:(h + 1) * HALF], slice(h * HALF, (h + 1) * HALF)
                    pe.matmul(o, HTh[:, j, :], mhi[:, q % NSP, cols], start=(j == 0), stop=False)
                    pe.matmul(o, HTh[:, j, :], mlo[:, q % NSP, cols], start=False, stop=False)
                    last = pe.matmul(o, HTl[:, j, :], mhi[:, q % NSP, cols], start=False, stop=(j == 3))
                last.then_inc(S("m_used"), 1)

    def turned_rows(e, is_act):
        for h in range(2):
            src = X[h][:].rearrange("p (m n) -> p m n", m=4)
            if is_act:
                e(XTh[:, 4 * h:4 * h + 4, :], src)
            else:
                e(XTl[:, 4 * h:4 * h + 4, :], src, XTh[:, 4 * h:4 * h + 4, :].bitcast(F32))

    @block.scalar
    def _(act):
        ch = chain(act, "moe_act")
        n = slot_count(act)
        act.sem_inc(S("m_used"), NSP)
        act.sem_inc(S("y_out"), 1)
        act.sem_inc(S("ys_free"), 1)

        def rows_hi(s):
            act.wait_ge(S("x_turned"), s + 1)
            turned_rows(lambda o, i: ch(act.activation(o, i, ACT.Copy)), True)
            act.sem_inc(S("x_hi"), 1)

        def high(s, q):
            per = 32 if q < UPS else 16
            act.wait_ge(S(f"m_land{q}"), s * per + (per + 32 if q < UPS else per))
            act.wait_ge(S("m_used"), s * PIECES + q + 1)
            act.activation(mhi[:, q % NSP, :], mraw[:, q, :], ACT.Copy).then_inc(S("m_hi"), 1)

        act.wait_ge(S("x_turned"), 1)
        turned_rows(lambda o, i: ch(act.activation(o, i, ACT.Copy)), True)
        act.sem_inc(S("x_hi"), 1)
        with act.Fori(0, n) as s:
            ch.enter(s, 5)
            for q in range(UPS):
                high(s, q)
            act.wait_ge(S("m_used"), s * PIECES + UPS + NSP)
            ch(act.activation(SG[:], acc[0][:, 0:FE], ACT.Silu))
            act.sem_inc(S("silu"), 1)
            rows_hi(s + 1)
            for q in range(UPS, PIECES):
                high(s, q)
            act.wait_ge(S("h_turned"), s + 1)
            ch(act.activation(HTh[:], Y[:, 0:HALF].rearrange("p (m n) -> p m n", m=4), ACT.Copy))
            act.sem_inc(S("h_hi"), 1)
            act.wait_ge(S("m_used"), s * PIECES + PIECES + NSP)
            act.wait_ge(S("ys_free"), s + 1)
            ch(act.activation(YO[:], acc[1][:], ACT.Copy))
            act.sem_inc(S("y_out"), 1)
        act.wait_ge(S("ys_free"), n + 1)
        act.sem_inc(S("experts_done"), 1)

    @block.vector
    def _(dve):
        ch = chain(dve, "moe_dve")
        n = slot_count(dve)

        def rows_lo(s):
            dve.wait_ge(S("x_hi"), s + 1)
            turned_rows(lambda o, i, h: ch(dve.tensor_tensor(o, i, h, ALU.subtract)), False)
            dve.sem_inc(S("x_lo"), 1)

        def low(s, q):
            dve.wait_ge(S("m_hi"), s * PIECES + q + 1)
            dve.tensor_tensor(mlo[:, q % NSP, :], mraw[:, q, :], mhi[:, q % NSP, :].bitcast(F32), ALU.subtract)\
               .then_inc(S("m_lo"), 1)
        dve.tensor_copy(IDC[:], IDX[:, 0:1]).then_inc(S("slot_rows"), 1)
        rows_lo(0)
        with dve.Fori(0, n) as s:
            ch.enter(s, 4)
            dve.wait_ge(S("xs_in"), s * 16 + 16)
            dve.tensor_copy(IDC[:], IDX[:, ds(s + 1, 1)]).then_inc(S("slot_rows"), 1)
            for q in range(UPS):
                low(s, q)
            dve.wait_ge(S("silu"), s + 1)
            ch(dve.tensor_tensor(Hm[:], SG[:], acc[0][:, FE:], ALU.mult))
            dve.sem_inc(S("hidden"), 1)
            rows_lo(s + 1)
            for q in range(UPS, PIECES):
                low(s, q)
            dve.wait_ge(S("h_hi"), s + 1)
            ch(dve.tensor_tensor(HTl[:], Y[:, 0:HALF].rearrange("p (m n) -> p m n", m=4), HTh[:].bitcast(F32),
                                 ALU.subtract))
            dve.sem_inc(S("h_lo"), 1)
            dve.wait_ge(S("ys_free"), s + 1)
            dve.tensor_copy(IDD[:], DST[:, ds(s, 1)]).then_inc(S("slot_dst"), 1)

    @block.sync
    def _(sp):
        sp.wait_ge(S("experts_done"), 1)
        for b in range(NB):
            sp.dma_start(G12[:, b, :, :], ys[2 * b * P:2 * (b + 1) * P, :].rearrange("(p k) n -> p k n", k=2))\
              .then_inc(S(f"y_in{b % 2}"), 16)
            if b == 1:
                sp.dma_start(C[:], tiles(x1T)).then_inc(S("x1T_in"), 16)
        for m in range(KD):
            sp.wait_ge(S("x2_done"), m + 1)
            sp.dma_start(x2T[m * P:(m + 1) * P, :], C[:, m, :]).then_inc(S("x2T_st"), 16)

    @block.tensor
    def _(pe):
        pe.wait_ge(S("y_sum"), NB)
        for m in range(KD):
            pe.wait_ge(acc_free[m % 2], take(m % 2))
            for b in range(NB):
                last = pe.transpose(acc[m % 2][:, b * P:(b + 1) * P], G12[:, b, 0, m * P:(m + 1) * P], ident[:])
            last.then_inc(S("y_turned"), 1)

    @block.vector
    def _(dve):
        ch = chain(dve, "dve")
        for b in range(NB):
            dve.wait_ge(S(f"y_in{b % 2}"), 16 * NB // 2)
            ch(dve.tensor_scalar(G12[:, b, 0, :], G12[:, b, 0, :], WTOK[:, 0, b:b + 1], None, ALU.mult))
            ch(dve.scalar_tensor_tensor(G12[:, b, 0, :], G12[:, b, 1, :], WTOK[:, 1, b:b + 1], G12[:, b, 0, :],
                                        ALU.mult, ALU.add))
            dve.sem_inc(S("y_sum"), 1)
        dve.wait_ge(S("x1T_in"), 16)
        for m in range(KD):
            dve.wait_ge(S("y_turned"), m + 1)
            ch(dve.scalar_tensor_tensor(C[:, m, :], acc[m % 2][:], MOD[:, 40 + m:41 + m], C[:, m, :],
                                        ALU.mult, ALU.add))
            dve.sem_inc(acc_free[m % 2], 1)
            dve.sem_inc(S("x2_done"), 1)

    @block.sync
    def _(sp):
        sp.wait_ge(S("x2T_st"), 16 * KD)

    stage.close()
    lasting = [n for n in sems if n.startswith(("w_", "acc_free")) or n in ("act_step", "dve_step", "pool_step")]
    nc.clear_and_free_semaphores([sems[n] for n in sems if n not in lasting])
    nc.all_engine_barrier()
    sems, suffix = {n: sems[n] for n in lasting}, "_b2"
    stage = ExitStack()
    block = stage.enter_context(nc.Block())

    mean_square("n3", C, TT, lambda act, m: None)
    normed("n3", C, TT[:, 2, :], lambda m: vec("g_mix_pre_2", m), None, Ah, Al, lambda dve: None)

    @block.sync
    def _(sp):
        sp.dma_start(pfix[:].rearrange("p g n -> p (g n)"), A["pool_fix"].broadcast_to([P, 64])).then_inc(S("fix_in"), 16)
        for name, n, c0 in (("rx", 8, 512), ("rg", 8, 1536), ("g2", 16, 2560), ("pool", 4, 0)):
            load_run(sp, N0[name], n, lambda j, c0=c0: W2[:, :, ds(j * P + c0, P)])
            if name == "rx":
                sp.wait_ge(S("bd_zero"), 1)
                for g in range(2):
                    for h in range(2):
                        sp.dma_start(bdr[h * HD:(h + 1) * HD, g * 8:g * 8 + 8, h * HD:(h + 1) * HD],
                                     A["w_rg_gates_2"][0, g].rearrange("(j h) i o -> h i j o", h=2)[h])\
                          .then_inc(S("bd_in"), 16)

    @block.gpsimd
    def _(pool):
        ch = chain(pool, "pool")
        ch(pool.memset(bdr[:], 0.0))
        pool.sem_inc(S("bd_zero"), 1)
        for name, n in (("rx", 8), ("rg", 8), ("g2", 16), ("pool", 4)):
            split_run(pool, N0[name], n)

    @block.tensor
    def _(pe):
        pe.wait_ge(S("n3_lo"), KD)
        product_run(pe, N0["rx"], 36, Ah, Al)

    @block.scalar
    def _(act):
        ch = chain(act, "act")
        with act.Fori(0, 4) as i:
            ch.enter(i, 2)
            for r in range(2):
                j = 2 * i + r
                act.wait_ge(w_used, N0["rg"] + j + 1)
                ch(act.activation(row(RG, j), acc[r][:], ACT.Gelu_apprx_tanh))
                act.sem_inc(acc_free[r], 1)
            ch.leave(4)
        for r in range(2):
            act.sem_inc(S(f"gates2_st{r}"), 16)
        with act.Fori(0, 8) as i:
            ch.enter(i, 2)
            for r in range(2):
                j = 2 * i + r
                act.wait_ge(w_used, N0["g2"] + j + 1)
                act.wait_ge(S(f"gates2_st{r}"), i * 16 + 16)
                ch(act.activation(TT[:, 2 + r, :], acc[r][:], ACT.Sigmoid))
                act.sem_inc(acc_free[r], 1)
                act.dma_start(gates2[ds(j * P, P), :], TT[:, 2 + r, :]).then_inc(S(f"gates2_st{r}"), 16)
            ch.leave(8)
        for g in range(4):
            act.wait_ge(w_used, N0["pool"] + g + 1)
            ch(act.activation(UP[:, g, :], acc[g % 2][:], ACT.Copy))
            act.sem_inc(acc_free[g % 2], 1)
            act.sem_inc(S("u_out"), 1)
        act.wait_ge(S("lru_abs"), 1)
        ch(act.activation(sp8[:, 1, :], sp8[:, 0, :], ACT.Exp, scale=-1.0))
        ch(act.activation(sp8[:, 2, :], sp8[:, 1, :], ACT.Ln, bias=1.0))
        act.sem_inc(S("lru_ln"), 1)

    @block.vector
    def _(dve):
        ch = chain(dve, "dve")
        with dve.Fori(0, 4) as i:
            ch.enter(i, 8)
            for r in range(2):
                j = 2 * i + r
                dve.wait_ge(w_used, N0["rx"] + j + 1)
                x = row(C, j)
                ch(dve.tensor_scalar(x, acc[r][:], vecd("conv_w_2", j + 24), vecd("conv_b_2", j), ALU.mult, ALU.add))
                for back in range(1, 4):
                    ch(dve.scalar_tensor_tensor(x[:, back:], acc[r][:, 0:T - back], vecd("conv_w_2", j + 8 * (3 - back)),
                                                x[:, back:], ALU.mult, ALU.add))
                dve.sem_inc(acc_free[r], 1)
            ch.leave(4)
        lam = vec("lru_lambda_2", 0, 8)
        z, e, l = (sp8[:, k, :] for k in range(3))
        ch(dve.scalar_tensor_tensor(z, lam, -1.0, lam, ALU.mult, ALU.max))
        dve.sem_inc(S("lru_abs"), 1)
        dve.wait_ge(S("lru_ln"), 1)
        ch(dve.tensor_scalar(z, e, 1.0, 1.0, ALU.add, ALU.subtract))
        ch(dve.tensor_scalar(z, z, 1e-30, None, ALU.max))
        ch(dve.reciprocal(z, z))
        ch(dve.tensor_tensor(z, z, e, ALU.mult))
        ch(dve.tensor_scalar(z, z, 2.0, None, ALU.min))
        ch(dve.tensor_tensor(l, l, z, ALU.mult))
        ch(dve.tensor_scalar(z, lam, -1.0, 0.0, ALU.mult, ALU.max))
        ch(dve.tensor_tensor(l, l, z, ALU.add))
        ch(dve.tensor_scalar(sp8[:, 0, :], l, LRU_C, None, ALU.mult))
        dve.wait_ge(S("fix_in"), 16)
        for g, w in enumerate(POOL_WINDOWS):
            dve.wait_ge(S("u_out"), g + 1)
            s, d, k = UP[:, g, :], 1, 0
            while d < w:
                ch(dve.tensor_copy(TT[:, k, 0:d], s[:, 0:d]))
                ch(dve.tensor_tensor(TT[:, k, d:], s[:, d:], s[:, 0:T - d], ALU.add))
                s, d, k = TT[:, k, :], 2 * d, 1 - k
            ch(dve.tensor_scalar(s, s, 1.0 / w, None, ALU.mult))
            ch(dve.tensor_tensor(s[:, 0:16], s[:, 0:16], pfix[:, g, :], ALU.mult))
            ch(dve.tensor_tensor(UP[:, g, :], s, UP[:, g, :], ALU.subtract))
        dve.wait_ge(S("bd_in"), 64)
        ch(dve.tensor_copy(bdh[:], bdr[:]))
        ch(dve.tensor_tensor(bdl[:], bdr[:], bdh[:].bitcast(F32), ALU.subtract))
        dve.sem_inc(S("bd_split"), 1)

    @block.tensor
    def _(pe):
        pe.wait_ge(S("bd_split"), 1)
        for j in range(KD):
            pe.wait_ge(S("xc_lo"), j + 1)
            for g in range(2):
                pe.wait_ge(acc_free[g], take(g))
                for h in range(2):
                    o, cols = acc[g][:, h * HALF:(h + 1) * HALF], slice(h * HALF, (h + 1) * HALF)
                    pe.matmul(o, bdh[:, g * 8 + j, :], Ah[:, j, cols], start=True, stop=False)
                    pe.matmul(o, bdh[:, g * 8 + j, :], Al[:, j, cols], start=False, stop=False)
                    last = pe.matmul(o, bdl[:, g * 8 + j, :], Ah[:, j, cols], start=False, stop=True)
                last.then_inc(S("rg_ps"), 1)

    @block.scalar
    def _(act):
        ch = chain(act, "act")
        act.wait_ge(w_used, N0["pool"] + 4)
        for j in range(KD):
            ch(act.activation(Ah[:, j, :], C[:, j, :], ACT.Copy))
            act.sem_inc(S("xc_hi"), 1)
        for j in range(KD):
            act.wait_ge(S("rg_ps"), 2 * j + 2)
            ch(act.activation(AF[:, j, :], acc[0][:], ACT.Sigmoid, bias=vec("b_rg_gates_2", j)))
            act.sem_inc(acc_free[0], 1)
            if j >= 2:
                act.wait_ge(S("ixc"), j - 1)
            else:
                act.wait_ge(S(f"gates2_st{j}"), 16 * 9)
            ch(act.activation(TT[:, 2 + j % 2, :], acc[1][:], ACT.Sigmoid, bias=vec("b_rg_gates_2", 8 + j)))
            act.sem_inc(acc_free[1], 1)
            act.sem_inc(S("ri"), 1)
        for j in range(KD):
            act.wait_ge(S("z"), j + 1)
            ch(act.activation(AG[:, j, :], AF[:, j, :], ACT.Exp, scale=-1.0))
        for j in range(KD):
            ch(act.activation(AF[:, j, :], AF[:, j, :], ACT.Tanh))
        for j in range(KD):
            if j >= 2:
                act.wait_ge(S("log_diff"), j - 1)
            ch(act.activation(TT[:, 2 + j % 2, :], AF[:, j, :], ACT.Ln, bias=1.0))
            ch(act.activation(AF[:, j, :], AF[:, j, :], ACT.Ln, scale=2.0))
            act.sem_inc(S("logs"), 1)
        for j in range(KD):
            act.wait_ge(S("log_diff"), j + 1)
            ch(act.activation(AF[:, j, :], AF[:, j, :], ACT.Exp, scale=0.5))
            act.sem_inc(S("mult"), 1)
        for j in range(KD):
            act.wait_ge(S("lru"), j + 1)
            act.activation(Bh[:, j, :], C[:, j, :], ACT.Copy).then_inc(S("lru_hi"), 1)
        for g in range(4):
            if g == 0:
                act.wait_ge(S("lru"), KD)
            act.activation(Ah[:, g, :], UP[:, g, :], ACT.Copy).then_inc(S("d_hi"), 1)

    @block.vector
    def _(dve):
        ch = chain(dve, "dve")
        for j in range(KD):
            dve.wait_ge(S("xc_hi"), j + 1)
            ch(dve.tensor_tensor(Al[:, j, :], C[:, j, :], Ah[:, j, :].bitcast(F32), ALU.subtract))
            dve.sem_inc(S("xc_lo"), 1)
        for j in range(KD):
            dve.wait_ge(S("ri"), j + 1)
            ch(dve.tensor_tensor(C[:, j, :], C[:, j, :], TT[:, 2 + j % 2, :], ALU.mult))
            dve.sem_inc(S("ixc"), 1)
            ch(dve.tensor_scalar(AF[:, j, :], AF[:, j, :], sp8[:, 0, j:j + 1], None, ALU.mult))
            dve.sem_inc(S("z"), 1)
        for j in range(KD):
            dve.wait_ge(S("logs"), j + 1)
            ch(dve.tensor_tensor(AF[:, j, :], AF[:, j, :], TT[:, 2 + j % 2, :], ALU.subtract))
            dve.sem_inc(S("log_diff"), 1)
        for j in range(KD):
            dve.wait_ge(S("mult"), j + 1)
            ch(dve.memset(AF[:, j, 0:1], 1.0))
            ch(dve.tensor_tensor(AF[:, j, :], AF[:, j, :], C[:, j, :], ALU.mult))
            ch(dve.tensor_tensor_scan(C[:, j, :], AG[:, j, :], AF[:, j, :], 0.0, ALU.mult, ALU.add))
            ch(dve.tensor_tensor(C[:, j, :], C[:, j, :], RG[:, j, :], ALU.mult))
            dve.sem_inc(S("lru"), 1)
        for j in range(KD):
            dve.wait_ge(S("lru_hi"), j + 1)
            ch(dve.tensor_tensor(Cl[:, j, :], C[:, j, :], Bh[:, j, :].bitcast(F32), ALU.subtract))
            dve.sem_inc(S("lru_lo"), 1)
        for g in range(4):
            dve.wait_ge(S("d_hi"), g + 1)
            ch(dve.tensor_tensor(Al[:, g, :], UP[:, g, :], Ah[:, g, :].bitcast(F32), ALU.subtract))
            dve.sem_inc(S("d_lo"), 1)
        for g in range(4):
            dve.wait_ge(w_used, N0["poolw"] + g + 1)
            ch(dve.tensor_scalar(TT[:, g % 2, :], acc[g % 2][:], vec("pool_scale_2", g), None, ALU.mult))
            dve.sem_inc(acc_free[g % 2], 1)
            ch(dve.tensor_copy(Bl[:, g, :], TT[:, g % 2, :]))
            ch(dve.tensor_tensor(Bl2[:, g, :], TT[:, g % 2, :], Bl[:, g, :].bitcast(F32), ALU.subtract))
            dve.sem_inc(S("py_lo"), 1)

    @block.sync
    def _(sp):
        for g in range(4):
            load(sp, N0["poolw"] + g, g % 2, A["pool_w_2"][0, g].rearrange("p (a n) -> p a n", a=1), k=1)

        def weights(m):
            load(sp, 2 * m + N0["mix"], 0, WPO[:, :, ds(m * P, P)], k=4)
            load(sp, 2 * m + N0["mix"] + 1, 1, WRO[:, :, ds(m * P, P)])

        def gate_pair(m, r):
            for g in range(2):
                sp.dma_start(TT[:, 2 * r + g, :], gates2[ds(m * P + g * D, P), :]).then_inc(S(f"gate_in{r}"), 16)
        for m in range(2):
            weights(m)
        sp.wait_ge(S("py_lo"), 4)
        for m in range(2):
            gate_pair(m, m)
        with sp.Fori(1, 4) as i:
            for r in range(2):
                weights(2 * i + r)
                sp.wait_ge(S("merged"), 2 * i + r - 1)
                gate_pair(2 * i + r, r)
        load_run(sp, N0["wo"], 8, lambda m: WO[:, :, ds(m * P, P)])
        sp.wait_ge(w_used, N0["mix"] + 16)
        sp.dma_start(RG[:], tiles(x2T)).then_inc(S("x2T_in"), 16)

    @block.gpsimd
    def _(pool):
        for g in range(4):
            split(pool, N0["poolw"] + g, g % 2, landed[N0["poolw"] + g], k=1)
        ch = chain(pool, "pool")
        with pool.Fori(0, 8) as i:
            ch.enter(i, 2)
            for r in range(2):
                split(pool, N0["mix"] + 2 * i + r, r, i * 16 + landed[N0["mix"] + r], (4, 8)[r])
            ch.leave(8)
        split_run(pool, N0["wo"], 8)

    @block.tensor
    def _(pe):
        for g in range(4):
            pe.wait_ge(S("d_lo"), g + 1)
            product(pe, N0["poolw"] + g, g % 2, Ah, Al, 1, g, free=take(g % 2))
        pe.wait_ge(S("py_lo"), 4)
        pe.wait_ge(S("lru_lo"), KD)
        with pe.Fori(0, 8) as m:
            product(pe, 2 * m + N0["mix"], 0, Bl, Bl2, 4, free=m + taken[0])
            product(pe, 2 * m + N0["mix"] + 1, 1, Bh, Cl, free=m + taken[1])
        taken[0] += 8
        taken[1] += 8
        pe.wait_ge(S("merged"), 8)
        product_run(pe, N0["wo"], 8, Ah, Al)

    @block.vector
    def _(dve):
        ch = chain(dve, "dve")
        with dve.Fori(0, 4) as i:
            ch.enter(i, 8)
            for r in range(2):
                m = 2 * i + r
                dve.wait_ge(S(f"gate_in{r}"), i * 32 + 32)
                for g in range(2):
                    dve.wait_ge(w_used, 2 * m + N0["mix"] + g + 1)
                    ch(dve.tensor_tensor(TT[:, 2 * r + g, :], TT[:, 2 * r + g, :], acc[g][:], ALU.mult))
                    dve.sem_inc(acc_free[g], 1)
                ch(dve.tensor_tensor(TT[:, 2 * r, :], TT[:, 2 * r, :], TT[:, 2 * r + 1, :], ALU.add))
                dve.sem_inc(S("merge_sum"), 1)
                dve.wait_ge(S("merge_hi"), m + 1)
                ch(dve.tensor_tensor(row(Al, m), TT[:, 2 * r, :], row(Ah, m).bitcast(F32), ALU.subtract))
                dve.sem_inc(S("merged"), 1)
            ch.leave(4)

    @block.scalar
    def _(act):
        ch = chain(act, "act")
        with act.Fori(0, 4) as i:
            for r in range(2):
                m = 2 * i + r
                act.wait_ge(S("merge_sum"), m + 1)
                act.activation(row(Ah, m), TT[:, 2 * r, :], ACT.Copy).then_inc(S("merge_hi"), 1)

    def after_product(tag, n0, gain, residual_in, stored, result):
        def copied(act, m):
            act.wait_ge(w_used, n0 + m + 1)
            ch = chain(act, "act")
            ch(act.activation(C[:, m, :], acc[m % 2][:], ACT.Copy))
            act.sem_inc(acc_free[m % 2], 1)
        mean_square(tag, C, TT, copied)
        finish(tag, gain, residual_in, stored, result)

    def finish(tag, gain, residual_in, stored, result):
        @block.vector
        def _(dve):
            ch = chain(dve, "dve")
            dve.wait_ge(S(residual_in), 16)
            for m in range(KD):
                ch(dve.scalar_tensor_tensor(C[:, m, :], C[:, m, :], vec(gain, m), TT[:, 2, :], ALU.mult, ALU.mult))
                ch(dve.tensor_tensor(C[:, m, :], C[:, m, :], RG[:, m, :], ALU.add))
                dve.sem_inc(S(tag + "_added"), 1)

        @block.sync
        def _(sp):
            for m in range(KD):
                sp.wait_ge(S(tag + "_added"), m + 1)
                sp.dma_start(result[m * P:(m + 1) * P, :], C[:, m, :]).then_inc(S(stored), 16)

    after_product("n4", N0["wo"], "g_mix_post_2", "x2T_in", "x3T_st", x3T)
    mean_square("n5", C, TT, lambda act, m: act.wait_ge(S("n4_added"), (m + 1) if m else KD))
    normed("n5", C, TT[:, 2, :], lambda m: vec("g_ffn_pre_2", m), None, Ah, Al,
           lambda dve: dve.wait_ge(S("x3T_st"), 16 * KD))

    CH = D_FF // D
    for c in range(CH):
        n0 = N0[f"ffn{c}"]

        @block.sync
        def _(sp):
            with sp.Fori(0, 8) as j:
                for r in range(2):
                    load(sp, n0 + 2 * j + r, r, WUP[:, :, ds(j * P + (c * D + r * D_FF), P)])
            load_run(sp, n0 + 16, 8, lambda m: WDN[:, c * KD:(c + 1) * KD, ds(m * P, P)])

        @block.gpsimd
        def _(pool):
            split_run(pool, n0, 24)

        @block.tensor
        def _(pe):
            if c == 0:
                pe.wait_ge(S("n5_lo"), KD)
            product_run(pe, n0, 16, Ah, Al)
            pe.wait_ge(S("hid_lo"), 8 * c + 8)
            product_run(pe, n0 + 16, 8, Bh, Bl)

        @block.vector
        def _(dve):
            ch = chain(dve, "dve")
            if c == 0:
                dve.wait_ge(S("n5_lo"), KD)
            with dve.Fori(0, 4) as i:
                ch.enter(i, 10)
                for r in range(2):
                    j = 2 * i + r
                    g = TT[:, 2 * r, :]
                    dve.wait_ge(w_used, 2 * j + n0 + 1)
                    ch(dve.tensor_scalar(g, acc[0][:], vecd("ffn_conv_w_2", j + 8 * c + 48), vecd("ffn_conv_b_2", j + 8 * c),
                                         ALU.mult, ALU.add))
                    for back in range(1, 3):
                        ch(dve.scalar_tensor_tensor(g[:, back:], acc[0][:, 0:T - back],
                                                    vecd("ffn_conv_w_2", j + 8 * c + 24 * (2 - back)), g[:, back:],
                                                    ALU.mult, ALU.add))
                    dve.sem_inc(acc_free[0], 1)
                    dve.sem_inc(S("conv"), 1)
                    dve.wait_ge(w_used, 2 * j + n0 + 2)
                    dve.wait_ge(S("gelu"), j + 8 * c + 1)
                    ch(dve.tensor_tensor(g, g, acc[1][:], ALU.mult))
                    dve.sem_inc(acc_free[1], 1)
                    dve.sem_inc(S("hid"), 1)
                    dve.wait_ge(S("hid_hi"), j + 8 * c + 1)
                    ch(dve.tensor_tensor(row(Bl, j), g, row(Bh, j).bitcast(F32), ALU.subtract))
                    dve.sem_inc(S("hid_lo"), 1)
                ch.leave(4)
            if c < CH - 1:
                with dve.Fori(0, 4) as i:
                    ch.enter(i, 2)
                    for r in range(2):
                        m = 2 * i + r
                        dve.wait_ge(w_used, m + n0 + 17)
                        if c == 0:
                            ch(dve.tensor_copy(row(C, m), acc[r][:]))
                        else:
                            ch(dve.tensor_tensor(row(C, m), acc[r][:], row(C, m), ALU.add))
                        dve.sem_inc(acc_free[r], 1)
                    ch.leave(4)
            else:
                for m in range(KD):
                    dve.wait_ge(w_used, m + n0 + 17)
                    ch(dve.tensor_tensor(C[:, m, :], acc[m % 2][:], C[:, m, :], ALU.add))
                    dve.sem_inc(acc_free[m % 2], 1)
                    dve.sem_inc(S("down"), 1)
                    if m:
                        dve.wait_ge(S("n6_sq"), m)
                        if m == 1:
                            ch(dve.tensor_copy(TT[:, 2, :], TT[:, 0, :]))
                        else:
                            ch(dve.tensor_tensor(TT[:, 2, :], TT[:, 2, :], TT[:, (m - 1) % 2, :], ALU.add))
                        dve.sem_inc(S("n6_sum"), 1)

        @block.scalar
        def _(act):
            ch = chain(act, "act")
            with act.Fori(0, 4) as i:
                ch.enter(i, 2)
                for r in range(2):
                    j = 2 * i + r
                    act.wait_ge(S("conv"), j + 8 * c + 1)
                    ch(act.activation(TT[:, 2 * r, :], TT[:, 2 * r, :], ACT.Gelu_apprx_tanh))
                    act.sem_inc(S("gelu"), 1)
                    act.wait_ge(S("hid"), j + 8 * c + 1)
                    act.activation(row(Bh, j), TT[:, 2 * r, :], ACT.Copy).then_inc(S("hid_hi"), 1)
                ch.leave(4)

    mean_square("n6", C, TT, lambda act, m: act.wait_ge(S("down"), m + 1), summed=KD - 1)

    @block.sync
    def _(sp):
        sp.wait_ge(w_used, N0["ffn2"] + 24)
        sp.dma_start(RG[:], tiles(x3T)).then_inc(S("x3T_in"), 16)
        sp.dma_start(PR[:], A["p_2"][0, 0].rearrange("(b p) n -> p b n", p=P)).then_inc(S("p_in"), 16)
    finish("n6", "g_ffn_post_2", "x3T_in", "x4T_st", x4T)

    @block.tensor
    def _(pe):
        pe.wait_ge(S("p_in"), 16)
        for k in range(2):
            pe.wait_ge(acc_free[k], take(k))
            for b in range(NB):
                last = pe.transpose(acc[k][:, b * P:(b + 1) * P], PR[:, b, k * P:(k + 1) * P], ident[:])
            last.then_inc(S("p_turned"), 1)

    mean_square("n7", C, TT, lambda act, m: act.wait_ge(S("n6_added"), (m + 1) if m else KD))

    @block.scalar
    def _(act):
        for k in range(2):
            act.wait_ge(S("p_turned"), k + 1)
            act.activation(pTh[:, k, :], acc[k][:], ACT.Copy).then_inc(S("p_hi"), 1)

    @block.vector
    def _(dve):
        ch = chain(dve, "dve")
        for k in range(2):
            dve.wait_ge(S("p_hi"), k + 1)
            ch(dve.tensor_tensor(pTl[:, k, :], acc[k][:], pTh[:, k, :].bitcast(F32), ALU.subtract))
            dve.sem_inc(acc_free[k], 1)
            dve.sem_inc(S("p_lo"), 1)
    normed("n7", C, TT[:, 2, :], lambda m: vec("g_ple_gate_2", m), None, Ah, Al,
           lambda dve: dve.wait_ge(S("x4T_st"), 16 * KD))

    @block.sync
    def _(sp):
        load_run(sp, N0["plep"], 8, lambda m: WPP[:, :, ds(m * P, P)], k=2)
        load_run(sp, N0["pleg"], 8, lambda m: WPG[:, :, ds(m * P, P)])
        sp.wait_ge(S("n6_added"), KD)
        sp.wait_ge(S("x4T_st"), 16 * KD)
        sp.dma_start(RG[:], tiles(x4T)).then_inc(S("x4T_in"), 16)

    @block.gpsimd
    def _(pool):
        split_run(pool, N0["plep"], 8, k=2)
        split_run(pool, N0["pleg"], 8)

    @block.tensor
    def _(pe):
        pe.wait_ge(S("p_lo"), 2)
        product_run(pe, N0["plep"], 8, pTh, pTl, 2)

    def plep_out(act, m):
        if m == 0:
            act.wait_ge(S("n7_lo"), KD)
        act.wait_ge(w_used, N0["plep"] + m + 1)
        ch = chain(act, "act")
        ch(act.activation(C[:, m, :], acc[m % 2][:], ACT.Copy))
        act.sem_inc(acc_free[m % 2], 1)
    mean_square("n8", C, TT, plep_out)

    @block.tensor
    def _(pe):
        pe.wait_ge(S("n7_lo"), KD)
        product_run(pe, N0["pleg"], 8, Ah, Al)

    @block.scalar
    def _(act):
        for m in range(KD):
            act.wait_ge(w_used, N0["pleg"] + m + 1)
            ch = chain(act, "act")
            ch(act.activation(BG[:, m, :], acc[m % 2][:], ACT.Sigmoid))
            act.sem_inc(acc_free[m % 2], 1)
            act.sem_inc(S("ple_gate"), 1)
        for b in range(NB):
            act.wait_ge(S("out_turned"), b + 1)
            ch(act.activation(AF[:, b, :], acc[b % 2][:], ACT.Copy))
            act.sem_inc(acc_free[b % 2], 1)
            act.sem_inc(S("out_row"), 1)

    @block.vector
    def _(dve):
        ch = chain(dve, "dve")
        for m in range(KD):
            ch(dve.scalar_tensor_tensor(C[:, m, :], C[:, m, :], vec("g_ple_post_2", m), TT[:, 2, :], ALU.mult, ALU.mult))
        dve.wait_ge(S("x4T_in"), 16)
        for m in range(KD):
            dve.wait_ge(S("ple_gate"), m + 1)
            ch(dve.tensor_tensor(C[:, m, :], C[:, m, :], BG[:, m, :], ALU.mult))
            ch(dve.tensor_tensor(C[:, m, :], C[:, m, :], RG[:, m, :], ALU.add))
        dve.sem_inc(S("result"), 1)

    @block.tensor
    def _(pe):
        pe.wait_ge(S("result"), 1)
        for b in range(NB):
            pe.wait_ge(acc_free[b % 2], take(b % 2))
            for m in range(KD):
                last = pe.transpose(acc[b % 2][:, m * P:(m + 1) * P], C[:, m, b * P:(b + 1) * P], ident[:])
            last.then_inc(S("out_turned"), 1)

    @block.sync
    def _(sp):
        for b in range(NB):
            sp.wait_ge(S("out_row"), b + 1)
            sp.dma_start(out[0, b * P:(b + 1) * P, :], AF[:, b, :]).then_inc(S("out_st"), 16)
        sp.wait_ge(S("out_st"), 16 * NB)

    stage.close()


_INS = ['x', 'c', 'positions', 'ada_w', 'ada_b', 'norm1_g', 'norm2_g', 'w_in', 'b_fgt', 'b_gate', 'qn_fox',
        'kn_fox', 'qn_dsa', 'kn_dsa', 'w_proj_fox', 'w_proj_dsa', 'w_out', 'router_w_grp', 'router_b_grp',
        'router_w_exp', 'router_b_exp', 'exp_w1', 'exp_w3', 'exp_w2', 'p_2', 'g_mix_pre_2', 'g_mix_post_2',
        'w_in_2', 'pool_w_2', 'pool_scale_2', 'w_pool_out_2', 'conv_w_2', 'conv_b_2', 'w_rg_gates_2',
        'b_rg_gates_2', 'lru_lambda_2', 'w_rg_out_2', 'w_o_2', 'g_ffn_pre_2', 'g_ffn_post_2', 'w_up_2',
        'ffn_conv_w_2', 'ffn_conv_b_2', 'w_down_2', 'g_ple_gate_2', 'w_ple_gate_2', 'w_ple_proj_2',
        'g_ple_post_2']


def rotation_constants():
    j = np.arange(P) % HD
    return np.stack([10000.0 ** (-(j % 32) / 32.0), np.where(j < 32, -1.0, 1.0)]).astype(np.float32)


def routing_constants():
    rows = np.arange(2 * T, dtype=np.int32).reshape(NB, P, 2).transpose(1, 2, 0).copy()
    return np.arange(N_EXP, 0, -1, dtype=np.float32)[None], rows, np.arange(2 * T, 2 * T + P, dtype=np.int32)[None]


def pooling_constants():
    return np.stack([w / np.minimum(np.arange(16) + 1.0, w) for w in POOL_WINDOWS]).astype(np.float32).reshape(1, 64)


def kernel(**inputs):
    import concourse.bacc as _bacc
    from concourse.bass_utils import run_bass_kernel_spmd as _run

    nc = _bacc.Bacc("TRN2", target_bir_lowering=False, num_devices=1)
    arrays, args = {}, {}
    given = {name: np.ascontiguousarray(inputs[name]) for name in _INS}
    given["freq"] = rotation_constants()
    given["from_end"], given["result_row"], given["no_row"] = routing_constants()
    given["pool_fix"] = pooling_constants()
    for name, a in given.items():
        arrays[f"in_{name}"] = a
        args[name] = nc.dram_tensor(f"in_{name}", a.shape, mybir.dt.from_np(a.dtype), kind="ExternalInput").ap()
    out = nc.dram_tensor("out_dram", (1, T, D), F32, kind="ExternalOutput").ap()
    program(nc, args, out)
    r = _run(nc, [arrays], core_ids=[0])
    return r.results[0]["out_dram"]
```

```python
from contextlib import ExitStack

import numpy as np

import concourse.bass as bass
from concourse import mybir

F32 = mybir.dt.float32
F32R = mybir.dt.float32r
BF16 = mybir.dt.bfloat16
I32 = mybir.dt.int32
ACT = mybir.ActivationFunctionType
ALU = mybir.AluOpType
AX = mybir.AxisListType
ds = bass.ds

P = 128
D = 1024
T = 1024
KD = D // P
NB = T // P
HALF = 512
HD = 64
NH = 8
TOPK = 256
EPS = 1e-6
SCALE = HD ** -0.5
NEG = -1e30
N_GRP, N_EXP, PER_GRP = 4, 32, 8
FE = 512
D_FF = 3072
POOL_WINDOWS = (2, 4, 8, 16)
LRU_C = 8.0
SLOTS = (2 * T + N_EXP * (P - 1)) // P
FAR = 3e38
ROUND = 1.5 * 2.0 ** 23
PI_IN = 3.1415925
TWO_PI = 2 * np.pi


def split_two_pi():
    a = 6.28125
    rest = TWO_PI - a
    b = float(np.round(rest * 2.0 ** 21) / 2.0 ** 21)
    return a, b, float(np.float32(rest - b))


class Chain:

    def __init__(self, engine, semaphore):
        self.e, self.s, self.n, self.off = engine, semaphore, 0, 0

    def __call__(self, ins):
        ins.then_inc(self.s, 1)
        self.n += 1
        self.e.wait_ge(self.s, self.off + self.n)

    def count(self, ins):
        ins.then_inc(self.s, 1)
        self.n += 1

    def enter(self, i, per):
        self.off, self.start, self.per = i * per, self.n, per

    def leave(self, count):
        assert self.n - self.start == self.per, (self.n - self.start, self.per)
        self.n, self.off = self.start + self.per * count, 0


VECTORS = [
    [("ada_b", 48), ("norm1_g", 8), ("norm2_g", 8), ("b_gate", 16), ("c", 8), ("g_mix_pre_2", 8),
     ("g_mix_post_2", 8), ("g_ffn_pre_2", 8), ("g_ffn_post_2", 8), ("qn_fox", 1), ("kn_fox", 1),
     ("qn_dsa", 1), ("kn_dsa", 1), ("freq", 2)],
    [("g_ple_gate_2", 8), ("g_ple_post_2", 8), ("conv_w_2", 32), ("conv_b_2", 8), ("b_rg_gates_2", 16),
     ("lru_lambda_2", 8), ("ffn_conv_b_2", 24), ("pool_scale_2", 4)],
    [("ffn_conv_w_2", 72)],
]
VROWS = [sum(n for _, n in t) for t in VECTORS]
VCOL = {}
for _t, _tile in enumerate(VECTORS):
    _at = _t * P
    for _name, _n in _tile:
        VCOL[_name] = _at
        _at += _n

C_FQ, C_FK, C_FV, C_FL, C_DQ, C_DK, C_DV, C_IQ, C_IK, C_IW, C_G = (
    0, 512, 1024, 1536, 1544, 2056, 2120, 2184, 2696, 2760, 2768)

ITEMS = [("iq", 4), ("ik", 1), ("dviw", 1), ("fv", 4), ("flog", 1), ("dk", 1), ("gates", 16),
         ("qkd", 12), ("proj", 16), ("wout", 8),
         ("pool", 4), ("rx", 8), ("g2", 16), ("rg", 8), ("poolw", 4), ("mix", 16), ("wo", 8),
         ("ffn0", 24), ("ffn1", 24), ("ffn2", 24), ("plep", 8), ("pleg", 8)]
N0 = {}
_at = 0
for _name, _n in ITEMS:
    N0[_name] = _at
    _at += _n

N_VEC = sum(2 if n == 1 else 1 for t in VECTORS for _, n in t) + 1


def flat(ap):
    names = [f"a{i}" for i in range(len(ap.shape))]
    return ap.rearrange(f"{' '.join(names)} -> ({' '.join(names)})")


def program(nc, A, out):
    alloc = nc.alloc_sbuf_tensor_at
    sems, suffix = {}, ""

    def S(name):
        if name not in sems:
            sems[name] = nc.alloc_semaphore(name=name + suffix)
        return sems[name]

    base = 16512
    at = base

    def place(nbytes):
        nonlocal at
        o = at
        at += nbytes
        return o

    o_raw, o_whi, o_wlo = place(8192), place(8192), place(8192)
    o_ah, o_al = place(32768), place(32768)
    o_b = place(98304)
    o_bh, o_bl, o_c = o_b, o_b + 32768, o_b + 65536
    o_t = place(16384)

    wraw = alloc("wraw", [P, 2, KD, P], F32, offset=o_raw)
    whi = alloc("whi", [P, 2, KD, P], F32R, offset=o_whi)
    wlo = alloc("wlo", [P, 2, KD, P], F32R, offset=o_wlo)
    Ah = alloc("Ah", [P, KD, T], F32R, offset=o_ah)
    Al = alloc("Al", [P, KD, T], F32R, offset=o_al)
    Bh = alloc("Bh", [P, KD, T], F32R, offset=o_bh)
    Bl = alloc("Bl", [P, KD, T], F32R, offset=o_bl)
    C = alloc("C", [P, KD, T], F32, offset=o_c)
    TT = alloc("TT", [P, 4, T], F32, offset=o_t)

    def small(name, shape, dt=F32):
        n = int(np.prod(shape[1:])) * (2 if dt == BF16 else 4)
        return alloc(name, shape, dt, offset=place((n + 31) // 32 * 32))

    ident = small("ident", [P, P])
    identb = small("identb", [P, P], BF16)
    causb = small("causb", [P, P], BF16)
    meanD = small("meanD", [P, P])
    meanH = small("meanH", [P, P])
    strict = small("strict", [P, P], BF16)
    onesb = small("onesb", [P, P], BF16)
    VEC = small("VEC", [P, 3 * P])
    MOD = small("MOD", [P, 48])
    cact = small("cact", [P, 2, 8])
    gm = small("gm", [P, 2, 8])
    fb = small("fb", [NH, 1])
    bs = small("bs", [P, 10, 8])
    att = small("att", [P, 4, 4])
    gq = small("gq", [P, 13])
    one = small("one", [P, 1])
    small_end = at

    def vec(name, j=0, n=1):
        return VEC[:, VCOL[name] + j:VCOL[name] + j + n]

    def vecd(name, j):
        return VEC[:, ds(j + VCOL[name], 1)]

    xrows = alloc("xrows", [P, NB, D], F32, offset=o_bh)
    adaraw = alloc("adaraw", [P, KD, D], F32, offset=o_bl)
    vrows = alloc("vrows", [P, 3, P], F32, offset=o_ah)
    posi = alloc("posi", [P, T], I32, offset=o_t)
    trig = alloc("trig", [P, 4, T], F32, offset=o_b + 71936)
    QKD = alloc("QKD", [P, 12, T], F32, offset=o_b)
    IQ = alloc("IQ", [P, 4, T], F32, offset=o_b + 32768)
    KX = alloc("KX", [P, T], F32, offset=o_b + 49152)
    V = alloc("V", [P, NB, 512], F32, offset=o_b + 53248)
    DV = alloc("DV", [P, NB, 72], F32, offset=o_b + 69632)
    SCW = [(b + 1) * P for b in range(NB)]
    SCO = [sum(SCW[:b]) for b in range(NB)]
    SC = alloc("SC", [P, sum(SCW)], F32, offset=o_b + 71936)
    FS = alloc("FS", [NH, 4, T], F32, offset=o_b + 71936)
    nF = alloc("nF", [NH, T], F32, offset=o_b + 90368)
    SQ = alloc("SQ", [P, T], F32, offset=o_b + 90368)
    E = alloc("E", [P, 8, T], F32, offset=o_b)
    junk = alloc("junk", [P, T], BF16, offset=o_b + 28672)
    IK = alloc("IK", [P, T], F32, offset=o_b + 24576)
    nFb = [alloc(f"nFb{h}", [P, T], F32, offset=o_ah + 4096 * h) for h in range(4)]
    Qz = alloc("Qz", [P, 2, T], F32, offset=o_al)
    Pb = [alloc(f"Pb{i}", [P, T], F32, offset=(o_ah + 16384, o_ah + 20480, o_al + 8192)[i]) for i in range(3)]
    PT = [alloc(f"PT{i}", [P, NB, P], F32, offset=o_ah + 24576 + 4096 * i) for i in range(2)]
    OF = alloc("OF", [P, 4, T], F32, offset=o_al + 16384)
    OD = alloc("OD", [P, 4, T], F32, offset=o_t)
    rw = alloc("rw", [P, KD, 36], F32, offset=o_bh)
    rwh = alloc("rwh", [P, KD, 36], F32R, offset=o_bh + 1152)
    rwl = alloc("rwl", [P, KD, 36], F32R, offset=o_bh + 2304)
    rbias = alloc("rbias", [P, 36], F32, offset=o_bh + 3456)
    R = lambda name, shape, off, dt=F32: alloc(name, shape, dt, offset=o_bh + 4096 + off)
    rL = R("rL", [P, NB, 36], 0)
    rG = R("rG", [P, NB, N_EXP], 1536)
    rT = R("rT", [P, NB, N_EXP], 2560)
    rO1 = R("rO1", [P, NB, N_EXP], 3584)
    rO2 = R("rO2", [P, NB, N_EXP], 4608)
    rOb = R("rOb", [P, NB, N_EXP], 5632, BF16)
    rK = R("rK", [P, NB, N_EXP], 6656)
    rS = R("rS", [P, 12, NB], 7680)
    rI = R("rI", [P, N_EXP], 8192)
    rGg = R("rGg", [P, NB, N_GRP], 8448)
    rN = R("rN", [P, N_EXP], 8704)
    rNt = R("rNt", [P, 4, N_EXP], 9344)
    rSi = R("rSi", [P, SLOTS + 1], 9856)
    rTk = R("rTk", [P, 2, NB], 10048, I32)
    rZ = R("rZ", [SLOTS + 1, P], 11808, I32)
    rLi = R("rLi", [SLOTS + 1, P], 10784, I32)
    rLf = R("rLf", [SLOTS + 1, P], 11296)
    rLT = alloc("rLT", [N_GRP + N_EXP, T], F32, offset=o_bh + 16448)
    hrow = alloc("hrow", [P, NB, D], F32, offset=o_bl)
    SLOTE = small("SLOTE", [P, SLOTS + 1], I32)
    NSL = small("NSL", [P, 2], I32)
    POS = small("POS", [P, 2, NB], I32)
    WTOK = small("WTOK", [P, 2, NB])
    IDX = small("IDX", [P, SLOTS + 1], I32)
    DST = small("DST", [P, SLOTS + 1], I32)
    IDC = small("IDC", [P, 1], I32)
    sp8 = small("sp8", [P, 3, KD])
    pfix = small("pfix", [P, 4, 16])
    IDD = small("IDD", [P, 1], I32)
    assert at <= 229344, at
    PIECES, UPS = 12, 8
    mraw = alloc("mraw", [P, PIECES, 1024], F32, offset=o_b)
    mlo = alloc("mlo", [P, PIECES, 1024], F32R, offset=o_b + 49152)
    mhi = alloc("mhi", [P, PIECES, 1024], F32R, offset=o_ah + 16384)
    Xs = alloc("Xs", [P, D], F32, offset=o_t)
    YO = alloc("YO", [P, D], F32, offset=o_t + 4096)
    XTh = alloc("XTh", [P, KD, P], F32R, offset=o_ah)
    XTl = alloc("XTl", [P, KD, P], F32R, offset=o_ah + 4096)
    SG = alloc("SG", [P, FE], F32, offset=o_ah + 8192)
    Hm = alloc("Hm", [P, FE], F32, offset=o_ah + 10240)
    HTh = alloc("HTh", [P, 4, P], F32R, offset=o_ah + 12288)
    HTl = alloc("HTl", [P, 4, P], F32R, offset=o_ah + 14336)
    G12 = alloc("G12", [P, NB, 2, D], F32, offset=o_ah)
    RG = alloc("RG", [P, KD, T], F32, offset=o_bh)
    UP = alloc("UP", [P, 4, T], F32, offset=o_bl)
    bdr = alloc("bdr", [P, 2, 8, P], F32, offset=o_bl + 16384)
    bdh = alloc("bdh", [P, 2, P], F32R, offset=o_bl + 24576)
    bdl = alloc("bdl", [P, 2, P], F32R, offset=o_bl + 25600)
    Bl2 = alloc("Bl2", [P, 4, T], F32R, offset=o_bl + 16384)
    Cl = alloc("Cl", [P, KD, T], F32R, offset=o_c)
    AF = alloc("AF", [P, KD, T], F32, offset=o_ah)
    BG = alloc("BG", [P, KD, T], F32, offset=o_bl)
    PR = alloc("PR", [P, NB, 256], F32, offset=o_bl + 16384)
    pTh = alloc("pTh", [P, 2, T], F32R, offset=o_bl)
    pTl = alloc("pTl", [P, 2, T], F32R, offset=o_bl + 8192)

    assert at <= 229344, at

    acc = [nc.alloc_psum_tensor(f"acc{i}", [P, T], F32) for i in range(2)]
    X = [nc.alloc_psum_tensor(f"X{i}", [P, HALF], F32) for i in range(2)]
    Y = nc.alloc_psum_tensor("Y", [P, T], F32)

    dram = lambda name, shape, dt=F32: nc.dram_tensor(name, shape, dt).ap()
    x0T = dram("x0T", [D, T])
    gates1 = dram("gates1", [2 * D, T])
    nFd = dram("nFd", [NH, T])
    x1T = dram("x1T", [D, T])
    h2rows = dram("h2rows", [T, D])
    slotlist = dram("slotlist", [(SLOTS + 1) * P, 1], I32)
    ys = dram("ys", [2 * T + P, D])
    x2T = dram("x2T", [D, T])
    gates2 = dram("gates2", [2 * D, T])
    x3T = dram("x3T", [D, T])
    x4T = dram("x4T", [D, T])
    tiles = lambda t: t.rearrange("(m p) n -> p m n", p=P)

    w_land = [S("w_land0"), S("w_land1")]
    w_lo, w_used = S("w_lo"), S("w_used")
    acc_free = [S("acc_free0"), S("acc_free1")]

    W1 = A["w_in"][0].rearrange("(k p) n -> p k n", p=P)
    ADA = A["ada_w"][0].rearrange("(k p) n -> p k n", p=P)
    WPF = A["w_proj_fox"][0].rearrange("(k p) n -> p k n", p=P)
    WPD = A["w_proj_dsa"][0].rearrange("(k p) n -> p k n", p=P)
    WOUT = A["w_out"][0].rearrange("(k p) n -> p k n", p=P)
    W2 = A["w_in_2"][0].rearrange("(k p) n -> p k n", p=P)
    WPO = A["w_pool_out_2"][0].rearrange("(k p) n -> p k n", p=P)
    WRO = A["w_rg_out_2"][0].rearrange("(k p) n -> p k n", p=P)
    WO = A["w_o_2"][0].rearrange("(k p) n -> p k n", p=P)
    WUP = A["w_up_2"][0].rearrange("(k p) n -> p k n", p=P)
    WDN = A["w_down_2"][0].rearrange("(k p) n -> p k n", p=P)
    WPG = A["w_ple_gate_2"][0].rearrange("(k p) n -> p k n", p=P)
    WPP = A["w_ple_proj_2"][0].rearrange("(k p) n -> p k n", p=P)

    landed = {}
    count = [0, 0]
    for name, n in ITEMS:
        for j in range(n):
            i = N0[name] + j
            count[i % 2] += 16 * (2 if name in ("ik", "dk", "dviw") else 1)
            landed[i] = count[i % 2]

    stage = ExitStack()
    block = stage.enter_context(nc.Block())
    chains = {}

    def chain(e, name):
        if name not in chains:
            chains[name] = Chain(e, S(f"{name}_step"))
        chains[name].e = e
        return chains[name]

    taken = [0, 0]

    def take(r):
        taken[r] += 1
        return taken[r] - 1 or None

    def product_run(pe, n0, n, ih, il, k=KD, k0=0):
        with pe.Fori(0, n // 2) as i:
            for r in range(2):
                product(pe, n0 + 2 * i + r, r, ih, il, k, k0, free=i + taken[r])
        taken[0] += n // 2
        taken[1] += n // 2

    def load(sp, n, r, src, k=KD, m=P, first=False, part=0):
        if not first:
            sp.wait_ge(w_lo, n - 1)
        sp.dma_start(wraw[:, r, 0:k, part:part + m], src).then_inc(w_land[r], 16)

    def load_run(sp, n0, n, src_of, k=KD):
        with sp.Fori(0, n // 2) as i:
            for r in range(2):
                load(sp, n0 + 2 * i + r, r, src_of(2 * i + r), k)

    def split(pool, n, r, land, k=KD, m=P, first=False):
        ch = chain(pool, "pool")
        pool.wait_ge(w_land[r], land)
        if not first:
            pool.wait_ge(w_used, n - 1)
        ch(pool.tensor_tensor(whi[:, r, 0:k, 0:m], wraw[:, r, 0:k, 0:m], one[:, 0:1].unsqueeze(2).broadcast_to([P, k, m]),
                              ALU.mult))
        pool.tensor_tensor(wlo[:, r, 0:k, 0:m], wraw[:, r, 0:k, 0:m], whi[:, r, 0:k, 0:m].bitcast(F32),
                           ALU.subtract).then_inc(w_lo, 1)

    def split_run(pool, n0, n, k=KD):
        ch = chain(pool, "pool")
        with pool.Fori(0, n // 2) as i:
            ch.enter(i, 2)
            for r in range(2):
                split(pool, n0 + 2 * i + r, r, i * 16 + landed[n0 + r], k)
            ch.leave(n // 2)

    def product(pe, n, r, ih, il, k=KD, k0=0, m=P, free=None, ready=None):
        pe.wait_ge(w_lo, n + 1)
        if free is not None:
            pe.wait_ge(acc_free[r], free)
        for j in range(k):
            if ready is not None:
                pe.wait_ge(ready[0], ready[1] + j + 1)
            for h in range(2):
                o = acc[r][0:m, h * HALF:(h + 1) * HALF]
                cols = slice(h * HALF, (h + 1) * HALF)
                pe.matmul(o, whi[:, r, j, 0:m], ih[:, k0 + j, cols], start=(j == 0), stop=False)
                pe.matmul(o, whi[:, r, j, 0:m], il[:, k0 + j, cols], start=False, stop=False)
                last = pe.matmul(o, wlo[:, r, j, 0:m], ih[:, k0 + j, cols], start=False, stop=(j == k - 1))
        last.then_inc(w_used, 1)

    def ada_load(sp, dst, q, k, landed_sem):
        sp.dma_start(dst, A["ada_w"][0, k * P:(k + 1) * P, q * D:(q + 1) * D]).then_inc(landed_sem, 16)

    def ada_rows(dve, ch, total, rows, k):
        if k == 0:
            ch(dve.tensor_scalar(total, rows, cact[:, 1, k:k + 1], None, ALU.mult))
        else:
            ch(dve.scalar_tensor_tensor(total, rows, cact[:, 1, k:k + 1], total, ALU.mult, ALU.add))
        dve.sem_inc(S("ada_used"), 1)

    def ada_columns(pe, total, cols, n):
        pe.wait_ge(S("ada_sum"), n)
        for m in range(KD):
            last = pe.matmul(cols[:, m:m + 1], total[:, m * P:(m + 1) * P], one[:], start=True, stop=True)
        last.then_inc(S("ada_cols"), 1)

    @block.gpsimd
    def _(pool):
        ch = chain(pool, "pool")
        for t, v in ((one, 1.0), (ident, 0.0), (identb, 0.0), (causb, 0.0), (strict, 1.0), (onesb, 1.0),
                     (meanD, 1.0 / D), (meanH, 0.0)):
            ch(pool.memset(t[:], v))
        ch(pool.memset(meanH[0:HD, 0:HD], 1.0 / HD))
        ch(pool.memset(meanH[HD:P, HD:P], 1.0 / HD))
        for t in (ident, identb):
            ch(pool.affine_select(out=t[:], in_=t[:], compare_op=ALU.not_equal, fill=1.0, base=0,
                                  pattern=[[-1, P]], channel_multiplier=1))
        ch(pool.affine_select(out=causb[:], in_=causb[:], compare_op=ALU.is_ge, fill=NEG, base=0,
                              pattern=[[-1, P]], channel_multiplier=1))
        ch(pool.affine_select(out=strict[:], in_=strict[:], compare_op=ALU.is_gt, fill=0.0, base=0,
                              pattern=[[1, P]], channel_multiplier=-1))
        pool.sem_inc(S("consts"), 1)

    @block.sync
    def _(sp):
        for b in range(NB):
            sp.dma_start(xrows[:, b, :], A["x"][0, b * P:(b + 1) * P, :]).then_inc(S("x_in"), 16)
        for t, tile in enumerate(VECTORS):
            for name, n in tile:
                r0 = VCOL[name] - t * P
                if n == 1:
                    for h in range(2):
                        sp.dma_start(vrows[r0:r0 + 1, t, h * HD:(h + 1) * HD], A[name]).then_inc(S("vec_in"), 16)
                else:
                    src = flat(A[name])
                    sp.dma_start(vrows[r0:r0 + n, t, :], src.rearrange("(j p) -> j p", p=P)).then_inc(S("vec_in"), 16)
        sp.dma_start(fb[:], flat(A["b_fgt"]).rearrange("(h a) -> h a", a=1)).then_inc(S("vec_in"), 16)
        sp.dma_start(posi[:], A["positions"].broadcast_to([P, T])).then_inc(S("pos_in"), 16)
        for q in range(2):
            for k in range(KD):
                if q:
                    sp.wait_ge(S("ada_used"), k + 1)
                ada_load(sp, adaraw[:, k, :], 1 - q, k, S(f"m_land{k}"))
        for n in range(2):
            load(sp, n, n, W1[:, :, C_IQ + n * P:C_IQ + (n + 1) * P], first=True)
        sp.wait_ge(S("xT_done"), 8)
        sp.dma_start(tiles(x0T), C[:]).then_inc(S("x0T_st"), 16)

    @block.tensor
    def _(pe):
        pe.wait_ge(S("consts"), 1)
        pe.wait_ge(S("vec_in"), 16 * N_VEC)
        for t, n in enumerate(VROWS):
            last = pe.transpose(X[0][:, t * P:t * P + n], vrows[0:n, t, :], ident[0:n, 0:n])
        last.then_inc(S("vecT"), 1)
        pe.wait_ge(S("x_in"), 16 * NB)
        for m in range(KD):
            free = take(m % 2)
            if free is not None:
                pe.wait_ge(acc_free[m % 2], free)
            for b in range(NB):
                last = pe.transpose(acc[m % 2][:, b * P:(b + 1) * P], xrows[:, b, m * P:(m + 1) * P], ident[:])
            last.then_inc(S("xT_ps"), 1)

    @block.scalar
    def _(act):
        ch = chain(act, "act")
        act.wait_ge(S("vecs"), 1)
        ch(act.activation(cact[:, 0, :], vec("c", 0, 8), ACT.Sigmoid))
        act.sem_inc(S("csig"), 1)
        for m in range(KD):
            act.wait_ge(S("xT_ps"), m + 1)
            ch(act.activation(C[:, m, :], acc[m % 2][:], ACT.Copy))
            act.sem_inc(acc_free[m % 2], 1)
            act.sem_inc(S("xT_done"), 1)

    @block.vector
    def _(dve):
        ch = chain(dve, "dve")
        dve.wait_ge(S("vecT"), 1)
        for t, n in enumerate(VROWS):
            ch(dve.tensor_copy(VEC[:, t * P:t * P + n], X[0][:, t * P:t * P + n]))
        dve.sem_inc(S("vecs"), 1)
        dve.wait_ge(S("csig"), 1)
        ch(dve.tensor_tensor(cact[:, 1, :], cact[:, 0, :], vec("c", 0, 8), ALU.mult))
        for q in range(2):
            for k in range(KD):
                dve.wait_ge(S(f"m_land{k}"), 16 * (q + 1))
                ada_rows(dve, ch, TT[:, 2 + q, :], adaraw[:, k, :], k)
            dve.sem_inc(S("ada_sum"), 1)
        dve.wait_ge(S("ada_cols"), 2)
        ch(dve.tensor_tensor(MOD[:, 0:16], X[1][:, 0:16], vec("ada_b", 0, 16), ALU.add))
        ch(dve.scalar_tensor_tensor(gm[:, 0, :], MOD[:, 8:16], 1.0, vec("norm1_g", 0, 8), ALU.add, ALU.mult))
        dve.sem_inc(S("gm1"), 1)

    def mean_square(tag, src, tmp, wait, summed=0, on_pe=False, k=0):

        @block.scalar
        def _(act):
            ch = chain(act, "act")
            for m in range(KD):
                wait(act, m)
                if m >= 2:
                    act.wait_ge(S(tag + "_sum"), KD * k + m - 1)
                ch(act.activation(tmp[:, m % 2, :], src[:, m, :], ACT.Square))
                act.sem_inc(S(tag + "_sq"), 1)
            act.wait_ge(S(tag + "_v"), k + 1)
            ch(act.activation(tmp[:, 2, :], tmp[:, 3, :], ACT.Ln))
            ch(act.activation(tmp[:, 2, :], tmp[:, 2, :], ACT.Exp, scale=-0.5))
            act.sem_inc(S(tag + "_root"), 1)

        @block.tensor
        def _(pe):
            if not on_pe:
                pe.wait_ge(S(tag + "_sum"), KD * k + KD)
            for m in range(KD if on_pe else 1):
                if on_pe:
                    pe.wait_ge(S(tag + "_sq"), KD * k + m + 1)
                for h in range(2):
                    last = pe.matmul(Y[:, h * HALF:(h + 1) * HALF], meanD[:],
                                     tmp[:, m % 2 if on_pe else 2, h * HALF:(h + 1) * HALF],
                                     start=(m == 0), stop=(m == KD - 1 or not on_pe))
                last.then_inc(S(tag + ("_sum" if on_pe else "_mean")), 1)

        @block.vector
        def _(dve):
            ch = chain(dve, "dve")
            for m in range(KD if on_pe else summed, KD):
                dve.wait_ge(S(tag + "_sq"), KD * k + m + 1)
                if m == 0:
                    ch(dve.tensor_copy(tmp[:, 2, :], tmp[:, 0, :]))
                else:
                    ch(dve.tensor_tensor(tmp[:, 2, :], tmp[:, 2, :], tmp[:, m % 2, :], ALU.add))
                dve.sem_inc(S(tag + "_sum"), 1)
            if on_pe:
                dve.wait_ge(S(tag + "_sum"), KD * k + KD)
            else:
                dve.wait_ge(S(tag + "_mean"), k + 1)
            ch(dve.tensor_scalar(tmp[:, 3, :], Y[:], EPS, None, ALU.add))
            dve.sem_inc(S(tag + "_v"), 1)
            dve.wait_ge(S(tag + "_root"), k + 1)
            newton_step(dve, ch, tmp[:, 2, :], tmp[:, 3, :])

    def newton_step(dve, ch, r, v):
        ch(dve.scalar_tensor_tensor(Y[:], r, -0.5, r, ALU.mult, ALU.mult))
        ch(dve.tensor_tensor(Y[:], Y[:], v, ALU.mult))
        ch(dve.scalar_tensor_tensor(r, Y[:], 1.5, r, ALU.add, ALU.mult))

    def normed(tag, src, rstd, gain, shift, dh, dl, wait, keep=False):

        @block.vector
        def _(dve):
            ch = chain(dve, "dve")

            def scale(m):
                ch(dve.scalar_tensor_tensor(src[:, m, :], src[:, m, :], gain(m), rstd, ALU.mult, ALU.mult))
                dve.sem_inc(S(tag + "_scaled"), 1)

            def low(m):
                dve.wait_ge(S(tag + "_hi"), m + 1)
                if shift is None or keep:
                    low_part = dve.tensor_tensor(dl[:, m, :], src[:, m, :], dh[:, m, :].bitcast(F32), ALU.subtract)
                else:
                    low_part = dve.scalar_tensor_tensor(dl[:, m, :], src[:, m, :], shift(m), dh[:, m, :].bitcast(F32),
                                                        ALU.add, ALU.subtract)
                low_part.then_inc(S(tag + "_lo"), 1)

            wait(dve)
            scale(0)
            scale(1)
            for m in range(KD):
                if m + 2 < KD:
                    scale(m + 2)
                low(m)

        @block.scalar
        def _(act):
            for m in range(KD):
                act.wait_ge(S(tag + "_scaled"), m + 1)
                if keep:
                    chain(act, "act")(act.activation(src[:, m, :], src[:, m, :], ACT.Identity, bias=shift(m)))
                if shift is None or keep:
                    high_part = act.activation(dh[:, m, :], src[:, m, :], ACT.Copy)
                else:
                    high_part = act.activation(dh[:, m, :], src[:, m, :], ACT.Identity, bias=shift(m))
                high_part.then_inc(S(tag + "_hi"), 1)

    N1T = alloc("N1T", [P, 4, T], F32, offset=o_bh)
    mean_square("n1", C, N1T, lambda act, m: act.wait_ge(S("xT_done"), m + 1) if m else act.wait_ge(S("xT_ps"), 8),
                on_pe=True)

    @block.tensor
    def _(pe):
        for q in range(2):
            ada_columns(pe, TT[:, 2 + q, :], X[1][:, (1 - q) * 8:(1 - q) * 8 + 8], q + 1)

    def n1_wait(dve):
        dve.wait_ge(S("x0T_st"), 16)
    normed("n1", C, N1T[:, 2, :], lambda m: gm[:, 0, m:m + 1], lambda m: MOD[:, m:m + 1], Ah, Al, n1_wait)

    def rotate(dve, ch, x, swapped, tmp):
        ch(dve.tensor_tensor(tmp, x, TT[:, 0, :], ALU.mult))
        ch(dve.tensor_tensor(swapped, swapped, TT[:, 1, :], ALU.mult))
        ch(dve.tensor_tensor(x, tmp, swapped, ALU.add))

    def swap_halves(act, dst, src, done):
        for q in range(4):
            act.dma_start(dst[32 * q:32 * q + 32, :], src[32 * (q ^ 1):32 * (q ^ 1) + 32, :]).then_inc(done, 16)

    BY_ACT = (2, 5, 7)
    SEARCH = 32
    roped = [IQ[:, j, :] for j in range(4)] + [IK[:], KX[:]]
    SCb = [SC[:, SCO[b]:SCO[b] + SCW[b]] for b in range(NB)]
    index_units = [(b, h) for h in range(NH) for b in range(2, NB)]
    NU = NB - 2

    row = lambda t, j: t[:, ds(j, 1), :].rearrange("p a n -> p (a n)")
    half = lambda h: slice(HD * (h % 2), HD * (h % 2) + HD)
    iqz = lambda h: E[:, (3, 7)[h % 2], :]

    @block.sync
    def _(sp):
        for n in (2, 3):
            load(sp, n, n % 2, W1[:, :, C_IQ + n * P:C_IQ + (n + 1) * P])
        load(sp, 4, 0, W1[:, :, C_IK:C_IK + HD], m=HD)
        load(sp, 4, 0, W1[:, :, C_IK:C_IK + HD], m=HD, part=HD, first=True)
        load(sp, 5, 1, W1[:, :, C_DV:C_DV + HD], m=HD)
        load(sp, 5, 1, W1[:, :, C_IW:C_IW + 8], m=8, part=HD, first=True)
        for j in range(4):
            load(sp, 6 + j, j % 2, W1[:, :, C_FV + j * P:C_FV + (j + 1) * P])
        load(sp, 10, 0, W1[:, :, C_FL:C_FL + 8], m=8)
        load(sp, 11, 1, W1[:, :, C_DK:C_DK + HD], m=HD)
        load(sp, 11, 1, W1[:, :, C_DK:C_DK + HD], m=HD, part=HD, first=True)
        sp.wait_ge(S("nF_done"), 1)
        sp.dma_start(nFd, nF[:]).then_inc(S("nF_st"), 16)
        load_run(sp, N0["gates"], 16, lambda j: W1[:, :, ds(j * P + C_G, P)])
        load_run(sp, N0["qkd"], 4, lambda j: W1[:, :, ds(j * P + C_DQ, P)])
        load_run(sp, N0["qkd"] + 4, 8, lambda j: W1[:, :, ds(j * P + C_FQ, P)])

    @block.gpsimd
    def _(pool):
        for n in range(12):
            split(pool, n, n % 2, landed[n], m={5: 72, 10: NH}.get(n, P), first=n < 2)
        split_run(pool, N0["gates"], 16)
        split_run(pool, N0["qkd"], 12)

    @block.tensor
    def _(pe):
        def to_rows(n, m):
            pe.wait_ge(S("v_cols"), n - 4)
            if n > 5:
                pe.wait_ge(S("v_rows"), n - 5)
            for b in range(NB):
                last = pe.transpose(Y[:, b * P:b * P + m], E[0:m, 4 + n % 2, b * P:(b + 1) * P], ident[0:m, 0:m])
            last.then_inc(S("v_turned"), 1)

        for n in range(12):
            product(pe, n, n % 2, Ah, Al, free=take(n % 2), ready=(S("n1_lo"), 0) if n == 0 else None,
                    m={5: 72, 10: NH}.get(n, P))
            if 6 <= n <= 10:
                to_rows(n - 1, 72 if n == 6 else P)
        pe.wait_ge(S("roped"), 5)
        pe.wait_ge(S("zeroed"), 1)
        for u, (b, h) in enumerate(index_units):
            pe.wait_ge(acc_free[u % 2], take(u % 2))
            if b == 2:
                pe.wait_ge(S("padded"), h + 1)
            for c in range(0, SCW[b], HALF):
                w = min(HALF, SCW[b] - c)
                last = pe.matmul(acc[u % 2][:, c:c + w], iqz(h)[:, b * P:(b + 1) * P], IK[:, c:c + w],
                                 start=True, stop=True)
            last.then_inc(S("dots"), 1)
        pe.wait_ge(S("v_rows"), 5)
        pe.wait_ge(S("k_sq"), 1)
        for h in range(2):
            last = pe.matmul(Y[:, h * HALF:(h + 1) * HALF], meanH[:], E[:, 4, h * HALF:(h + 1) * HALF],
                             start=True, stop=True)
        last.then_inc(S("k_mean"), 1)
        product_run(pe, N0["gates"], 16, Ah, Al)

        def q_mean(j):
            pe.wait_ge(S("q_sq"), j + 1)
            pe.wait_ge(S("q_normed"), j + 1)
            for h in range(2):
                last = pe.matmul(Y[:, h * HALF:(h + 1) * HALF], meanH[:], SQ[:, h * HALF:(h + 1) * HALF],
                                 start=True, stop=True)
            last.then_inc(S("q_mean"), 1)

        n0 = N0["qkd"]
        product(pe, n0, 0, Ah, Al, free=take(0))
        with pe.Fori(0, 5) as i:
            product(pe, n0 + 1 + 2 * i, 1, Ah, Al, free=i + taken[1])
            q_mean(2 * i)
            product(pe, n0 + 2 + 2 * i, 0, Ah, Al, free=i + taken[0])
            q_mean(2 * i + 1)
        taken[0] += 5
        taken[1] += 5
        product(pe, n0 + 11, 1, Ah, Al, free=take(1))
        q_mean(10)
        q_mean(11)

    @block.scalar
    def _(act):
        ch = chain(act, "act")

        def out_of(n, dst, src, func=ACT.Copy, **kw):
            act.wait_ge(w_used, n + 1)
            ch(act.activation(dst, src, func, **kw))
            act.sem_inc(acc_free[n % 2], 1)

        act.wait_ge(S("angles"), 1)
        ch(act.activation(trig[:, 3, :], trig[:, 1, :], ACT.Sin))
        ch(act.activation(TT[:, 0, :], trig[:, 2, :], ACT.Sin))
        act.sem_inc(S("sines"), 1)
        for j in range(4):
            out_of(j, IQ[:, j, :], acc[j % 2][:])
            if j >= 2:
                act.wait_ge(S("roped"), j - 1)
            swap_halves(act, E[:, 2 * (j % 2), :], IQ[:, j, :], S(f"swapped{j % 2}"))
        out_of(4, IK[:], acc[0][:])
        act.wait_ge(S("roped"), 3)
        swap_halves(act, E[:, 0, :], IK[:], S("swapped0"))
        def from_rows(n):
            act.wait_ge(S("v_turned"), n - 4)
            rows = Y[:].rearrange("p (b n) -> p b n", b=NB)
            if n == 5:
                ch(act.activation(DV[:], rows[:, :, 0:72], ACT.Copy))
            else:
                ch(act.activation(V[:, :, (n - 6) * P:(n - 5) * P], rows, ACT.Copy))
            act.sem_inc(S("v_rows"), 1)

        for n in range(5, 10):
            m = 72 if n == 5 else P
            out_of(n, E[0:m, 4 + n % 2, :], acc[n % 2][0:m, :])
            act.sem_inc(S("v_cols"), 1)
            if n >= 6:
                from_rows(n - 1)
        from_rows(9)
        out_of(10, FS[:, 0, :], acc[0][0:NH, :], ACT.Identity, bias=fb[:])
        act.sem_inc(S("forget"), 1)
        act.wait_ge(S("roped"), 5)
        out_of(11, KX[:], acc[1][:])
        act.wait_ge(S("forget_abs"), 1)
        ch(act.activation(FS[:, 1, :], FS[:, 1, :], ACT.Exp, scale=-1.0))
        ch(act.activation(FS[:, 2, :], FS[:, 1, :], ACT.Ln, bias=1.0))
        act.sem_inc(S("forget_ln"), 1)
        def pad(h):
            if h >= 2:
                act.wait_ge(S("dots"), NU * (h - 1))
            act.activation(iqz(h)[half(h), 2 * P:], IQ[half(h), h // 2, 2 * P:], ACT.Copy).then_inc(S("padded"), 1)
        pad(0)
        pad(1)
        for u, (b, h) in enumerate(index_units):
            if u % NU == 1 and 1 <= h < NH - 1:
                pad(h + 1)
            act.wait_ge(S("dots"), u + 1)
            if u >= 2:
                act.wait_ge(S("index_sum"), u - 1)
            ch(act.activation(E[:, 4 + u % 2, 0:SCW[b]], acc[u % 2][:, 0:SCW[b]], ACT.Relu))
            act.sem_inc(acc_free[u % 2], 1)
            act.sem_inc(S("relu"), 1)
        act.wait_ge(S("index_sum"), len(index_units))
        ch(act.activation(E[:, 4, :], KX[:], ACT.Square))
        act.sem_inc(S("k_sq"), 1)
        act.wait_ge(S("k_v"), 1)
        ch(act.activation(E[:, 4, :], E[:, 5, :], ACT.Ln))
        ch(act.activation(E[:, 4, :], E[:, 4, :], ACT.Exp, scale=-0.5))
        act.sem_inc(S("k_root"), 1)
        act.wait_ge(S("k_normed"), 1)
        swap_halves(act, E[:, 2, :], KX[:], S("swapped1"))
        for r in range(2):
            act.sem_inc(S(f"gates1_st{r}"), 16)
        def gate_tiles(i0, n, searches):
            with act.Fori(0, n) as i:
                ch.enter(i, 2 + 2 * searches * len(BY_ACT))
                for r in range(2):
                    j = 2 * i + 2 * i0 + r
                    act.wait_ge(w_used, N0["gates"] + j + 1)
                    act.wait_ge(S(f"gates1_st{r}"), i * 16 + 16 * (i0 + 1))
                    ch(act.activation(TT[:, 2 + r, :], acc[r][:], ACT.Sigmoid, bias=vecd("b_gate", j)))
                    act.sem_inc(acc_free[r], 1)
                    act.dma_start(gates1[ds(j * P, P), :], TT[:, 2 + r, :]).then_inc(S(f"gates1_st{r}"), 16)
                    for q in range(searches):
                        act.wait_ge(S("mid"), i * (2 * searches) + r * searches + q + 1)
                        for b in BY_ACT:
                            ch(act.activation(E[:, 5, 0:SCW[b]], SCb[b], ACT.Sign, bias=bs[:, 5, b - 2:b - 1],
                                              accum_out=bs[:, 3, b - 2:b - 1]))
                        act.sem_inc(S("signs"), 1)
                ch.leave(n)

        gate_tiles(0, 8, SEARCH // 16)
        for r in range(2):
            act.wait_ge(S(f"gates1_st{r}"), 16 * 9)
        act.wait_ge(S("nF_st"), 16)

        def q_tiles(first, n, place):
            with act.Fori(0, n // 2) as i:
                ch.enter(i, 8)
                for r in range(2):
                    j = 2 * i + first + r
                    act.wait_ge(w_used, N0["qkd"] + j + 1)
                    ch(act.activation(row(QKD, 2 * i + place + r), acc[r][:], ACT.Copy))
                    ch(act.activation(SQ[:], acc[r][:], ACT.Square))
                    act.sem_inc(acc_free[r], 1)
                    act.sem_inc(S("q_sq"), 1)
                    act.wait_ge(S("q_v"), j + 1)
                    ch(act.activation(TT[:, 2, :], TT[:, 3, :], ACT.Ln))
                    ch(act.activation(TT[:, 2, :], TT[:, 2, :], ACT.Exp, scale=-0.5))
                    act.sem_inc(S("q_root"), 1)
                ch.leave(n // 2)
        q_tiles(0, 4, 8)
        act.wait_ge(S("masks"), 1)
        q_tiles(4, 8, 0)

    @block.vector
    def _(dve):
        ch = chain(dve, "dve")
        dve.wait_ge(S("pos_in"), 16)
        a, n, u = trig[:, 0, :], trig[:, 1, :], trig[:, 2, :]
        ch(dve.tensor_copy(u, posi[:]))
        ch(dve.tensor_scalar(a, u, vec("freq"), None, ALU.mult))
        ch(dve.tensor_scalar(n, a, 1.0 / TWO_PI, ROUND, ALU.mult, ALU.add))
        ch(dve.tensor_scalar(n, n, ROUND, None, ALU.subtract))
        for part in split_two_pi():
            ch(dve.scalar_tensor_tensor(a, n, -part, a, ALU.mult, ALU.add))
        ch(dve.tensor_scalar(u, a, float(np.float32(np.pi / 2)), -TWO_PI, ALU.is_gt, ALU.mult))
        ch(dve.scalar_tensor_tensor(u, a, float(np.pi / 2), u, ALU.add, ALU.add))
        ch(dve.tensor_scalar(n, a, PI_IN, -PI_IN, ALU.min, ALU.max))
        ch(dve.tensor_scalar(u, u, PI_IN, -PI_IN, ALU.min, ALU.max))
        dve.sem_inc(S("angles"), 1)
        dve.wait_ge(S("sines"), 1)
        ch(dve.tensor_scalar(TT[:, 1, :], trig[:, 3, :], vec("freq", 1), None, ALU.mult))
        for j in range(13):
            src = "qn_fox" if j < 4 else "kn_fox" if j < 8 else "qn_dsa" if j < 12 else "kn_dsa"
            ch(dve.tensor_copy(gq[:, j:j + 1], vec(src)))

        def rope(j, swaps):
            dve.wait_ge(S(f"swapped{j % 2}"), 64 * swaps)
            rotate(dve, ch, roped[j], E[:, 2 * (j % 2), :], E[:, 1, :])
            dve.sem_inc(S("roped"), 1)
        for j in range(5):
            rope(j, j // 2 + 1)
        for h in range(2):
            ch(dve.memset(iqz(h)[half(h + 1), :], 0.0))
        dve.sem_inc(S("zeroed"), 1)

        dve.wait_ge(S("forget"), 1)
        z, e, l, t = (FS[:, k, :] for k in range(4))
        ch(dve.scalar_tensor_tensor(e, z, -1.0, z, ALU.mult, ALU.max))
        dve.sem_inc(S("forget_abs"), 1)
        dve.wait_ge(S("forget_ln"), 1)
        ch(dve.tensor_scalar(t, e, 1.0, 1.0, ALU.add, ALU.subtract))
        ch(dve.tensor_scalar(t, t, 1e-30, None, ALU.max))
        ch(dve.reciprocal(t, t))
        ch(dve.tensor_tensor(t, t, e, ALU.mult))
        ch(dve.tensor_scalar(t, t, 2.0, None, ALU.min))
        ch(dve.tensor_tensor(l, l, t, ALU.mult))
        ch(dve.tensor_scalar(z, z, 0.0, None, ALU.min))
        ch(dve.tensor_tensor_scan(nF[:], z, l, 0.0, ALU.add, ALU.subtract))
        ch(dve.tensor_scalar(nF[:], nF[:], -1.0 / SCALE, None, ALU.mult))
        dve.sem_inc(S("nF_done"), 1)

        dve.wait_ge(S("v_rows"), 1)
        for u, (b, h) in enumerate(index_units):
            dve.wait_ge(S("relu"), u + 1)
            e, w = E[:, 4 + u % 2, 0:SCW[b]], DV[:, b, HD + h:HD + h + 1]
            if h == 0:
                ch(dve.tensor_scalar(SCb[b], e, w, None, ALU.mult))
            else:
                ch(dve.scalar_tensor_tensor(SCb[b], e, w, SCb[b], ALU.mult, ALU.add))
            dve.sem_inc(S("index_sum"), 1)

        dve.wait_ge(S("k_mean"), 1)
        ch(dve.tensor_scalar(E[:, 5, :], Y[:], EPS, None, ALU.add))
        dve.sem_inc(S("k_v"), 1)
        dve.wait_ge(S("k_root"), 1)
        newton_step(dve, ch, E[:, 4, :], E[:, 5, :])
        ch(dve.scalar_tensor_tensor(KX[:], KX[:], gq[:, 12:13], E[:, 4, :], ALU.mult, ALU.mult))
        dve.sem_inc(S("k_normed"), 1)
        rope(5, 3)

        lo, hi, mid, cnt, goal, nmid, t1, t2, need = (bs[:, k, 0:6] for k in range(9))
        for b in range(2, NB):
            c = slice(b - 2, b - 1)
            ch(dve.tensor_reduce(lo[:, c], SCb[b], AX.X, ALU.min))
            ch(dve.tensor_reduce(mid[:, c], SCb[b], AX.X, ALU.max))
            ch(dve.memset(goal[:, c], float(2 * TOPK - SCW[b] if b in BY_ACT else TOPK)))
        ch(dve.scalar_tensor_tensor(cnt, mid, -1.0, mid, ALU.mult, ALU.max))
        ch(dve.scalar_tensor_tensor(hi, cnt, 2.0 ** -20, mid, ALU.mult, ALU.add))
        ch(dve.tensor_scalar(hi, hi, 1e-30, None, ALU.add))
        for b in range(2, NB):
            ch(dve.memset(SC[0:HD, SCO[b] + b * P + HD:SCO[b] + (b + 1) * P], NEG))
        with dve.Fori(0, SEARCH) as i:
            ch.enter(i, 9 + NB - 2 - len(BY_ACT))
            ch(dve.tensor_tensor(t1, lo, hi, ALU.add))
            ch(dve.tensor_scalar(mid, t1, 0.5, None, ALU.mult))
            ch(dve.tensor_scalar(nmid, t1, -0.5, None, ALU.mult))
            dve.sem_inc(S("mid"), 1)
            for b in range(2, NB):
                if b not in BY_ACT:
                    ch(dve.tensor_scalar(junk[:, 0:SCW[b]], SCb[b], mid[:, b - 2:b - 1], None, ALU.is_ge, ALU.add,
                                         accum_out=cnt[:, b - 2:b - 1]))
            dve.wait_ge(S("signs"), i + 1)
            ch(dve.tensor_tensor(t1, cnt, goal, ALU.is_ge))
            ch(dve.scalar_tensor_tensor(t2, t1, FAR, mid, ALU.mult, ALU.add))
            ch(dve.tensor_tensor(hi, hi, t2, ALU.min))
            ch(dve.tensor_scalar(t1, t1, 1.0, FAR, ALU.subtract, ALU.mult))
            ch(dve.tensor_tensor(t2, t1, mid, ALU.add))
            ch(dve.tensor_tensor(lo, lo, t2, ALU.max))
            ch.leave(SEARCH)
        def mask(b):
            w, c = SCW[b], slice(b - 2, b - 1)
            above, tied, rank = E[:, 0, 0:w], E[:, 1, 0:w], E[:, 3, 0:w]
            ch(dve.tensor_scalar(above, SCb[b], hi[:, c], None, ALU.is_gt, ALU.add, accum_out=cnt[:, c]))
            ch(dve.tensor_scalar(need[:, c], cnt[:, c], -1.0, float(TOPK), ALU.mult, ALU.add))
            ch(dve.scalar_tensor_tensor(tied, SCb[b], lo[:, c], above, ALU.is_ge, ALU.subtract))
            ch(dve.tensor_tensor_scan(rank, tied, above, 0.0, ALU.add, ALU.bypass))
            ch(dve.scalar_tensor_tensor(tied, rank, need[:, c], tied, ALU.is_le, ALU.mult))
            ch(dve.tensor_tensor(above, above, tied, ALU.add))
            ch(dve.tensor_scalar(SCb[b], above, 1.0, -NEG, ALU.subtract, ALU.mult))

        def q_norm(j, tile):
            dve.wait_ge(S("q_mean"), j + 1)
            ch(dve.tensor_scalar(TT[:, 3, :], Y[:], EPS, None, ALU.add))
            dve.sem_inc(S("q_v"), 1)
            dve.wait_ge(S("q_root"), j + 1)
            newton_step(dve, ch, TT[:, 2, :], TT[:, 3, :])
            q = row(QKD, tile)
            ch(dve.scalar_tensor_tensor(q, q, gq[:, ds(tile, 1)], TT[:, 2, :], ALU.mult, ALU.mult))
            dve.sem_inc(S("q_normed"), 1)

        dve.sem_inc(S("q_normed"), 1)
        for b in range(2):
            ch(dve.memset(SCb[b], 0.0))
            ch(dve.memset(SC[0:HD, SCO[b] + b * P + HD:SCO[b] + (b + 1) * P], NEG))
        for j, blocks in enumerate(((2, 3), (4, 5), (6,), (7,))):
            for b in blocks:
                mask(b)
            if j == 3:
                dve.sem_inc(S("masks"), 1)
            q_norm(j, 8 + j)
        with dve.Fori(0, 8) as j:
            ch.enter(j, 5)
            q_norm(j + 4, j)
            ch.leave(8)

    units = [(kind, h, b) for kind in ("fox", "dsa") for h in range(NH) for b in range(NB)]
    groups = [[(c, min(4, b + 1 - c)) for c in range(0, b + 1, 4)] for _, _, b in units]
    g0 = [sum(len(g) for g in groups[:u]) for u in range(len(units) + 1)]
    nmax, psum = (lambda u: att[:, 0, u % 4:u % 4 + 1]), (lambda u: att[:, 1, u % 4:u % 4 + 1])
    rinv = lambda u: att[:, 2, u % 4:u % 4 + 1]

    @block.sync
    def _(sp):
        sp.wait_ge(S("nF_st"), 16)
        sp.wait_ge(w_used, N0["qkd"] + 12)
        def forget_sums(h):
            if h >= 4:
                sp.wait_ge(S("s_max"), NB * (h - 3))
            sp.dma_start(nFb[h % 4][:], nFd[h:h + 1, :].broadcast_to([P, T])).then_inc(S("nF_in"), 16)
        for h in range(5):
            forget_sums(h)
        sp.wait_ge(S("q_roped"), 4)
        for n in range(4 * KD):
            if n % KD == 0 and n:
                forget_sums(n // KD + 4)
            if n >= 2:
                sp.wait_ge(S("ada_used"), 2 * KD + n - 1)
            ada_load(sp, TT[:, n % 2, :], 2 + n // KD, n % KD, S("ada2_land%d" % (n % 2)))

    @block.tensor
    def _(pe):
        def scores(u):
            kind, h, b = units[u]
            pe.wait_ge(acc_free[u % 2], take(u % 2))
            if b == 0:
                pe.wait_ge(S("padded"), NH + u // NB + 1)
            q, k = Qz[:, h % 2, :], QKD[:, 4 + h // 2, :] if kind == "fox" else KX[:]
            for c in range(0, SCW[b], HALF):
                w = min(HALF, SCW[b] - c)
                diagonal = kind == "fox" and c + w == SCW[b]
                last = pe.matmul(acc[u % 2][:, c:c + w], q[:, b * P:(b + 1) * P], k[:, c:c + w],
                                 start=True, stop=not diagonal)
            if kind == "fox":
                last = pe.matmul(acc[u % 2][:, b * P:(b + 1) * P], identb[:], causb[:], start=False, stop=True)
            last.then_inc(S("s_ps"), 1)

        def turn(u):
            pe.wait_ge(S("p_ready"), u + 1)
            for i, (c, n) in enumerate(groups[u]):
                g = g0[u] + i
                if g >= 2:
                    pe.wait_ge(S("pt_ready"), g - 1)
                for j in range(n):
                    last = pe.transpose(X[g % 2][:, j * P:(j + 1) * P], Pb[u % 3][:, (c + j) * P:(c + j + 1) * P],
                                        ident[:])
                last.then_inc(S("p_turned"), 1)

        def values(u):
            kind, h, b = units[u]
            if u >= NB and b % 4 == 0:
                pe.wait_ge(S("o_out"), 2 * (u // NB - 1) + b // 4 + 1)
            q = u // NB - 2
            if b == 0 and 0 <= q < 4:
                pe.wait_ge(S("o_out"), 2 * (u // NB))
                ada_columns(pe, TT[:, 2 + q % 2, :], Y[:, HALF:HALF + KD], q + 3)
            if b == 4 and 0 <= q < 4:
                pe.wait_ge(S("mod_out"), q + 1)
            pe.wait_ge(S("pt_ready"), g0[u + 1])
            out_ = Y[HD * (h % 2):HD * (h % 2) + HD, b * P:(b + 1) * P]
            for k in range(b + 1):
                v = V[:, k, h * HD:(h + 1) * HD] if kind == "fox" else DV[:, k, 0:HD]
                last = pe.matmul(out_, v, PT[u % 2][:, k, :], start=(k == 0), stop=(k == b))
            last.then_inc(S("pv"), 1)

        pe.wait_ge(S("q_normed"), 13)
        pe.wait_ge(S("zeroed"), 2)
        scores(0)
        scores(1)
        scores(2)
        for u in range(len(units)):
            turn(u)
            if u:
                values(u - 1)
            if u + 3 < len(units):
                scores(u + 3)
        values(len(units) - 1)

    @block.vector
    def _(dve):
        ch = chain(dve, "dve")

        def biased(u):
            kind, h, b = units[u]
            w = SCW[b]
            dve.wait_ge(S("s_ps"), u + 1)
            if kind == "fox" and b == 0:
                dve.wait_ge(S("nF_in"), 16 * max(h + 1, 4))
            if u >= 3:
                dve.wait_ge(S("p_turned"), g0[u - 2])
            bias = nFb[h % 4][:, 0:w] if kind == "fox" else SCb[b]
            ch(dve.tensor_tensor_reduce(Pb[u % 3][:, 0:w], acc[u % 2][:, 0:w], bias, -SCALE, 3e38, ALU.add, ALU.min,
                                        nmax(u)))
            dve.sem_inc(acc_free[u % 2], 1)
            dve.sem_inc(S("s_max"), 1)

        def scaled(u):
            dve.wait_ge(S("exps"), u + 1)
            ch(dve.reciprocal(rinv(u), psum(u)))
            w = SCW[units[u][2]]
            dve.tensor_scalar(Pb[u % 3][:, 0:w], Pb[u % 3][:, 0:w], rinv(u), None, ALU.mult).then_inc(S("p_ready"), 1)

        def ada(n):
            q, k = n // KD, n % KD
            if 0 <= q < 4:
                dve.wait_ge(S("ada2_land%d" % (n % 2)), 16 * (n // 2 + 1))
                ada_rows(dve, ch, TT[:, 2 + q % 2, :], TT[:, n % 2, :], k)
                if k == KD - 1:
                    dve.sem_inc(S("ada_sum"), 1)
            q -= 1
            if k == 2 and 0 <= q < 4:
                dve.wait_ge(S("ada_cols"), q + 3)
                c = 16 + KD * q
                ch(dve.tensor_tensor(MOD[:, c:c + KD], Y[:, HALF:HALF + KD], vec("ada_b", c, KD), ALU.add))
                dve.sem_inc(S("mod_out"), 1)
                if q == 3:
                    ch(dve.scalar_tensor_tensor(gm[:, 1, :], MOD[:, 32:40], 1.0, vec("norm2_g", 0, 8), ALU.add, ALU.mult))

        dve.wait_ge(w_used, N0["qkd"] + 12)
        for h in range(2):
            ch(dve.memset(Qz[half(h + 1), h, :], 0.0))
        dve.sem_inc(S("zeroed"), 1)
        biased(0)
        for u in range(len(units)):
            if u + 1 < len(units):
                biased(u + 1)
            scaled(u)
            if u % 2 == 1 and u < NB:
                j = u // 2
                dve.wait_ge(S("swapped1"), 64 * (j + 4))
                rotate(dve, ch, QKD[:, 8 + j, :], TT[:, 3, :], TT[:, 2, :])
                dve.sem_inc(S("q_roped"), 1)
            ada(u - NB)

    @block.scalar
    def _(act):
        ch = chain(act, "act")

        def exps(u):
            w = SCW[units[u][2]]
            act.wait_ge(S("s_max"), u + 1)
            act.activation(Pb[u % 3][:, 0:w], Pb[u % 3][:, 0:w], ACT.Exp, bias=nmax(u), scale=-1.0,
                           accum_out=psum(u)).then_inc(S("exps"), 1)

        def turned(u):
            if u >= 2:
                act.wait_ge(S("pv"), u - 1)
            for i, (c, n) in enumerate(groups[u]):
                g = g0[u] + i
                act.wait_ge(S("p_turned"), g + 1)
                act.activation(PT[u % 2][:, c:c + n, :], X[g % 2][:, 0:n * P].rearrange("p (a b) -> p a b", b=P),
                               ACT.Copy).then_inc(S("pt_ready"), 1)

        def out_of_bank(u):
            kind, h, b = units[u]
            act.wait_ge(S("pv"), u + 1)
            rows = slice(HD * (h % 2), HD * (h % 2) + HD)
            cols = slice((b - 3) * P, (b + 1) * P)
            dst = OF if kind == "fox" else OD
            act.activation(dst[rows, h // 2, cols], Y[rows, cols], ACT.Copy).then_inc(S("o_out"), 1)

        def pad(hh):
            if hh >= 2:
                act.wait_ge(S("s_ps"), NB * (hh - 1))
            q = QKD[half(hh), hh // 2 if hh < NH else 8 + (hh - NH) // 2, :]
            act.activation(Qz[half(hh), hh % 2, :], q, ACT.Copy).then_inc(S("padded"), 1)

        act.wait_ge(S("q_normed"), 13)
        act.wait_ge(S("zeroed"), 2)
        pad(0)
        pad(1)
        exps(0)
        exps(1)
        for u in range(len(units)):
            turned(u)
            if u and units[u - 1][2] % 4 == 3:
                out_of_bank(u - 1)
            if u % 2 == 0 and u < NB:
                if u:
                    act.wait_ge(S("q_roped"), u // 2)
                swap_halves(act, TT[:, 3, :], QKD[:, 8 + u // 2, :], S("swapped1"))
            if u + 2 < len(units):
                exps(u + 2)
            if u % NB == 2 and 1 <= u // NB < 2 * NH - 1:
                if u // NB == NH - 1:
                    act.wait_ge(S("q_roped"), 4)
                pad(u // NB + 1)
        out_of_bank(len(units) - 1)
        act.wait_ge(S("pv"), len(units))
        act.wait_ge(S("o_out"), 32)
        for j in range(8):
            src = OF if j < 4 else OD
            act.activation(Ah[:, j, :], src[:, j % 4, :], ACT.Copy).then_inc(S("o_hi"), 1)

    @block.vector
    def _(dve):
        ch = chain(dve, "dve")
        for j in range(8):
            dve.wait_ge(S("o_hi"), 8 if j == 4 else j + 1)
            src = OF if j < 4 else OD
            ch(dve.tensor_tensor(Al[:, j, :], src[:, j % 4, :], Ah[:, j, :].bitcast(F32), ALU.subtract))
            dve.sem_inc(S("o_lo"), 1)

    @block.sync
    def _(sp):
        def weights(m):
            n = 2 * m + N0["proj"]
            load(sp, n, 0, WPF[:, :, ds(m * P, P)], k=4)
            load(sp, n + 1, 1, WPD[:, :, ds(m * P, P)], k=4)

        def gate_pair(m, r):
            for g in range(2):
                sp.dma_start(TT[:, 2 * r + g, :], gates1[ds(m * P + g * D, P), :]).then_inc(S(f"gate_in{r}"), 16)
        for m in range(2):
            weights(m)
        sp.wait_ge(S("o_lo"), 8)
        for m in range(2):
            gate_pair(m, m)
        with sp.Fori(1, 4) as i:
            for r in range(2):
                weights(2 * i + r)
                sp.wait_ge(S("merged"), 2 * i + r - 1)
                gate_pair(2 * i + r, r)
        sp.dma_start(C[:], tiles(x0T)).then_inc(S("x0T_in"), 16)
        load_run(sp, N0["wout"], 8, lambda m: WOUT[:, :, ds(m * P, P)])

    @block.gpsimd
    def _(pool):
        split_run(pool, N0["proj"], 16, k=4)
        split_run(pool, N0["wout"], 8)

    @block.tensor
    def _(pe):
        pe.wait_ge(S("o_lo"), 8)
        with pe.Fori(0, 8) as m:
            for r in range(2):
                product(pe, 2 * m + N0["proj"] + r, r, Ah, Al, 4, 4 * r, free=m + taken[r])
        taken[0] += 8
        taken[1] += 8
        pe.wait_ge(S("merged"), 8)
        product_run(pe, N0["wout"], 8, Bh, Bl)

    @block.vector
    def _(dve):
        ch = chain(dve, "dve")
        with dve.Fori(0, 4) as i:
            ch.enter(i, 8)
            for r in range(2):
                m = 2 * i + r
                dve.wait_ge(S(f"gate_in{r}"), i * 32 + 32)
                for g in range(2):
                    dve.wait_ge(w_used, 2 * m + N0["proj"] + g + 1)
                    ch(dve.tensor_tensor(TT[:, 2 * r + g, :], TT[:, 2 * r + g, :], acc[g][:], ALU.mult))
                    dve.sem_inc(acc_free[g], 1)
                ch(dve.tensor_tensor(TT[:, 2 * r, :], TT[:, 2 * r, :], TT[:, 2 * r + 1, :], ALU.add))
                dve.sem_inc(S("merge_sum"), 1)
                dve.wait_ge(S("merge_hi"), m + 1)
                ch(dve.tensor_tensor(row(Bl, m), TT[:, 2 * r, :], row(Bh, m).bitcast(F32), ALU.subtract))
                dve.sem_inc(S("merged"), 1)
            ch.leave(4)
        dve.wait_ge(S("x0T_in"), 16)
        for m in range(KD):
            dve.wait_ge(w_used, N0["wout"] + m + 1)
            ch(dve.scalar_tensor_tensor(C[:, m, :], acc[m % 2][:], MOD[:, 16 + m:17 + m], C[:, m, :],
                                        ALU.mult, ALU.add))
            dve.sem_inc(acc_free[m % 2], 1)
            dve.sem_inc(S("x1_done"), 1)

    @block.scalar
    def _(act):
        ch = chain(act, "act")
        with act.Fori(0, 4) as i:
            for r in range(2):
                m = 2 * i + r
                act.wait_ge(S("merge_sum"), m + 1)
                act.activation(row(Bh, m), TT[:, 2 * r, :], ACT.Copy).then_inc(S("merge_hi"), 1)

    @block.sync
    def _(sp):
        for m in range(KD):
            sp.wait_ge(S("x1_done"), m + 1)
            sp.dma_start(x1T[m * P:(m + 1) * P, :], C[:, m, :]).then_inc(S("x1T_st"), 16)
        sp.wait_ge(w_used, N0["wout"] + 8)
        sp.dma_start(rw[:, :, 0:N_GRP], A["router_w_grp"][0].rearrange("(k p) n -> p k n", p=P)).then_inc(S("rt_in"), 16)
        sp.dma_start(rw[:, :, N_GRP:], A["router_w_exp"][0].rearrange("(k p) n -> p k n", p=P)).then_inc(S("rt_in"), 16)
        sp.dma_start(rbias[:, 0:N_GRP], A["router_b_grp"].broadcast_to([P, N_GRP])).then_inc(S("rt_in"), 16)
        sp.dma_start(rbias[:, N_GRP:], A["router_b_exp"].broadcast_to([P, N_EXP])).then_inc(S("rt_in"), 16)
        sp.dma_start(rI[:], A["from_end"].broadcast_to([P, N_EXP])).then_inc(S("rt_in"), 16)
        sp.dma_start(rTk[:], A["result_row"]).then_inc(S("rt_in"), 16)

    def squares_after_merge(act, m):
        if m == 0:
            act.wait_ge(S("merged"), 8)
        act.wait_ge(S("x1_done"), m + 1)
    mean_square("n2", C, TT, squares_after_merge)

    @block.vector
    def _(dve):
        ch = chain(dve, "dve")
        dve.wait_ge(S("rt_in"), 16 * 6)
        ch(dve.tensor_copy(rwh[:], rw[:]))
        ch(dve.tensor_tensor(rwl[:], rw[:], rwh[:].bitcast(F32), ALU.subtract))
        dve.sem_inc(S("rt_split"), 1)

    normed("n2", C, TT[:, 2, :], lambda m: gm[:, 1, m:m + 1], lambda m: MOD[:, 24 + m:25 + m], Ah, Al,
           lambda dve: dve.wait_ge(S("x1T_st"), 16 * KD), keep=True)

    LOGITS = N_GRP + N_EXP

    @block.sync
    def _(sp):
        sp.dma_start(rZ[:], A["no_row"].broadcast_to([SLOTS + 1, P])).then_inc(S("none_in"), 16)
        sp.wait_ge(S("none_in"), 16)
        sp.dma_start(slotlist.rearrange("(s p) a -> s (p a)", p=P), rZ[:]).then_inc(S("none_st"), 16)
        for b in range(NB):
            sp.wait_ge(S("h2_row"), b + 1)
            sp.dma_start(h2rows[b * P:(b + 1) * P, :], hrow[:, b, :]).then_inc(S("h2_st"), 16)
        sp.wait_ge(S("scattered"), 16 * 2 * NB)
        sp.dma_start(rLi[:], slotlist.rearrange("(s p) a -> s (p a)", p=P)).then_inc(S("list_in"), 16)

    @block.gpsimd
    def _(pool):
        pool.wait_ge(S("none_st"), 16)
        pool.wait_ge(S("rt_in"), 16 * 6)
        pool.wait_ge(S("placed"), 1)
        for k in range(2):
            for b in range(NB):
                pool.indirect_dma_start(slotlist, bass.IndirectOffsetOnAxis(ap=POS[:, k, b:b + 1], axis=0),
                                        rTk[:, k, b:b + 1], None).then_inc(S("scattered"), 16)

    @block.tensor
    def _(pe):
        pe.wait_ge(S("rt_split"), 1)
        for j in range(KD):
            pe.wait_ge(S("n2_lo"), j + 1)
            for h in range(2):
                o, cols = Y[0:LOGITS, h * HALF:(h + 1) * HALF], slice(h * HALF, (h + 1) * HALF)
                pe.matmul(o, rwh[:, j, :], Ah[:, j, cols], start=(j == 0), stop=False)
                pe.matmul(o, rwh[:, j, :], Al[:, j, cols], start=False, stop=False)
                last = pe.matmul(o, rwl[:, j, :], Ah[:, j, cols], start=False, stop=(j == KD - 1))
        last.then_inc(S("logits"), 1)
        pe.wait_ge(S("logits"), 2)
        for b in range(NB):
            last = pe.transpose(X[0][:, b * LOGITS:(b + 1) * LOGITS], rLT[:, b * P:(b + 1) * P],
                                ident[0:LOGITS, 0:LOGITS])
        last.then_inc(S("logits"), 1)
        for b in range(NB):
            pe.wait_ge(acc_free[b % 2], take(b % 2))
            for m in range(KD):
                last = pe.transpose(acc[b % 2][:, m * P:(m + 1) * P], C[:, m, b * P:(b + 1) * P], ident[:])
            last.then_inc(S("h2_turned"), 1)
        pe.wait_ge(S("chosen"), 1)
        for b in range(NB + 1):
            o = Y[:, HALF + b * N_EXP:HALF + (b + 1) * N_EXP]
            if b < NB:
                last = pe.matmul(o, strict[:], rOb[:, b, :], start=True, stop=(b == 0))
            for c in range(b):
                last = pe.matmul(o, onesb[:], rOb[:, c, :], start=(b == NB and c == 0), stop=(c == b - 1))
        last.then_inc(S("ranks"), 1)
        pe.wait_ge(S("list_f"), 1)
        pe.transpose(X[0][:, 0:SLOTS + 1], rLf[:], ident[0:SLOTS + 1, 0:SLOTS + 1]).then_inc(S("list_turned"), 1)

    @block.scalar
    def _(act):
        ch = chain(act, "act")
        act.wait_ge(S("logits"), 1)
        ch(act.activation(rLT[:], Y[0:LOGITS, :], ACT.Copy))
        act.sem_inc(S("logits"), 1)
        for b in range(NB):
            act.wait_ge(S("h2_turned"), b + 1)
            ch(act.activation(hrow[:, b, :], acc[b % 2][:], ACT.Copy))
            act.sem_inc(acc_free[b % 2], 1)
            act.sem_inc(S("h2_row"), 1)
        act.wait_ge(S("gaps"), 1)
        ch(act.activation(rGg[:], rGg[:], ACT.Exp))
        ch(act.activation(rS[:, 3, :], rS[:, 2, :], ACT.Exp))
        act.sem_inc(S("gap_exp"), 1)

    @block.vector
    def _(dve):
        ch = chain(dve, "dve")
        dve.wait_ge(S("logits"), 3)
        along = lambda t, n: t.unsqueeze(2).broadcast_to([P, NB, n])
        every = lambda t, n: t.unsqueeze(1).broadcast_to([P, NB, n])
        ch(dve.tensor_tensor(rL[:], X[0][:, 0:NB * LOGITS].rearrange("p (b n) -> p b n", b=NB), every(rbias[:], LOGITS),
                             ALU.add))
        g, e = rL[:, :, 0:N_GRP], rL[:, :, N_GRP:]
        top, first, gap, p2, norm, gw = (rS[:, k, :] for k in range(6))

        def first_largest(x, n, onehot, largest):
            ch(dve.tensor_reduce(largest, x, AX.X, ALU.max))
            ch(dve.tensor_tensor(onehot, x, along(largest, n), ALU.is_equal))
            ch(dve.tensor_tensor(onehot, onehot, every(rI[:, N_EXP - n:], n), ALU.mult))
            ch(dve.tensor_reduce(first, onehot, AX.X, ALU.max))
            ch(dve.tensor_tensor(onehot, every(rI[:, N_EXP - n:], n), along(first, n), ALU.is_equal))

        grp = rGg[:]
        first_largest(g, N_GRP, grp, top)
        e4 = lambda t: t.rearrange("p b (g n) -> p b g n", g=N_GRP)
        wide = grp.unsqueeze(3).broadcast_to([P, NB, N_GRP, PER_GRP])
        ch(dve.tensor_tensor(e4(rG[:]), e4(e), wide, ALU.mult))
        ch(dve.tensor_scalar(e4(rT[:]), wide, 1.0, -NEG, ALU.subtract, ALU.mult))
        ch(dve.tensor_tensor(rG[:], rG[:], rT[:], ALU.add))
        ch(dve.tensor_tensor(grp, g, along(top, N_GRP), ALU.subtract))
        first_largest(rG[:], N_EXP, rO1[:], gap)
        ch(dve.scalar_tensor_tensor(rG[:], rO1[:], 2 * NEG, rG[:], ALU.mult, ALU.add))
        first_largest(rG[:], N_EXP, rO2[:], top)
        ch(dve.tensor_tensor(gap, top, gap, ALU.subtract))
        dve.sem_inc(S("gaps"), 1)
        ch(dve.tensor_tensor(rOb[:], rO1[:], rO2[:], ALU.add))
        dve.sem_inc(S("chosen"), 1)
        dve.wait_ge(S("gap_exp"), 1)
        ch(dve.tensor_reduce(gw, grp, AX.X, ALU.add))
        ch(dve.tensor_scalar(norm, p2, 1.0, None, ALU.add))
        ch(dve.tensor_tensor(norm, norm, gw, ALU.mult))
        ch(dve.reciprocal(WTOK[:, 0, :], norm))
        ch(dve.tensor_tensor(WTOK[:, 1, :], WTOK[:, 0, :], p2, ALU.mult))
        dve.wait_ge(S("ranks"), 1)
        number, taken_by, after, before = (rNt[:, k, :] for k in range(4))
        ch(dve.tensor_copy(number, Y[:, HALF + NB * N_EXP:HALF + (NB + 1) * N_EXP]))
        ch(dve.memset(taken_by, 0.0))
        for j in range(T // P):
            ch(dve.scalar_tensor_tensor(taken_by, number, float(j * P), taken_by, ALU.is_gt, ALU.add))
        ch(dve.tensor_tensor_scan(after, taken_by, taken_by, 0.0, ALU.add, ALU.bypass))
        ch(dve.tensor_tensor(before, after, taken_by, ALU.subtract))
        ch(dve.tensor_copy(NSL[:, 0:1], after[:, N_EXP - 1:N_EXP]))
        ch(dve.tensor_scalar(rS[:, 6, 0:1], after[:, N_EXP - 1:N_EXP], -1.0, None, ALU.add))
        ch(dve.tensor_copy(NSL[:, 1:2], rS[:, 6, 0:1]))
        ch(dve.tensor_scalar(before, before, float(P), None, ALU.mult))
        ch(dve.tensor_tensor(rK[:], Y[:, HALF:HALF + NB * N_EXP].rearrange("p (b n) -> p b n", b=NB),
                             every(before, N_EXP), ALU.add))
        for k, o in enumerate((rO1, rO2)):
            ch(dve.tensor_tensor(rT[:], o[:], rK[:], ALU.mult))
            ch(dve.tensor_reduce(top, rT[:], AX.X, ALU.add))
            ch(dve.tensor_copy(POS[:, k, :], top))
        dve.sem_inc(S("placed"), 1)
        for s in range(SLOTS + 1):
            ch(dve.tensor_scalar(number, after, float(s), None, ALU.is_le, ALU.add, accum_out=rSi[:, s:s + 1]))
        ch(dve.tensor_scalar(rSi[:], rSi[:], float(N_EXP - 1), None, ALU.min))
        ch(dve.tensor_copy(SLOTE[:], rSi[:]))
        dve.sem_inc(S("slots"), 1)
        dve.wait_ge(S("list_in"), 16)
        ch(dve.tensor_copy(rLf[:], rLi[:]))
        dve.sem_inc(S("list_f"), 1)
        dve.wait_ge(S("list_turned"), 1)
        ch(dve.tensor_copy(DST[:], X[0][:, 0:SLOTS + 1]))
        ch(dve.tensor_scalar(rSi[:], X[0][:, 0:SLOTS + 1], 0.5, -0.25, ALU.mult, ALU.add))
        ch(dve.tensor_scalar(rSi[:], rSi[:], ROUND, None, ALU.add))
        ch(dve.tensor_scalar(rSi[:], rSi[:], ROUND, None, ALU.subtract))
        ch(dve.tensor_scalar(rSi[:], rSi[:], float(T - 1), None, ALU.min))
        ch(dve.tensor_copy(IDX[:], rSi[:]))
        dve.sem_inc(S("idx_in"), 1)

    EW1 = A["exp_w1"].rearrange("l e (k p) n -> (l e k) p n", p=P)
    EW3 = A["exp_w3"].rearrange("l e (k p) n -> (l e k) p n", p=P)
    EW2 = A["exp_w2"].rearrange("l e (k p) n -> (l e k) p n", p=P)
    piece = lambda t, i: t[ds(i, 1)].rearrange("a p n -> p (a n)")

    def slot_count(e):
        e.wait_ge(S("slots"), 1)
        return e.value_load(NSL[0:1, 0:1], min_val=2 * T // P, max_val=SLOTS)

    def last_slot(e):
        return e.value_load(NSL[0:1, 1:2], min_val=2 * T // P - 1, max_val=SLOTS - 1)

    @block.sync
    def _(sp):
        def pieces(s, first):
            e = sp.value_load(SLOTE[0:1, ds(s, 1)], min_val=0, max_val=N_EXP - 1)
            for q in [5, 6, 7, 8, 9, 10, 11, 0, 1, 2, 3, 4] if first else range(PIECES):
                if first and q == 0:
                    sp.wait_ge(S("idx_in"), 1)
                if not first:
                    sp.wait_ge(S("m_lo"), s * PIECES - PIECES + q + 1)
                if q < UPS:
                    sp.dma_start(mraw[:, q, 0:FE], piece(EW1, e * UPS + q)).then_inc(S(f"m_land{q}"), 16)
                    sp.dma_start(mraw[:, q, FE:], piece(EW3, e * UPS + q)).then_inc(S(f"m_land{q}"), 16)
                else:
                    sp.dma_start(mraw[:, q, :], piece(EW2, e * 4 + q - UPS)).then_inc(S(f"m_land{q}"), 16)
        n = slot_count(sp)
        sp.wait_ge(S("h2_st"), 16 * NB)
        pieces(0, True)
        with sp.Fori(1, n) as s:
            pieces(s, False)
        sp.wait_ge(S("m_lo"), last_slot(sp) * PIECES + UPS)
        sp.dma_start(RG[:], tiles(x1T)).then_inc(S("x1T_in"), 16)

    @block.gpsimd
    def _(pool):
        slot_count(pool)
        def gather():
            pool.indirect_dma_start(Xs[:], None, h2rows, bass.IndirectOffsetOnAxis(ap=IDC[:], axis=0))\
                .then_inc(S("xs_in"), 16)
        pool.wait_ge(S("h2_st"), 16 * NB)
        def scatter(s):
            pool.wait_ge(S("y_out"), s + 2)
            pool.wait_ge(S("slot_dst"), s + 1)
            pool.sem_inc(S("gathers"), 1)
            pool.indirect_dma_start(ys, bass.IndirectOffsetOnAxis(ap=IDD[:], axis=0), YO[:], None)\
                .then_inc(S("ys_st"), 16)
            pool.wait_ge(S("ys_st"), s * 16 + 16)
            pool.sem_inc(S("ys_free"), 1)

        pool.wait_ge(S("slot_rows"), 1)
        gather()
        pool.wait_ge(S("slot_rows"), 2)
        pool.wait_ge(S("x_turned"), 1)
        gather()
        end = last_slot(pool)
        with pool.Fori(0, end) as s:
            pool.wait_ge(S("x_turned"), s + 2)
            pool.wait_ge(S("slot_rows"), s + 3)
            pool.sem_inc(S("gathers"), 1)
            gather()
            scatter(s)
        scatter(end)

    @block.tensor
    def _(pe):
        n = slot_count(pe)
        def turn_rows():
            for m in range(KD):
                last = pe.transpose(X[m // 4][:, m % 4 * P:(m % 4 + 1) * P], Xs[:, m * P:(m + 1) * P], ident[:])
            last.then_inc(S("x_turned"), 1)
        pe.wait_ge(S("xs_in"), 16)
        turn_rows()
        with pe.Fori(0, n) as s:
            pe.wait_ge(S("x_lo"), s + 1)
            for k in range(UPS):
                pe.wait_ge(S("m_lo"), s * PIECES + k + 1)
                for h in range(2):
                    o, cols = acc[0][:, h * FE:(h + 1) * FE], slice(h * FE, (h + 1) * FE)
                    pe.matmul(o, XTh[:, k, :], mhi[:, k, cols], start=(k == 0), stop=False)
                    pe.matmul(o, XTh[:, k, :], mlo[:, k, cols], start=False, stop=False)
                    last = pe.matmul(o, XTl[:, k, :], mhi[:, k, cols], start=False, stop=(k == UPS - 1))
                last.then_inc(S("m_used"), 1)
            pe.wait_ge(S("xs_in"), s * 16 + 32)
            turn_rows()
            pe.wait_ge(S("hidden"), s + 1)
            for j in range(4):
                last = pe.transpose(Y[:, j * P:(j + 1) * P], Hm[:, j * P:(j + 1) * P], ident[:])
            last.then_inc(S("h_turned"), 1)
            pe.wait_ge(S("h_lo"), s + 1)
            pe.wait_ge(S("y_out"), s + 1)
            for j in range(4):
                q = UPS + j
                pe.wait_ge(S("m_lo"), s * PIECES + q + 1)
                for h in range(2):
                    o, cols = acc[1][:, h * HALF:(h + 1) * HALF], slice(h * HALF, (h + 1) * HALF)
                    pe.matmul(o, HTh[:, j, :], mhi[:, q, cols], start=(j == 0), stop=False)
                    pe.matmul(o, HTh[:, j, :], mlo[:, q, cols], start=False, stop=False)
                    last = pe.matmul(o, HTl[:, j, :], mhi[:, q, cols], start=False, stop=(j == 3))
                last.then_inc(S("m_used"), 1)

    def turned_rows(e, is_act):
        for h in range(2):
            src = X[h][:].rearrange("p (m n) -> p m n", m=4)
            if is_act:
                e(XTh[:, 4 * h:4 * h + 4, :], src)
            else:
                e(XTl[:, 4 * h:4 * h + 4, :], src, XTh[:, 4 * h:4 * h + 4, :].bitcast(F32))

    @block.scalar
    def _(act):
        ch = chain(act, "moe_act")
        n = slot_count(act)
        act.sem_inc(S("m_used"), PIECES)
        act.sem_inc(S("y_out"), 1)
        act.sem_inc(S("ys_free"), 1)

        def rows_hi(s):
            act.wait_ge(S("x_turned"), s + 1)
            turned_rows(lambda o, i: ch(act.activation(o, i, ACT.Copy)), True)
            act.sem_inc(S("x_hi"), 1)

        def high(s, q):
            per = 32 if q < UPS else 16
            act.wait_ge(S(f"m_land{q}"), s * per + (per + 32 if q < UPS else per))
            act.wait_ge(S("m_used"), s * PIECES + q + 1)
            act.activation(mhi[:, q, :], mraw[:, q, :], ACT.Copy).then_inc(S("m_hi"), 1)

        def result(s):
            act.wait_ge(S("m_used"), s * PIECES + 2 * PIECES)
            act.wait_ge(S("ys_free"), s + 1)
            ch(act.activation(YO[:], acc[1][:], ACT.Copy))
            act.sem_inc(S("y_out"), 1)

        def slot(s, last):
            for q in range(UPS, PIECES):
                high(s, q)
            act.wait_ge(S("m_used"), s * PIECES + UPS + PIECES)
            ch(act.activation(SG[:], acc[0][:, 0:FE], ACT.Silu))
            act.sem_inc(S("silu"), 1)
            rows_hi(s + 1)
            act.wait_ge(S("h_turned"), s + 1)
            ch(act.activation(HTh[:], Y[:, 0:HALF].rearrange("p (m n) -> p m n", m=4), ACT.Copy))
            act.sem_inc(S("h_hi"), 1)
            if not last:
                for q in range(UPS):
                    high(s + 1, q)
            result(s)

        act.wait_ge(S("x_turned"), 1)
        turned_rows(lambda o, i: ch(act.activation(o, i, ACT.Copy)), True)
        act.sem_inc(S("x_hi"), 1)
        for q in range(UPS):
            high(0, q)
        end = last_slot(act)
        with act.Fori(0, end) as s:
            ch.enter(s, 5)
            slot(s, False)
        ch.n = ch.start
        ch.enter(end, 5)
        slot(end, True)
        act.wait_ge(S("ys_free"), n + 1)
        act.sem_inc(S("experts_done"), 1)

    @block.vector
    def _(dve):
        ch = chain(dve, "moe_dve")
        n = slot_count(dve)

        def rows_lo(s):
            dve.wait_ge(S("x_hi"), s + 1)
            turned_rows(lambda o, i, h: ch(dve.tensor_tensor(o, i, h, ALU.subtract)), False)
            dve.sem_inc(S("x_lo"), 1)

        def low(s, q):
            dve.wait_ge(S("m_hi"), s * PIECES + q + 1)
            dve.tensor_tensor(mlo[:, q, :], mraw[:, q, :], mhi[:, q, :].bitcast(F32), ALU.subtract)\
               .then_inc(S("m_lo"), 1)
        dve.tensor_copy(IDC[:], IDX[:, 0:1]).then_inc(S("slot_rows"), 1)
        dve.wait_ge(S("xs_in"), 16)
        dve.tensor_copy(IDC[:], IDX[:, 1:2]).then_inc(S("slot_rows"), 1)
        rows_lo(0)
        for q in range(UPS):
            low(0, q)

        def slot(s, last):
            for q in range(UPS, PIECES):
                low(s, q)
            dve.wait_ge(S("silu"), s + 1)
            ch(dve.tensor_tensor(Hm[:], SG[:], acc[0][:, FE:], ALU.mult))
            dve.sem_inc(S("hidden"), 1)
            rows_lo(s + 1)
            dve.wait_ge(S("h_hi"), s + 1)
            ch(dve.tensor_tensor(HTl[:], Y[:, 0:HALF].rearrange("p (m n) -> p m n", m=4), HTh[:].bitcast(F32),
                                 ALU.subtract))
            dve.sem_inc(S("h_lo"), 1)
            if not last:
                dve.wait_ge(S("xs_in"), s * 16 + 32)
                dve.tensor_copy(IDC[:], IDX[:, ds(s + 2, 1)]).then_inc(S("slot_rows"), 1)
                for q in range(UPS):
                    low(s + 1, q)
            dve.wait_ge(S("ys_free"), s + 1)
            dve.tensor_copy(IDD[:], DST[:, ds(s, 1)]).then_inc(S("slot_dst"), 1)

        end = last_slot(dve)
        with dve.Fori(0, end) as s:
            ch.enter(s, 4)
            slot(s, False)
        ch.n = ch.start
        ch.enter(end, 4)
        slot(end, True)

    @block.sync
    def _(sp):
        sp.wait_ge(S("experts_done"), 1)
        for b in range(NB):
            sp.dma_start(G12[:, b, :, :], ys[2 * b * P:2 * (b + 1) * P, :].rearrange("(p k) n -> p k n", k=2))\
              .then_inc(S(f"y_in{b % 2}"), 16)
        for m in range(KD):
            sp.wait_ge(S("x2_done"), m + 1)
            sp.dma_start(x2T[m * P:(m + 1) * P, :], C[:, m, :]).then_inc(S("x2T_st"), 16)

    @block.tensor
    def _(pe):
        pe.wait_ge(S("y_sum"), NB)
        for m in range(KD):
            pe.wait_ge(acc_free[m % 2], take(m % 2))
            for b in range(NB):
                last = pe.transpose(acc[m % 2][:, b * P:(b + 1) * P], G12[:, b, 0, m * P:(m + 1) * P], ident[:])
            last.then_inc(S("y_turned"), 1)

    @block.vector
    def _(dve):
        ch = chain(dve, "dve")
        for b in range(NB):
            dve.wait_ge(S(f"y_in{b % 2}"), 16 * NB // 2)
            ch(dve.tensor_scalar(G12[:, b, 0, :], G12[:, b, 0, :], WTOK[:, 0, b:b + 1], None, ALU.mult))
            ch(dve.scalar_tensor_tensor(G12[:, b, 0, :], G12[:, b, 1, :], WTOK[:, 1, b:b + 1], G12[:, b, 0, :],
                                        ALU.mult, ALU.add))
            dve.sem_inc(S("y_sum"), 1)
        dve.wait_ge(S("x1T_in"), 16)
        for m in range(KD):
            dve.wait_ge(S("y_turned"), m + 1)
            ch(dve.scalar_tensor_tensor(C[:, m, :], acc[m % 2][:], MOD[:, 40 + m:41 + m], RG[:, m, :],
                                        ALU.mult, ALU.add))
            dve.sem_inc(acc_free[m % 2], 1)
            dve.sem_inc(S("x2_done"), 1)

    mean_square("n2", C, TT, lambda act, m: act.wait_ge(S("x2_done"), m + 1), on_pe=True, k=1)

    stage.close()
    lasting = [n for n in sems if n.startswith(("w_", "acc_free")) or n in ("x2T_st", "act_step", "dve_step", "pool_step")]
    nc.clear_and_free_semaphores([sems[n] for n in sems if n not in lasting])
    nc.all_engine_barrier()
    sems, suffix = {n: sems[n] for n in lasting}, "_b2"
    stage = ExitStack()
    block = stage.enter_context(nc.Block())

    normed("n3", C, TT[:, 2, :], lambda m: vec("g_mix_pre_2", m), None, Ah, Al,
           lambda dve: dve.wait_ge(S("x2T_st"), 16 * KD))

    @block.sync
    def _(sp):
        sp.dma_start(pfix[:].rearrange("p g n -> p (g n)"), A["pool_fix"].broadcast_to([P, 64])).then_inc(S("fix_in"), 16)
        for name, n, c0 in (("pool", 4, 0), ("rx", 8, 512), ("g2", 16, 2560), ("rg", 8, 1536)):
            load_run(sp, N0[name], n, lambda j, c0=c0: W2[:, :, ds(j * P + c0, P)])
            if name == "pool":
                sp.wait_ge(S("bd_zero"), 1)
                for g in range(2):
                    for h in range(2):
                        sp.dma_start(bdr[h * HD:(h + 1) * HD, g, :, h * HD:(h + 1) * HD],
                                     A["w_rg_gates_2"][0, g].rearrange("(j h) i o -> h i j o", h=2)[h])\
                          .then_inc(S("bd_in"), 16)

    @block.gpsimd
    def _(pool):
        ch = chain(pool, "pool")
        ch(pool.memset(bdr[:], 0.0))
        pool.sem_inc(S("bd_zero"), 1)
        for name, n in (("pool", 4), ("rx", 8), ("g2", 16), ("rg", 8)):
            split_run(pool, N0[name], n)

    RZ, IN_, LG = RG[:, 2, :], RG[:, 3, :], RG[:, 4, :]

    @block.tensor
    def _(pe):
        product(pe, N0["pool"], 0, Ah, Al, free=take(0), ready=(S("n3_lo"), 0))
        product(pe, N0["pool"] + 1, 1, Ah, Al, free=take(1))
        product_run(pe, N0["pool"] + 2, 10, Ah, Al)
        with pe.Fori(0, 8) as j:
            product(pe, 2 * j + N0["g2"], 0, Ah, Al, free=j + taken[0])
            pe.wait_ge(S("xc_lo"), j + 1)
            pe.wait_ge(S("bd_split"), j + 1)
            pe.wait_ge(S("ri"), j + 1)
            for g in range(2):
                for h in range(2):
                    o = Y[:, h * HALF:(h + 1) * HALF] if g == 0 else X[h][:]
                    cols = slice(h * HALF, (h + 1) * HALF)
                    pe.matmul(o, bdh[:, g, :], Bh[:, 0, cols], start=True, stop=False)
                    pe.matmul(o, bdh[:, g, :], Bh[:, 1, cols], start=False, stop=False)
                    last = pe.matmul(o, bdl[:, g, :], Bh[:, 0, cols], start=False, stop=True)
            last.then_inc(S("rg_ps"), 1)
            product(pe, 2 * j + N0["g2"] + 1, 1, Ah, Al, free=j + taken[1])
        taken[0] += 8
        taken[1] += 8
        product_run(pe, N0["rg"], 8, Ah, Al)

    @block.scalar
    def _(act):
        ch = chain(act, "act")
        for g in range(4):
            act.wait_ge(w_used, N0["pool"] + g + 1)
            ch(act.activation(UP[:, g, :], acc[g % 2][:], ACT.Copy))
            act.sem_inc(acc_free[g % 2], 1)
            act.sem_inc(S("u_out"), 1)
        act.wait_ge(S("lru_abs"), 1)
        ch(act.activation(sp8[:, 1, :], sp8[:, 0, :], ACT.Exp, scale=-1.0))
        ch(act.activation(sp8[:, 2, :], sp8[:, 1, :], ACT.Ln, bias=1.0))
        act.sem_inc(S("lru_ln"), 1)
        for r in range(2):
            act.sem_inc(S(f"gates2_st{r}"), 16)
        act.sem_inc(S("ri"), 1)

        def gate_tile(j, r):
            act.wait_ge(w_used, 2 * j + N0["g2"] + r + 1)
            act.wait_ge(S(f"gates2_st{r}"), j * 16 + 16)
            ch(act.activation(TT[:, 2 + r, :], acc[r][:], ACT.Sigmoid))
            act.sem_inc(acc_free[r], 1)
            act.dma_start(gates2[ds(j * 2 * P + r * P, P), :], TT[:, 2 + r, :]).then_inc(S(f"gates2_st{r}"), 16)

        def high(j):
            ch(act.activation(Bh[:, 0, :], row(C, j), ACT.Copy))
            act.sem_inc(S("xc_hi"), 1)

        def tile(j, last):
            gate_tile(j, 0)
            act.wait_ge(S("rg_ps"), j + 1)
            act.wait_ge(S("lru"), j + 1)
            act.sem_inc(S("lru_go"), 1)
            ch.count(act.activation(RZ, Y[:], ACT.Sigmoid, bias=vecd("b_rg_gates_2", j)))
            for h in range(2):
                (ch if h else ch.count)(act.activation(IN_[:, h * HALF:(h + 1) * HALF], X[h][:], ACT.Sigmoid, bias=vecd("b_rg_gates_2", j + 8)))
            act.sem_inc(S("ri"), 1)
            if not last:
                high(j + 1)
            gate_tile(j, 1)
            act.wait_ge(S("z"), j + 1)
            ch(act.activation(IN_, RZ, ACT.Tanh))
            ch(act.activation(LG, IN_, ACT.Ln, bias=1.0))
            ch(act.activation(IN_, IN_, ACT.Ln, scale=2.0))
            act.sem_inc(S("logs"), 1)
            ch(act.activation(RZ, RZ, ACT.Exp, scale=-1.0))
            act.wait_ge(S("log_diff"), j + 1)
            ch(act.activation(IN_, IN_, ACT.Exp, scale=0.5))
            act.sem_inc(S("mult"), 1)

        act.wait_ge(S("xc"), 1)
        high(0)
        with act.Fori(0, 7) as j:
            ch.enter(j, 11)
            tile(j, False)
            ch.leave(7)
        tile(7, True)
        act.sem_inc(S("lru_out"), 2)
        for j in range(KD + 1):
            if j < KD:
                act.wait_ge(w_used, N0["rg"] + j + 1)
                act.wait_ge(S("lru_out"), j + 1)
                ch(act.activation(TT[:, j % 2, :], acc[j % 2][:], ACT.Gelu_apprx_tanh))
                act.sem_inc(acc_free[j % 2], 1)
                act.sem_inc(S("rg_out"), 1)
            if j:
                act.wait_ge(S("lru_out"), j + 2)
                act.activation(Bh[:, j - 1, :], C[:, j - 1, :], ACT.Copy).then_inc(S("lru_hi"), 1)
        for g in range(4):
            act.activation(Ah[:, g, :], UP[:, g, :], ACT.Copy).then_inc(S("d_hi"), 1)

    @block.vector
    def _(dve):
        ch = chain(dve, "dve")
        lam = vec("lru_lambda_2", 0, 8)
        z, e, l = (sp8[:, k, :] for k in range(3))
        ch(dve.scalar_tensor_tensor(z, lam, -1.0, lam, ALU.mult, ALU.max))
        dve.sem_inc(S("lru_abs"), 1)
        dve.wait_ge(S("fix_in"), 16)
        for g, w in enumerate(POOL_WINDOWS):
            dve.wait_ge(S("u_out"), g + 1)
            s, d, k = UP[:, g, :], 1, 0
            while d < w:
                ch(dve.tensor_copy(TT[:, k, 0:d], s[:, 0:d]))
                ch(dve.tensor_tensor(TT[:, k, d:], s[:, d:], s[:, 0:T - d], ALU.add))
                s, d, k = TT[:, k, :], 2 * d, 1 - k
            ch(dve.tensor_scalar(s, s, 1.0 / w, None, ALU.mult))
            ch(dve.tensor_tensor(s[:, 0:16], s[:, 0:16], pfix[:, g, :], ALU.mult))
            ch(dve.tensor_tensor(UP[:, g, :], s, UP[:, g, :], ALU.subtract))
            for j in range(2 * g, 2 * g + 2):
                r = j % 2
                dve.wait_ge(w_used, N0["rx"] + j + 1)
                x = C[:, j, :]
                ch(dve.tensor_scalar(x, acc[r][:], vec("conv_w_2", j + 24), vec("conv_b_2", j), ALU.mult, ALU.add))
                for back in range(1, 4):
                    ch(dve.scalar_tensor_tensor(x[:, back:], acc[r][:, 0:T - back], vec("conv_w_2", j + 8 * (3 - back)),
                                                x[:, back:], ALU.mult, ALU.add))
                dve.sem_inc(acc_free[r], 1)
        dve.sem_inc(S("xc"), 1)
        dve.wait_ge(S("lru_ln"), 1)
        ch(dve.tensor_scalar(z, e, 1.0, 1.0, ALU.add, ALU.subtract))
        ch(dve.tensor_scalar(z, z, 1e-30, None, ALU.max))
        ch(dve.reciprocal(z, z))
        ch(dve.tensor_tensor(z, z, e, ALU.mult))
        ch(dve.tensor_scalar(z, z, 2.0, None, ALU.min))
        ch(dve.tensor_tensor(l, l, z, ALU.mult))
        ch(dve.tensor_scalar(z, lam, -1.0, 0.0, ALU.mult, ALU.max))
        ch(dve.tensor_tensor(l, l, z, ALU.add))
        ch(dve.tensor_scalar(sp8[:, 0, :], l, LRU_C, None, ALU.mult))
        dve.wait_ge(S("bd_in"), 64)

        def low(j):
            weights = bdr[:, :, ds(j, 1), :].rearrange("p g a n -> p g (a n)")
            ch(dve.tensor_copy(bdh[:], weights))
            ch(dve.tensor_tensor(bdl[:], weights, bdh[:].bitcast(F32), ALU.subtract))
            dve.sem_inc(S("bd_split"), 1)
            dve.wait_ge(S("xc_hi"), j + 1)
            ch(dve.tensor_tensor(Bh[:, 1, :], row(C, j), Bh[:, 0, :].bitcast(F32), ALU.subtract))
            dve.sem_inc(S("xc_lo"), 1)

        def tile(j, last):
            dve.wait_ge(S("ri"), j + 2)
            x = row(C, j)
            ch(dve.tensor_scalar(RZ, RZ, sp8[:, 0, ds(j, 1)], None, ALU.mult))
            ch(dve.tensor_tensor(x, x, IN_, ALU.mult))
            dve.sem_inc(S("z"), 1)
            if not last:
                low(j + 1)
            dve.wait_ge(S("logs"), j + 1)
            ch(dve.tensor_tensor(IN_, IN_, LG, ALU.subtract))
            dve.sem_inc(S("log_diff"), 1)
            dve.wait_ge(S("mult"), j + 1)
            ch(dve.memset(IN_[:, 0:1], 1.0))
            ch(dve.tensor_tensor(IN_, IN_, x, ALU.mult))
            ch(dve.tensor_tensor_scan(x, RZ, IN_, 0.0, ALU.mult, ALU.add))
            dve.sem_inc(S("lru"), 1)
        dve.sem_inc(S("lru"), 1)
        low(0)
        with dve.Fori(0, 7) as j:
            ch.enter(j, 9)
            tile(j, False)
            ch.leave(7)
        tile(7, True)
        with dve.Fori(0, 4) as i:
            ch.enter(i, 4)
            for r in range(2):
                j = 2 * i + r
                dve.wait_ge(S("rg_out"), j + 1)
                ch(dve.tensor_tensor(row(C, j), row(C, j), TT[:, r, :], ALU.mult))
                dve.sem_inc(S("lru_out"), 1)
                dve.wait_ge(S("lru_hi"), j + 1)
                ch(dve.tensor_tensor(row(Cl, j), row(C, j), row(Bh, j).bitcast(F32), ALU.subtract))
                dve.sem_inc(S("lru_lo"), 1)
            ch.leave(4)
        for g in range(4):
            dve.wait_ge(S("d_hi"), g + 1)
            ch(dve.tensor_tensor(Al[:, g, :], UP[:, g, :], Ah[:, g, :].bitcast(F32), ALU.subtract))
            dve.sem_inc(S("d_lo"), 1)
        for g in range(4):
            dve.wait_ge(w_used, N0["poolw"] + g + 1)
            ch(dve.tensor_scalar(TT[:, g % 2, :], acc[g % 2][:], vec("pool_scale_2", g), None, ALU.mult))
            dve.sem_inc(acc_free[g % 2], 1)
            ch(dve.tensor_copy(Bl[:, g, :], TT[:, g % 2, :]))
            ch(dve.tensor_tensor(Bl2[:, g, :], TT[:, g % 2, :], Bl[:, g, :].bitcast(F32), ALU.subtract))
            dve.sem_inc(S("py_lo"), 1)

    @block.sync
    def _(sp):
        for g in range(4):
            load(sp, N0["poolw"] + g, g % 2, A["pool_w_2"][0, g].rearrange("p (a n) -> p a n", a=1), k=1)

        def weights(m):
            load(sp, 2 * m + N0["mix"], 0, WPO[:, :, ds(m * P, P)], k=4)
            load(sp, 2 * m + N0["mix"] + 1, 1, WRO[:, :, ds(m * P, P)])

        def gate_pair(m, r):
            for g in range(2):
                sp.dma_start(TT[:, 2 * r + g, :], gates2[ds(m * P + g * D, P), :]).then_inc(S(f"gate_in{r}"), 16)
        for m in range(2):
            weights(m)
        sp.wait_ge(S("py_lo"), 4)
        for r in range(2):
            sp.wait_ge(S(f"gates2_st{r}"), 16 * 9)
        for m in range(2):
            gate_pair(m, m)
        with sp.Fori(1, 4) as i:
            for r in range(2):
                weights(2 * i + r)
                sp.wait_ge(S("merged"), 2 * i + r - 1)
                gate_pair(2 * i + r, r)
        load_run(sp, N0["wo"], 8, lambda m: WO[:, :, ds(m * P, P)])
        sp.wait_ge(w_used, N0["mix"] + 16)
        sp.wait_ge(S("x2T_st"), 16 * KD)
        sp.dma_start(RG[:], tiles(x2T)).then_inc(S("x2T_in"), 16)

    @block.gpsimd
    def _(pool):
        for g in range(4):
            split(pool, N0["poolw"] + g, g % 2, landed[N0["poolw"] + g], k=1)
        ch = chain(pool, "pool")
        with pool.Fori(0, 8) as i:
            ch.enter(i, 2)
            for r in range(2):
                split(pool, N0["mix"] + 2 * i + r, r, i * 16 + landed[N0["mix"] + r], (4, 8)[r])
            ch.leave(8)
        split_run(pool, N0["wo"], 8)

    @block.tensor
    def _(pe):
        for g in range(4):
            pe.wait_ge(S("d_lo"), g + 1)
            product(pe, N0["poolw"] + g, g % 2, Ah, Al, 1, g, free=take(g % 2))
        pe.wait_ge(S("py_lo"), 4)
        pe.wait_ge(S("lru_lo"), KD)
        with pe.Fori(0, 8) as m:
            product(pe, 2 * m + N0["mix"], 0, Bl, Bl2, 4, free=m + taken[0])
            product(pe, 2 * m + N0["mix"] + 1, 1, Bh, Cl, free=m + taken[1])
        taken[0] += 8
        taken[1] += 8
        pe.wait_ge(S("merged"), 8)
        product_run(pe, N0["wo"], 8, Ah, Al)

    @block.vector
    def _(dve):
        ch = chain(dve, "dve")
        with dve.Fori(0, 4) as i:
            ch.enter(i, 8)
            for r in range(2):
                m = 2 * i + r
                dve.wait_ge(S(f"gate_in{r}"), i * 32 + 32)
                for g in range(2):
                    dve.wait_ge(w_used, 2 * m + N0["mix"] + g + 1)
                    ch(dve.tensor_tensor(TT[:, 2 * r + g, :], TT[:, 2 * r + g, :], acc[g][:], ALU.mult))
                    dve.sem_inc(acc_free[g], 1)
                ch(dve.tensor_tensor(TT[:, 2 * r, :], TT[:, 2 * r, :], TT[:, 2 * r + 1, :], ALU.add))
                dve.sem_inc(S("merge_sum"), 1)
                dve.wait_ge(S("merge_hi"), m + 1)
                ch(dve.tensor_tensor(row(Al, m), TT[:, 2 * r, :], row(Ah, m).bitcast(F32), ALU.subtract))
                dve.sem_inc(S("merged"), 1)
            ch.leave(4)

    @block.scalar
    def _(act):
        ch = chain(act, "act")
        with act.Fori(0, 4) as i:
            for r in range(2):
                m = 2 * i + r
                act.wait_ge(S("merge_sum"), m + 1)
                act.activation(row(Ah, m), TT[:, 2 * r, :], ACT.Copy).then_inc(S("merge_hi"), 1)

    def after_product(tag, n0, gain, residual_in, stored, result):
        def copied(act, m):
            act.wait_ge(w_used, n0 + m + 1)
            ch = chain(act, "act")
            ch(act.activation(C[:, m, :], acc[m % 2][:], ACT.Copy))
            act.sem_inc(acc_free[m % 2], 1)
        mean_square(tag, C, TT, copied)
        finish(tag, gain, residual_in, stored, result)

    def finish(tag, gain, residual_in, stored, result):
        @block.vector
        def _(dve):
            ch = chain(dve, "dve")
            dve.wait_ge(S(residual_in), 16)
            for m in range(KD):
                ch(dve.scalar_tensor_tensor(C[:, m, :], C[:, m, :], vec(gain, m), TT[:, 2, :], ALU.mult, ALU.mult))
                ch(dve.tensor_tensor(C[:, m, :], C[:, m, :], RG[:, m, :], ALU.add))
                dve.sem_inc(S(tag + "_added"), 1)

        @block.sync
        def _(sp):
            for m in range(KD):
                sp.wait_ge(S(tag + "_added"), m + 1)
                sp.dma_start(result[m * P:(m + 1) * P, :], C[:, m, :]).then_inc(S(stored), 16)

    after_product("n4", N0["wo"], "g_mix_post_2", "x2T_in", "x3T_st", x3T)
    mean_square("n5", C, TT, lambda act, m: act.wait_ge(S("n4_added"), m + 1), on_pe=True)
    normed("n5", C, TT[:, 2, :], lambda m: vec("g_ffn_pre_2", m), None, Ah, Al,
           lambda dve: dve.wait_ge(S("x3T_st"), 16 * KD))

    CH = D_FF // D
    for c in range(CH):
        n0 = N0[f"ffn{c}"]

        @block.sync
        def _(sp):
            with sp.Fori(0, 8) as j:
                for r in range(2):
                    load(sp, n0 + 2 * j + r, r, WUP[:, :, ds(j * P + (c * D + r * D_FF), P)])
            load_run(sp, n0 + 16, 8, lambda m: WDN[:, c * KD:(c + 1) * KD, ds(m * P, P)])

        @block.gpsimd
        def _(pool):
            split_run(pool, n0, 24)

        @block.tensor
        def _(pe):
            if c == 0:
                product(pe, n0, 0, Ah, Al, free=take(0), ready=(S("n5_lo"), 0))
                product(pe, n0 + 1, 1, Ah, Al, free=take(1))
                product_run(pe, n0 + 2, 14, Ah, Al)
            else:
                product_run(pe, n0, 16, Ah, Al)
            pe.wait_ge(S("hid_lo"), 8 * c + 8)
            product_run(pe, n0 + 16, 8, Bh, Bl)

        @block.vector
        def _(dve):
            ch = chain(dve, "dve")
            if c == 0:
                dve.wait_ge(S("n5_lo"), KD)
            with dve.Fori(0, 4) as i:
                ch.enter(i, 10)
                for r in range(2):
                    j = 2 * i + r
                    g = TT[:, 2 * r, :]
                    dve.wait_ge(w_used, 2 * j + n0 + 1)
                    ch(dve.tensor_scalar(g, acc[0][:], vecd("ffn_conv_w_2", j + 8 * c + 48), vecd("ffn_conv_b_2", j + 8 * c),
                                         ALU.mult, ALU.add))
                    for back in range(1, 3):
                        ch(dve.scalar_tensor_tensor(g[:, back:], acc[0][:, 0:T - back],
                                                    vecd("ffn_conv_w_2", j + 8 * c + 24 * (2 - back)), g[:, back:],
                                                    ALU.mult, ALU.add))
                    dve.sem_inc(acc_free[0], 1)
                    dve.sem_inc(S("conv"), 1)
                    dve.wait_ge(w_used, 2 * j + n0 + 2)
                    dve.wait_ge(S("gelu"), j + 8 * c + 1)
                    ch(dve.tensor_tensor(g, g, acc[1][:], ALU.mult))
                    dve.sem_inc(acc_free[1], 1)
                    dve.sem_inc(S("hid"), 1)
                    dve.wait_ge(S("hid_hi"), j + 8 * c + 1)
                    ch(dve.tensor_tensor(row(Bl, j), g, row(Bh, j).bitcast(F32), ALU.subtract))
                    dve.sem_inc(S("hid_lo"), 1)
                ch.leave(4)
            if c < CH - 1:
                with dve.Fori(0, 4) as i:
                    ch.enter(i, 2)
                    for r in range(2):
                        m = 2 * i + r
                        dve.wait_ge(w_used, m + n0 + 17)
                        if c == 0:
                            ch(dve.tensor_copy(row(C, m), acc[r][:]))
                        else:
                            ch(dve.tensor_tensor(row(C, m), acc[r][:], row(C, m), ALU.add))
                        dve.sem_inc(acc_free[r], 1)
                    ch.leave(4)
            else:
                for m in range(KD):
                    dve.wait_ge(w_used, m + n0 + 17)
                    ch(dve.tensor_tensor(C[:, m, :], acc[m % 2][:], C[:, m, :], ALU.add))
                    dve.sem_inc(acc_free[m % 2], 1)
                    dve.sem_inc(S("down"), 1)
                    if m:
                        dve.wait_ge(S("n6_sq"), m)
                        if m == 1:
                            ch(dve.tensor_copy(TT[:, 2, :], TT[:, 0, :]))
                        else:
                            ch(dve.tensor_tensor(TT[:, 2, :], TT[:, 2, :], TT[:, (m - 1) % 2, :], ALU.add))
                        dve.sem_inc(S("n6_sum"), 1)

        @block.scalar
        def _(act):
            ch = chain(act, "act")
            with act.Fori(0, 4) as i:
                ch.enter(i, 2)
                for r in range(2):
                    j = 2 * i + r
                    act.wait_ge(S("conv"), j + 8 * c + 1)
                    ch(act.activation(TT[:, 2 * r, :], TT[:, 2 * r, :], ACT.Gelu_apprx_tanh))
                    act.sem_inc(S("gelu"), 1)
                    act.wait_ge(S("hid"), j + 8 * c + 1)
                    act.activation(row(Bh, j), TT[:, 2 * r, :], ACT.Copy).then_inc(S("hid_hi"), 1)
                ch.leave(4)

    mean_square("n6", C, TT, lambda act, m: act.wait_ge(S("down"), m + 1), summed=KD - 1)

    @block.sync
    def _(sp):
        sp.wait_ge(w_used, N0["ffn2"] + 24)
        sp.dma_start(RG[:], tiles(x3T)).then_inc(S("x3T_in"), 16)
        sp.dma_start(PR[:], A["p_2"][0, 0].rearrange("(b p) n -> p b n", p=P)).then_inc(S("p_in"), 16)
    finish("n6", "g_ffn_post_2", "x3T_in", "x4T_st", x4T)

    @block.tensor
    def _(pe):
        pe.wait_ge(S("p_in"), 16)
        for k in range(2):
            pe.wait_ge(acc_free[k], take(k))
            for b in range(NB):
                last = pe.transpose(acc[k][:, b * P:(b + 1) * P], PR[:, b, k * P:(k + 1) * P], ident[:])
            last.then_inc(S("p_turned"), 1)

    mean_square("n7", C, TT, lambda act, m: act.wait_ge(S("n6_added"), m + 1), on_pe=True)

    @block.scalar
    def _(act):
        for k in range(2):
            act.wait_ge(S("p_turned"), k + 1)
            act.activation(pTh[:, k, :], acc[k][:], ACT.Copy).then_inc(S("p_hi"), 1)

    @block.vector
    def _(dve):
        ch = chain(dve, "dve")
        for k in range(2):
            dve.wait_ge(S("p_hi"), k + 1)
            ch(dve.tensor_tensor(pTl[:, k, :], acc[k][:], pTh[:, k, :].bitcast(F32), ALU.subtract))
            dve.sem_inc(acc_free[k], 1)
            dve.sem_inc(S("p_lo"), 1)
    normed("n7", C, TT[:, 2, :], lambda m: vec("g_ple_gate_2", m), None, Ah, Al,
           lambda dve: dve.wait_ge(S("x4T_st"), 16 * KD))

    @block.sync
    def _(sp):
        load_run(sp, N0["plep"], 8, lambda m: WPP[:, :, ds(m * P, P)], k=2)
        load_run(sp, N0["pleg"], 8, lambda m: WPG[:, :, ds(m * P, P)])
        sp.wait_ge(S("n6_added"), KD)
        sp.wait_ge(S("x4T_st"), 16 * KD)
        sp.dma_start(RG[:], tiles(x4T)).then_inc(S("x4T_in"), 16)

    @block.gpsimd
    def _(pool):
        split_run(pool, N0["plep"], 8, k=2)
        split_run(pool, N0["pleg"], 8)

    @block.tensor
    def _(pe):
        pe.wait_ge(S("p_lo"), 2)
        product_run(pe, N0["plep"], 8, pTh, pTl, 2)

    def plep_out(act, m):
        if m == 0:
            act.wait_ge(S("n7_lo"), KD)
        act.wait_ge(w_used, N0["plep"] + m + 1)
        ch = chain(act, "act")
        ch(act.activation(C[:, m, :], acc[m % 2][:], ACT.Copy))
        act.sem_inc(acc_free[m % 2], 1)
    mean_square("n8", C, TT, plep_out)

    @block.tensor
    def _(pe):
        pe.wait_ge(S("n7_lo"), KD)
        product_run(pe, N0["pleg"], 8, Ah, Al)

    @block.scalar
    def _(act):
        for m in range(KD):
            act.wait_ge(w_used, N0["pleg"] + m + 1)
            ch = chain(act, "act")
            ch(act.activation(BG[:, m, :], acc[m % 2][:], ACT.Sigmoid))
            act.sem_inc(acc_free[m % 2], 1)
            act.sem_inc(S("ple_gate"), 1)
        for b in range(NB):
            act.wait_ge(S("out_turned"), b + 1)
            ch(act.activation(AF[:, b, :], acc[b % 2][:], ACT.Copy))
            act.sem_inc(acc_free[b % 2], 1)
            act.sem_inc(S("out_row"), 1)

    @block.vector
    def _(dve):
        ch = chain(dve, "dve")
        for m in range(KD):
            ch(dve.scalar_tensor_tensor(C[:, m, :], C[:, m, :], vec("g_ple_post_2", m), TT[:, 2, :], ALU.mult, ALU.mult))
        dve.wait_ge(S("x4T_in"), 16)
        for m in range(KD):
            dve.wait_ge(S("ple_gate"), m + 1)
            ch(dve.tensor_tensor(C[:, m, :], C[:, m, :], BG[:, m, :], ALU.mult))
            ch(dve.tensor_tensor(C[:, m, :], C[:, m, :], RG[:, m, :], ALU.add))
        dve.sem_inc(S("result"), 1)

    @block.tensor
    def _(pe):
        pe.wait_ge(S("result"), 1)
        for b in range(NB):
            pe.wait_ge(acc_free[b % 2], take(b % 2))
            for m in range(KD):
                last = pe.transpose(acc[b % 2][:, m * P:(m + 1) * P], C[:, m, b * P:(b + 1) * P], ident[:])
            last.then_inc(S("out_turned"), 1)

    @block.sync
    def _(sp):
        for b in range(NB):
            sp.wait_ge(S("out_row"), b + 1)
            sp.dma_start(out[0, b * P:(b + 1) * P, :], AF[:, b, :]).then_inc(S("out_st"), 16)
        sp.wait_ge(S("out_st"), 16 * NB)

    stage.close()


_INS = ['x', 'c', 'positions', 'ada_w', 'ada_b', 'norm1_g', 'norm2_g', 'w_in', 'b_fgt', 'b_gate', 'qn_fox',
        'kn_fox', 'qn_dsa', 'kn_dsa', 'w_proj_fox', 'w_proj_dsa', 'w_out', 'router_w_grp', 'router_b_grp',
        'router_w_exp', 'router_b_exp', 'exp_w1', 'exp_w3', 'exp_w2', 'p_2', 'g_mix_pre_2', 'g_mix_post_2',
        'w_in_2', 'pool_w_2', 'pool_scale_2', 'w_pool_out_2', 'conv_w_2', 'conv_b_2', 'w_rg_gates_2',
        'b_rg_gates_2', 'lru_lambda_2', 'w_rg_out_2', 'w_o_2', 'g_ffn_pre_2', 'g_ffn_post_2', 'w_up_2',
        'ffn_conv_w_2', 'ffn_conv_b_2', 'w_down_2', 'g_ple_gate_2', 'w_ple_gate_2', 'w_ple_proj_2',
        'g_ple_post_2']


def rotation_constants():
    j = np.arange(P) % HD
    return np.stack([10000.0 ** (-(j % 32) / 32.0), np.where(j < 32, -1.0, 1.0)]).astype(np.float32)


def routing_constants():
    rows = np.arange(2 * T, dtype=np.int32).reshape(NB, P, 2).transpose(1, 2, 0).copy()
    return np.arange(N_EXP, 0, -1, dtype=np.float32)[None], rows, np.arange(2 * T, 2 * T + P, dtype=np.int32)[None]


def pooling_constants():
    return np.stack([w / np.minimum(np.arange(16) + 1.0, w) for w in POOL_WINDOWS]).astype(np.float32).reshape(1, 64)


def kernel(**inputs):
    import concourse.bacc as _bacc
    from concourse.bass_utils import run_bass_kernel_spmd as _run

    nc = _bacc.Bacc("TRN2", target_bir_lowering=False, num_devices=1)
    arrays, args = {}, {}
    given = {name: np.ascontiguousarray(inputs[name]) for name in _INS}
    given["freq"] = rotation_constants()
    given["from_end"], given["result_row"], given["no_row"] = routing_constants()
    given["pool_fix"] = pooling_constants()
    for name, a in given.items():
        arrays[f"in_{name}"] = a
        args[name] = nc.dram_tensor(f"in_{name}", a.shape, mybir.dt.from_np(a.dtype), kind="ExternalInput").ap()
    out = nc.dram_tensor("out_dram", (1, T, D), F32, kind="ExternalOutput").ap()
    program(nc, args, out)
    r = _run(nc, [arrays], core_ids=[0])
    return r.results[0]["out_dram"]
```
